# Optimizing a Trainium2 kernel written in Bass

```python
import jax, jax.numpy as jnp
from jax import lax
import numpy as np

D_MODEL = 1024
BATCH = 1
SEQ = 256
DEPTH = 2

RET_HEADS = 4
RET_DK = 64
RET_DV = 64
RET_CHUNK = 128
ROPE_BASE = 10000.0
RWKV_HEADS = 6
RWKV_HEAD = 64
RWKV_W = RWKV_HEADS * RWKV_HEAD
DECAY_LORA = 64
AAA_LORA = 64
GATE_LORA = 128
RWKV_GN_EPS = 64e-5
GLA_HEADS = 4
GLA_DK = 48
GLA_DV = 96
GLA_GATE_LORA = 16
GLA_GATE_NORMALIZER = 16.0
GLA_CHUNK = 64
D_MIX = RET_HEADS * RET_DV + RWKV_W + GLA_HEADS * GLA_DV
PEER_HEADS = 8
PEER_NKEYS = 128
PEER_NEXPERTS = PEER_NKEYS * PEER_NKEYS
PEER_QDIM = 256
PEER_QHALF = PEER_QDIM // 2
PEER_TOPK = 16
PEER_BLOCK = 128
NORM_EPS = 1e-6
HEAD_NORM_EPS = 1e-5

RET_SIZES = (RET_HEADS * RET_DK, RET_HEADS * RET_DK, RET_HEADS * RET_DV, RET_HEADS * RET_DV)
RWKV_SIZES = (RWKV_W, RWKV_W, RWKV_W, DECAY_LORA, AAA_LORA, GATE_LORA)
GLA_SIZES = (GLA_HEADS * GLA_DK, GLA_HEADS * GLA_DK, GLA_HEADS * GLA_DV, GLA_GATE_LORA, GLA_HEADS * GLA_DV)
GROUP_SIZES = (sum(RET_SIZES), sum(RWKV_SIZES), sum(GLA_SIZES))
D_IN = sum(GROUP_SIZES)

kernel_name = "hymba_ret_rwkv7_gla_peer"

def _split(z, sizes):
    offs = np.cumsum(np.array(sizes))[:-1].tolist()
    return jnp.split(z, offs, axis=-1)

def rms_norm(x, g):
    xf = x.astype(jnp.float32)
    y = xf * lax.rsqrt(jnp.mean(xf * xf, axis=-1, keepdims=True) + NORM_EPS)
    return (y * g.astype(jnp.float32)).astype(x.dtype)

def _head_rms(o, eps):
    return o * lax.rsqrt(jnp.mean(o * o, axis=-1, keepdims=True) + eps)

def _to_bhsd(t, h):
    b, s, _ = t.shape
    return t.reshape(b, s, h, -1).transpose(0, 2, 1, 3)

def _to_chunks(t, n, c):
    b, h, _, d = t.shape
    return t.reshape(b, h, n, c, d).transpose(2, 0, 1, 3, 4)

def _from_chunks(o):
    n, b, h, c, d = o.shape
    return o.transpose(1, 2, 0, 3, 4).reshape(b, h, n * c, d)

def _rotary(t, pos):
    half = t.shape[-1] // 2
    inv = ROPE_BASE ** (-jnp.arange(half, dtype=jnp.float32) / half)
    ang = pos[:, None] * inv[None, :]
    cos, sin = jnp.cos(ang), jnp.sin(ang)
    t1, t2 = t[..., :half], t[..., half:]
    return jnp.concatenate([t1 * cos - t2 * sin, t1 * sin + t2 * cos], axis=-1)

def retention_mixer(q, k, v, g):
    f32 = jnp.float32
    b, s, _ = q.shape
    h, c = RET_HEADS, RET_CHUNK
    n = s // c
    pos = jnp.arange(s, dtype=f32)
    q = _rotary(_to_bhsd(q, h).astype(f32), pos)
    k = _rotary(_to_bhsd(k, h).astype(f32), pos) * (RET_DK ** -0.5)
    v = _to_bhsd(v, h).astype(f32)
    log_gamma = jnp.log1p(-jnp.exp(jnp.linspace(np.log(1.0 / 32.0), np.log(1.0 / 512.0), h).astype(f32)))
    idx = jnp.arange(c, dtype=f32)
    diff = idx[:, None] - idx[None, :]
    causal = diff >= 0
    dmat = jnp.where(causal, jnp.exp(log_gamma[:, None, None] * jnp.where(causal, diff, 0.0)), 0.0)
    q_decay = jnp.exp(log_gamma[:, None] * (idx + 1.0))[..., None]
    k_decay = jnp.exp(log_gamma[:, None] * (c - 1.0 - idx))[..., None]
    chunk_decay = jnp.exp(log_gamma * c)[:, None, None]

    def step(state, inp):
        qc, kc, vc = inp
        scores = jnp.einsum('bhid,bhjd->bhij', qc, kc) * dmat
        o = jnp.einsum('bhij,bhjv->bhiv', scores, vc) + jnp.einsum('bhid,bhdv->bhiv', qc * q_decay, state)
        state = state * chunk_decay + jnp.einsum('bhjd,bhjv->bhdv', kc * k_decay, vc)
        return state, o

    s0 = jnp.zeros((b, h, RET_DK, RET_DV), f32)
    _, o = lax.scan(step, s0, (_to_chunks(q, n, c), _to_chunks(k, n, c), _to_chunks(v, n, c)))
    o = _head_rms(_from_chunks(o), HEAD_NORM_EPS)
    o = o.transpose(0, 2, 1, 3).reshape(b, s, h * RET_DV)
    return o * jax.nn.silu(g.astype(f32))

def rwkv7_mixer(f, mu, w_up, w_bias, a_up, a_bias, g_up, k_k, k_a, r_k, ln_w, ln_b):
    f32 = jnp.float32
    b, s, _ = f.shape
    h, nh = RWKV_HEADS, RWKV_HEAD
    f = f.astype(f32)
    f_prev = jnp.pad(f, ((0, 0), (1, 0), (0, 0)))[:, :-1]
    f = f + (f_prev - f) * mu.astype(f32)
    r, k, v, wd, ad, gd = _split(f, RWKV_SIZES)
    w = -jax.nn.softplus(-(w_bias + jnp.tanh(wd) @ w_up)) - 0.5
    decay = jnp.exp(-jnp.exp(w.astype(f32)))
    a = jax.nn.sigmoid(a_bias + ad @ a_up).astype(f32)
    g = (jax.nn.sigmoid(gd) @ g_up).astype(f32)
    hs = lambda t: t.astype(f32).reshape(b, s, h, nh)
    kk = hs(k * k_k)
    kk = kk * lax.rsqrt(jnp.maximum(jnp.sum(kk * kk, axis=-1, keepdims=True), 1e-24))
    k = k * (1.0 + (a - 1.0) * k_a)
    r_h, k_h, v_h, a_h, w_h = hs(r), hs(k), hs(v), hs(a), hs(decay)
    tm = lambda t: t.transpose(1, 0, 2, 3)

    def step(state, inp):
        r_t, w_t, k_t, v_t, kk_t, a_t = inp
        sa = jnp.einsum('bhvk,bhk->bhv', state, -kk_t)
        state = (state * w_t[:, :, None, :] + sa[..., None] * (kk_t * a_t)[:, :, None, :]
                 + v_t[..., None] * k_t[:, :, None, :])
        return state, jnp.einsum('bhvk,bhk->bhv', state, r_t)

    s0 = jnp.zeros((b, h, nh, nh), f32)
    _, o = lax.scan(step, s0, (tm(r_h), tm(w_h), tm(k_h), tm(v_h), tm(kk), tm(a_h)))
    o = tm(o)
    mean = jnp.mean(o, axis=-1, keepdims=True)
    var = jnp.mean(jnp.square(o - mean), axis=-1, keepdims=True)
    o = (o - mean) * lax.rsqrt(var + RWKV_GN_EPS) * ln_w.astype(f32).reshape(h, nh) + ln_b.astype(f32).reshape(h, nh)
    o = o + jnp.sum(r_h * k_h * r_k.astype(f32), axis=-1, keepdims=True) * v_h
    return o.reshape(b, s, h * nh) * g

def gla_mixer(q, k, v, gk_d, g, gk_up, gk_bias, norm_w):
    f32 = jnp.float32
    b, s, _ = q.shape
    h, c = GLA_HEADS, GLA_CHUNK
    n = s // c
    gk = jax.nn.log_sigmoid((gk_d @ gk_up + gk_bias).astype(f32)) / GLA_GATE_NORMALIZER
    q = _to_bhsd(q.astype(f32), h) * (GLA_DK ** -0.5)
    k = _to_bhsd(k.astype(f32), h)
    v = _to_bhsd(v.astype(f32), h)
    gk = _to_bhsd(gk, h)
    mask = (jnp.arange(c)[:, None] >= jnp.arange(c)[None, :])[:, :, None]

    def step(state, inp):
        qc, kc, vc, gc = inp
        bcum = jnp.cumsum(gc, axis=-2)
        b_last = bcum[..., -1, :]
        o_inter = jnp.einsum('bhid,bhdv->bhiv', qc * jnp.exp(bcum), state)
        diff = bcum[..., :, None, :] - bcum[..., None, :, :]
        dec = jnp.where(mask, jnp.exp(jnp.where(mask, diff, 0.0)), 0.0)
        attn = jnp.sum(qc[..., :, None, :] * kc[..., None, :, :] * dec, axis=-1)
        o = o_inter + jnp.einsum('bhij,bhjv->bhiv', attn, vc)
        state = (state * jnp.exp(b_last)[..., None]
                 + jnp.einsum('bhjd,bhjv->bhdv', kc * jnp.exp(b_last[..., None, :] - bcum), vc))
        return state, o

    s0 = jnp.zeros((b, h, GLA_DK, GLA_DV), f32)
    _, o = lax.scan(step, s0, (_to_chunks(q, n, c), _to_chunks(k, n, c), _to_chunks(v, n, c), _to_chunks(gk, n, c)))
    o = _from_chunks(o).transpose(0, 2, 1, 3)
    o = _head_rms(o, HEAD_NORM_EPS) * norm_w.astype(f32).reshape(h, GLA_DV)
    return o.reshape(b, s, h * GLA_DV) * jax.nn.silu(g.astype(f32))

def peer_ffn(hn, w_q, sub_keys, u, v):
    b, s, d = hn.shape
    hb = hn.reshape((b * s) // PEER_BLOCK, PEER_BLOCK, d)

    def block(xb):
        p = xb.shape[0]
        q = (xb @ w_q).reshape(p, PEER_HEADS, 2, PEER_QHALF)
        sc = jnp.einsum('thpc,hpnc->thpn', q, sub_keys).astype(jnp.float32)
        s1, i1 = lax.top_k(sc[:, :, 0], PEER_TOPK)
        s2, i2 = lax.top_k(sc[:, :, 1], PEER_TOPK)
        cand = (s1[..., :, None] + s2[..., None, :]).reshape(p, PEER_HEADS, PEER_TOPK * PEER_TOPK)
        cand_idx = (i1[..., :, None] * PEER_NKEYS + i2[..., None, :]).reshape(p, PEER_HEADS, PEER_TOPK * PEER_TOPK)
        top_s, sel = lax.top_k(cand, PEER_TOPK)
        eidx = jnp.take_along_axis(cand_idx, sel, axis=-1).reshape(p, PEER_HEADS * PEER_TOPK)
        gate = jax.nn.softmax(top_s, axis=-1).reshape(p, PEER_HEADS * PEER_TOPK)
        act = jax.nn.gelu(jnp.einsum('td,ted->te', xb, u[eidx]).astype(jnp.float32), approximate=False) * gate
        return jnp.einsum('te,ted->td', act, v[eidx]).astype(xb.dtype)

    return lax.map(block, hb).reshape(b, s, d)

def setup_inputs(seed: int = 0) -> dict:
    key = jax.random.key(seed)
    ks = iter(jax.random.split(key, 32))
    nrm = lambda shape, scale: jax.random.normal(next(ks), shape, jnp.float32) * scale
    L = DEPTH
    return {
        "x": nrm((BATCH, SEQ, D_MODEL), 1.0),
        "norm_mix": 1.0 + nrm((L, D_MODEL), 0.02),
        "norm_ffn": 1.0 + nrm((L, D_MODEL), 0.02),
        "norm_final": 1.0 + nrm((D_MODEL,), 0.02),
        "w_in": nrm((L, D_MODEL, D_IN), D_MODEL ** -0.5),
        "w_out": nrm((L, D_MIX, D_MODEL), D_MIX ** -0.5),
        "rwkv_mu": jax.random.uniform(next(ks), (L, sum(RWKV_SIZES)), jnp.float32),
        "rwkv_w_up": nrm((L, DECAY_LORA, RWKV_W), 0.5 * DECAY_LORA ** -0.5),
        "rwkv_w_bias": jax.random.uniform(next(ks), (L, RWKV_W), jnp.float32, -6.0, 1.0),
        "rwkv_a_up": nrm((L, AAA_LORA, RWKV_W), AAA_LORA ** -0.5),
        "rwkv_a_bias": nrm((L, RWKV_W), 0.5),
        "rwkv_g_up": nrm((L, GATE_LORA, RWKV_W), GATE_LORA ** -0.5),
        "rwkv_k_k": 0.85 + nrm((L, RWKV_W), 0.1),
        "rwkv_k_a": 1.0 + nrm((L, RWKV_W), 0.1),
        "rwkv_r_k": nrm((L, RWKV_HEADS, RWKV_HEAD), 0.1),
        "rwkv_ln_w": 1.0 + nrm((L, RWKV_W), 0.02),
        "rwkv_ln_b": nrm((L, RWKV_W), 0.02),
        "gla_gk_up": nrm((L, GLA_GATE_LORA, GLA_HEADS * GLA_DK), GLA_GATE_LORA ** -0.5),
        "gla_gk_bias": nrm((L, GLA_HEADS * GLA_DK), 0.5),
        "gla_norm_w": 1.0 + nrm((L, GLA_HEADS * GLA_DV), 0.02),
        "peer_w_q": nrm((L, D_MODEL, PEER_HEADS * PEER_QDIM), D_MODEL ** -0.5),
        "peer_sub_keys": nrm((L, PEER_HEADS, 2, PEER_NKEYS, PEER_QHALF), PEER_QHALF ** -0.5),
        "peer_u": nrm((L, PEER_NEXPERTS, D_MODEL), D_MODEL ** -0.5),
        "peer_v": nrm((L, PEER_NEXPERTS, D_MODEL), PEER_TOPK ** -0.5),
    }

def reference(x, norm_mix, norm_ffn, norm_final, w_in, w_out, rwkv_mu, rwkv_w_up, rwkv_w_bias,
              rwkv_a_up, rwkv_a_bias, rwkv_g_up, rwkv_k_k, rwkv_k_a, rwkv_r_k, rwkv_ln_w, rwkv_ln_b,
              gla_gk_up, gla_gk_bias, gla_norm_w, peer_w_q, peer_sub_keys, peer_u, peer_v):
    for l in range(DEPTH):
        h = rms_norm(x, norm_mix[l])
        z = h @ w_in[l]
        z_ret, z_rwkv, z_gla = _split(z, GROUP_SIZES)
        o_ret = retention_mixer(*_split(z_ret, RET_SIZES))
        o_rwkv = rwkv7_mixer(z_rwkv, rwkv_mu[l], rwkv_w_up[l], rwkv_w_bias[l], rwkv_a_up[l], rwkv_a_bias[l],
                             rwkv_g_up[l], rwkv_k_k[l], rwkv_k_a[l], rwkv_r_k[l], rwkv_ln_w[l], rwkv_ln_b[l])
        o_gla = gla_mixer(*_split(z_gla, GLA_SIZES), gla_gk_up[l], gla_gk_bias[l], gla_norm_w[l])
        o = jnp.concatenate([o_ret, o_rwkv, o_gla], axis=-1).astype(x.dtype)
        x = x + o @ w_out[l]
        h = rms_norm(x, norm_ffn[l])
        x = x + peer_ffn(h, peer_w_q[l], peer_sub_keys[l], peer_u[l], peer_v[l])
    return rms_norm(x, norm_final)


_drawn_inputs = setup_inputs


def setup_inputs(seed=0):
    import zlib

    import numpy as np

    out = dict(_drawn_inputs(seed))
    spreads = {}
    factors = {'norm_final': 9.046,
     'rwkv_ln_w': 2.903,
     'rwkv_ln_b': 3.049,
     'gla_norm_w': 2.971,
     'norm_ffn': 3.118}
    for name, (base, spread) in spreads.items():
        noise = np.random.default_rng([zlib.crc32(name.encode()), seed]).standard_normal(out[name].shape)
        drawn = base * np.exp(spread * noise) if base else spread * noise
        out[name] = __import__('jax').numpy.asarray(drawn.astype(out[name].dtype))
    for name, factor in factors.items():
        out[name] = (out[name] * factor).astype(out[name].dtype)
    return out
```

```python
from contextlib import ExitStack

import numpy as np

import concourse.bass as bass
from concourse import mybir

F32 = mybir.dt.float32
F32R = mybir.dt.float32r
U32 = mybir.dt.uint32
I32 = mybir.dt.int32
ALU = mybir.AluOpType
ACT = mybir.ActivationFunctionType
AX = mybir.AxisListType

P = 128
S = 256
NT = S // P
D = 1024
DC = D // P
L = 2
NH = 6
CT = 3
GH, GDK, GDV = 4, 48, 96
RH, RDK = 4, 64
GC = 256
N_IN = 15
N_CH = 8
N_OUT = 4
PH, TOPK, NKEYS = 8, 16, 128
NEG = -3.0e38
N_BODY, POOL_BODIES, EXP_BODY, GATE_BODY, SEL_BODY = 32, 9, 10, 11, 14
LOG_DECAY_SCALE = -float(np.exp(-0.5))
NORM_EPS, HEAD_EPS, GN_EPS = 1e-6, 1e-5, 64e-5
CAND_ROWS = [TOPK // (i + 1) for i in range(TOPK)]
NC = sum(CAND_ROWS)

C_MIX, C_FFN, C_MU, C_WB, C_AB, C_KK, C_KA, C_RK, C_GB = 0, 8, 16, 27, 30, 33, 36, 39, 42
N_COLS = 44
W_WA, W_G, W_GK = 0, 384, 768
N_SMALL = 1024
K_ID, K_IOTA = 0, 128
N_CONST = 256
LEVELS = [1, 2, 4, 8, 16, 32, 64]
X_MASK2 = 0
X_LOW = 256
X_UP = X_LOW + 128 * 7
X_ONES = X_UP + 128 * 7
X_BLK = X_ONES + 2
X_HEAD = X_BLK + 128
X_DM = X_HEAD + 2
X_ROPE = X_DM + RH * 256
N_XCONST = X_ROPE + NT * 64


def trunk(nc, x_in, w_in, w_out, cols, small, rows, norm_final, w_q, keys, u_t, v_t, const, xconst, out):
    with ExitStack() as ctx:
        def sb(name, shape, dt=F32):
            return ctx.enter_context(nc.sbuf_tensor(name, shape, dt))

        layer_sems = []

        def sem(name, per_layer=True):
            s = ctx.enter_context(nc.semaphore(name))
            if per_layer:
                layer_sems.append(s)
            return s

        X = sb("x_res", [P, NT, D])
        HT = sb("h_t", [P, DC, S])
        HTH = sb("h_t_hi", [P, DC, S], F32R)
        HTL = sb("h_t_lo", [P, DC, S], F32R)
        RING = sb("w_ring", [P, 2, 2048])
        EH = sb("expert_hi", [P, 4, 512], F32R)
        EL = sb("expert_lo", [P, 4, 512], F32R)
        AH = sb("act_hi", [P, 2, S], F32R)
        AL = sb("act_lo", [P, 2, S], F32R)
        KONST = sb("const_sb", [P, N_CONST])
        COLS = sb("cols_sb", [P, N_COLS])
        IDXQ = sb("idx_quads", [P, S // 4, 8])
        GATET = sb("gate_t", [P, S])
        HOTX = sb("hot_extra", [P, 1024])
        STAT = sb("stat", [P, 64])
        PQ = sb("pool_scalars", [P, 3, 2])
        BIGW = 128 * S
        BIG = sb("big", [P, BIGW])
        PS = ctx.enter_context(nc.psum_tensor("ps", [P, 8, 512], F32))

        ident = KONST[:, K_ID:K_ID + 128]
        iota = KONST[:, K_IOTA:K_IOTA + 128]

        used = [0]

        def big(n):
            a = used[0]
            used[0] += n
            assert used[0] <= BIGW, used[0]
            return BIG[:, a:a + n]

        XC = big(N_XCONST)
        HN = big(NT * D).rearrange("p (t d) -> p t d", t=NT)
        SM = big(N_SMALL)
        ROWS = big(1152)
        RAW = big(2 * 2 * 257).rearrange("p (s b n) -> p s b n", s=2, b=2)
        FM = big(12 * S).rearrange("p (b n) -> p b n", b=12)
        SIGA = big(CT * 2 * S).rearrange("p (c k n) -> p c k n", c=CT, k=2)
        decays = used[0]
        CUM = big(CT * NT * 129).rearrange("p (c k n) -> p c k n", c=CT, k=NT)
        E1 = big(CT * NT * 129).rearrange("p (c k n) -> p c k n", c=CT, k=NT)
        E2 = big(CT * S).rearrange("p (c n) -> p c n", c=CT)
        BTOK = BIG[:, decays:decays + 384]
        KTOK = BIG[:, decays + 384:decays + 768]
        XU = BIG[:, decays + 768:decays + 1536].rearrange("p (a n) -> p a n", a=2)
        STATE = BIG[:, decays + 1536:decays + 1728].rearrange("p (c n) -> p c n", c=CT)
        AR = big(CT * NT * 256).rearrange("p (c k m n) -> p c k m n", c=CT, k=NT, m=2)
        BT = big(CT * S).rearrange("p (c n) -> p c n", c=CT)
        KT = big(CT * S).rearrange("p (c n) -> p c n", c=CT)
        KKN = big(CT * S).rearrange("p (c n) -> p c n", c=CT)
        TMP = big(CT * S).rearrange("p (c n) -> p c n", c=CT)
        MASKED = big(12 * 512).rearrange("p (u m n) -> p u m n", u=12, m=4)
        fm_flat = FM.rearrange("p b n -> p (b n)")
        TI = fm_flat[:, 0:1536].rearrange("p (u n) -> p u n", u=12)
        TT = fm_flat[:, 1536:3072].rearrange("p (u n) -> p u n", u=12)
        Y = SIGA.rearrange("p c k n -> p (c k n)").rearrange("p (u n) -> p u n", u=12)
        VTOK = KKN.rearrange("p c n -> p (c n)").rearrange("p (k n) -> p k n", k=NT)
        GG = RAW.rearrange("p s b n -> p (s b n)")[:, 0:780].rearrange("p (k n) -> p k n", k=NT)
        ZRET = big(NT * 1024).rearrange("p (t n) -> p t n", t=NT)
        ZGLA = big(NT * 768).rearrange("p (t n) -> p t n", t=NT)
        GQK = big(4 * S).rearrange("p (b n) -> p b n", b=4)
        def view(ap, shape_pat, **kw):
            return ap.rearrange(shape_pat, **kw)
        mflat = MASKED.rearrange("p u m n -> p (u m n)")
        at = [0]

        def reuse(n):
            a = at[0]
            at[0] += n
            assert at[0] <= 12 * 512
            return mflat[:, a:a + n]

        ROT = reuse(NT * 512).rearrange("p (t g h c) -> p t g h c", t=NT, g=8, h=2)
        QKT = reuse(4 * S).rearrange("p (b n) -> p b n", b=4)
        SCR = reuse(RH * 384).rearrange("p (h n) -> p h n", h=RH)
        GB = big(2 * S).rearrange("p (b n) -> p b n", b=2)
        GX = big(2 * S).rearrange("p (b n) -> p b n", b=2)
        GE = big(2 * S).rearrange("p (b n) -> p b n", b=2)
        TIf = TI.rearrange("p u n -> p (u n)")
        GACC = TIf.rearrange("p (t h n) -> p t h n", t=3, h=GH)
        XB = view(TT, "p u n -> p (u n)")[:, 0:768].rearrange("p (k n) -> p k n", k=NT)
        OT = HT
        used[0] = 0
        QT = big(16 * S).rearrange("p (b n) -> p b n", b=16)
        HNF = big(NT * D).rearrange("p (t d) -> p t d", t=NT)
        KEYS = big(16 * P).rearrange("p (b n) -> p b n", b=16)
        used[0] = 4 * (SEL_BODY + 1) * S
        SC = big(NT * 2048).rearrange("p (u n) -> p u n", u=32)
        SC2 = big(2048).rearrange("p (u n) -> p u n", u=16)
        VAL = big(32 * 16).rearrange("p (u n) -> p u n", u=32)
        IDX = big(32 * 16).rearrange("p (u n) -> p u n", u=32)
        IDXF = big(32 * 16).rearrange("p (u n) -> p u n", u=32)
        CAND = big(16 * NC).rearrange("p (u n) -> p u n", u=16)
        CAND2 = big(16 * NC).rearrange("p (u n) -> p u n", u=16)
        CIDX = big(16 * NC).rearrange("p (u n) -> p u n", u=16)
        TOPV, POS, POSF, EIDX, GATE, I1F, I2F = (big(256).rearrange("p (u n) -> p u n", u=16) for _ in range(7))
        EQ = big(2 * 16 * NC).rearrange("p (s k n) -> p s k n", s=2, k=16)
        ACTS = BIG[:, :].rearrange("p (e t) -> p e t", t=S)
        ht_flat = HT[:, :, :].rearrange("p c n -> p (c n)")
        HOT = [v.rearrange("p (m n) -> p m n", m=8) for v in (ht_flat[:, 0:1024], ht_flat[:, 1024:2048], HOTX[:, :])]
        FROW = BIG[:, 0:D]
        YOUT = BIG[:, D:D + NT * D].rearrange("p (t d) -> p t d", t=NT)

        const_landed = sem("const_landed", False)
        go = sem("layer_go", False)
        arrived = sem("layer_arrived")
        dve_step, act_step, pool_step = sem("dve_step"), sem("act_step"), sem("pool_step")
        params_landed, ring0_landed, ring1_landed = sem("params_landed"), sem("ring0_landed"), sem("ring1_landed")
        ring_free, keys_copied = sem("ring_free"), sem("keys_copied")
        sumsq_ready, rms_ready, rstd_ready = sem("sumsq_ready"), sem("rms_ready"), sem("rstd_ready")
        h_ready, h_turned, ht_ready = sem("h_ready"), sem("h_turned"), sem("ht_ready")
        proj_done, proj_out = sem("proj_done"), sem("proj_out")
        mixed = sem("mixed")
        zeros_ready = sem("zeros_ready")
        tanh_ready, lora_done, sig_ready = sem("tanh_ready"), sem("lora_done"), sem("sig_ready")
        cum_ready, exp_ready = sem("cum_ready"), sem("exp_ready")
        kksq_ready, kknorm_done, kkmax_ready, kksqrt_ready = sem("kksq_ready"), sem("kknorm_done"), sem("kkmax_ready"), sem("kksqrt_ready")
        gg_done, gg_out = sem("gg_done"), sem("gg_out")
        rk_ready, ab_ready = sem("rk_ready"), sem("ab_ready")
        vtok_done, vtok_out = sem("vtok_done"), sem("vtok_out")
        unit_done, unit_out = sem("unit_done"), sem("unit_out")
        mrow_done, mrow_out = sem("mrow_done"), sem("mrow_out")
        y_done, y_out, z_done, z_out = sem("y_done"), sem("y_out"), sem("z_done"), sem("z_out")
        bk_done, bk_out = sem("bk_done"), sem("bk_out")
        chunk_x, chunk_x_out, chunk_u, chunk_u_out = sem("chunk_x"), sem("chunk_x_out"), sem("chunk_u"), sem("chunk_u_out")
        chunk_o, chunk_o_out, state_done, state_out = sem("chunk_o"), sem("chunk_o_out"), sem("state_done"), sem("state_out")
        var_ready, sd_ready = sem("var_ready"), sem("sd_ready")
        rot_ready, rot_done, rot_out = sem("rot_ready"), sem("rot_done"), sem("rot_out")
        score_done, score_out, ret_o, ret_o_out = sem("score_done"), sem("score_out"), sem("ret_o"), sem("ret_o_out")
        gk_done, gk_out, gabs_ready, gln_ready = sem("gk_done"), sem("gk_out"), sem("gabs_ready"), sem("gln_ready")
        gd_ready, ge_ready, gx_ready, gs_done, gs_out = sem("gd_ready"), sem("ge_ready"), sem("gx_ready"), sem("gs_done"), sem("gs_out")
        gla_o, gla_o_out = sem("gla_o"), sem("gla_o_out")
        silu_ready, mix_ready = sem("silu_ready"), sem("mix_ready")
        ot_done, ot_out = sem("ot_done"), sem("ot_out")
        res_done, res_out = sem("res_done"), sem("res_out")
        split_ready = sem("split_ready")
        q_done, q_out, sc_done, sc_out = sem("q_done"), sem("q_out"), sem("sc_done"), sem("sc_out")
        gdiff_ready, gexp_ready, sel_ready, sel_done, sel_out = sem("gdiff_ready"), sem("gexp_ready"), sem("sel_ready"), sem("sel_done"), sem("sel_out")
        uring = [sem("u0_landed"), sem("u1_landed")]
        u_lo_pool = sem("u_lo_pool")
        u_hi, u_lo, u_done, u_act = sem("u_hi"), sem("u_lo"), sem("u_done"), sem("u_act")
        hot_eq, hot_gate, hot_pool, quad_done, quad_out = (sem(n) for n in ("hot_eq", "hot_gate", "hot_pool", "quad_done", "quad_out"))
        pool_copied, pool_seen = sem("pool_copied"), sem("pool_seen")
        vring = [sem("v0_landed"), sem("v1_landed")]
        v_hi, v_lo, a_hi, a_lo, v_done = sem("v_hi"), sem("v_lo"), sem("a_hi"), sem("a_lo"), sem("v_done")
        peer_done, peer_out = sem("peer_done"), sem("peer_out")
        final_row, y_ready, stored = sem("final_row", False), sem("y_ready", False), sem("stored", False)
        final_ss, final_ms, final_rt = sem("final_ss", False), sem("final_ms", False), sem("final_rt", False)
        ring_landed = [ring0_landed, ring1_landed]
        N_RING = N_IN + N_OUT + 1 + PH

        block = ctx.enter_context(nc.Block())

        @block.sync
        def _(sp):
            sp.dma_start(X[:, :, :], x_in.rearrange("a (t p) d -> p (a t) d", p=P)).then_inc(const_landed, 16)
            sp.dma_start(KONST[:, :], const).then_inc(const_landed, 16)
            with sp.Fori(0, L) as l:
                sp.dma_start(COLS[:, :], cols[l]).then_inc(params_landed, 16)
                sp.dma_start(XC, xconst).then_inc(params_landed, 16)
                sp.dma_start(SM, small[l]).then_inc(params_landed, 16)
                sp.dma_start(ROWS, rows[l].partition_broadcast(P)).then_inc(params_landed, 16)
                src = ([w_in[l, g] for g in range(N_IN)] + [w_out[l, g] for g in range(N_OUT)] + [keys[l]]
                       + [w_q[l, g] for g in range(PH)])
                for n in range(N_RING):
                    if n == N_IN + N_OUT + 2:
                        sp.wait_ge(keys_copied, 1)
                    elif n >= 2:
                        sp.wait_ge(ring_free, n - 1 - (n > N_IN + N_OUT + 2))
                    sp.dma_start(RING[:, n % 2, :], src[n]).then_inc(ring_landed[n % 2], 16)
                for i in range(2):
                    sp.wait_ge(ring_free, N_RING - 2 + i)
                    sp.dma_start(RING[:, i, :], u_t[l, i]).then_inc(uring[i], 16)
                with sp.Fori(1, POOL_BODIES + 1) as j:
                    for i in range(2):
                        sp.wait_ge(u_lo_pool, 8 * j + 4 * i - 4)
                        sp.dma_start(RING[:, i, :], u_t[l, 2 * j + i]).then_inc(uring[i], 16)
                with sp.Fori(1, N_BODY - POOL_BODIES) as j:
                    for i in range(2):
                        sp.wait_ge(u_lo, 8 * j + 4 * i - 4)
                        sp.dma_start(RING[:, i, :], u_t[l, 2 * (j + POOL_BODIES) + i]).then_inc(uring[i], 16)
                for i in range(2):
                    sp.wait_ge(u_lo, 8 * (N_BODY - POOL_BODIES) - 4 + 4 * i)
                    sp.dma_start(RING[:, i, :], v_t[l, i]).then_inc(vring[i], 16)
                with sp.Fori(1, 32) as j:
                    for i in range(2):
                        sp.wait_ge(v_lo, 8 * j + 4 * i - 4)
                        sp.dma_start(RING[:, i, :], v_t[l, 2 * j + i]).then_inc(vring[i], 16)
                sp.wait_ge(arrived, 4)
                for s in layer_sems:
                    sp.sem_clear(s)
                sp.sem_inc(go, 1)
            sp.dma_start(FROW, norm_final.partition_broadcast(P)).then_inc(final_row, 16)
            for t in range(NT):
                sp.wait_ge(y_ready, t + 1)
                sp.dma_start(out[0, t * P:(t + 1) * P, :], YOUT[:, t, :]).then_inc(stored, 16)
            sp.wait_ge(stored, 16 * NT)

        @block.tensor
        def _(pe):
            pe.wait_ge(const_landed, 32)

            def turn_h(src, k):
                for t in range(NT):
                    pe.wait_ge(h_ready, NT * k + t + 1)
                    for c in range(DC):
                        mm = pe.transpose(PS[:, 2 * t + c // 4, (c % 4) * P:(c % 4 + 1) * P], src[:, t, c * P:(c + 1) * P], ident)
                        if c % 4 == 3:
                            mm.then_inc(h_turned, 1)

            def group(g):
                pe.wait_ge(ring_landed[g % 2], 16 * (g // 2 + 1))
                if g == 0:
                    pe.wait_ge(ht_ready, 4)
                if g >= 4:
                    pe.wait_ge(proj_out, g - 3)
                w = RING[:, g % 2, :].rearrange("p (c n) -> p c n", c=DC)
                for b in range(2):
                    o = PS[:, g % 4, b * 256:(b + 1) * 256]
                    for c in range(DC):
                        if g < N_CH:
                            mm = pe.matmul(o, w[:, c, b * P:(b + 1) * P], HT[:, c, :], start=c == 0, stop=c == DC - 1)
                        else:
                            mm = pe.matmul(o, HT[:, c, b * P:(b + 1) * P], w[:, c, :], start=c == 0, stop=c == DC - 1)
                mm.then_inc(proj_done, 1)
                pe.wait_ge(proj_done, g + 1)
                pe.sem_inc(ring_free, 1)

            def lora():
                pe.wait_ge(params_landed, 64)
                pe.wait_ge(tanh_ready, 1)
                for c in range(CT):
                    o = slice(c % 2 * 256, c % 2 * 256 + 256)
                    pe.matmul(PS[:, 4 + c // 2, o], SM[0:64, W_WA + c * P:W_WA + (c + 1) * P], FM[0:64, 0, :], start=True, stop=True)
                    pe.matmul(PS[:, 6 + c // 2, o], SM[64:128, W_WA + c * P:W_WA + (c + 1) * P], FM[64:128, 0, :],
                              start=True, stop=True).then_inc(lora_done, 1)

            def gk_up():
                pe.wait_ge(sig_ready, 7)
                for b in range(2):
                    mm = pe.matmul(PS[:, 5, b * 256:(b + 1) * 256], SM[0:16, W_GK + b * P:W_GK + (b + 1) * P], FM[0:16, 11, :],
                                   start=True, stop=True)
                mm.then_inc(gk_done, 1)

            def kk_norm():
                pe.wait_ge(kksq_ready, 1)
                pe.wait_ge(sig_ready, 7)
                for c in range(CT):
                    o = PS[:, 7, c * 256:(c + 1) * 256] if c < 2 else PS[:, 4, 0:256]
                    mm = pe.matmul(o, XC[:, X_BLK:X_BLK + P], TMP[:, c, :], start=True, stop=True)
                mm.then_inc(kknorm_done, 1)

            def gate_and_bonus():
                pe.wait_ge(rk_ready, 1)
                pe.wait_ge(sig_ready, 7)
                pe.wait_ge(kkmax_ready, 1)
                for t in range(NT):
                    pe.matmul(PS[:, 6 + t, 0:384], FM[:, 1, t * P:(t + 1) * P], SM[:, W_G:W_G + 384], start=True, stop=True)
                    for c in range(CT):
                        mm = pe.matmul(PS[:, 6 + t, 384 + 2 * c:386 + 2 * c], TMP[:, c, t * P:(t + 1) * P],
                                       XC[:, X_HEAD:X_HEAD + 2], start=True, stop=True)
                    mm.then_inc(gg_done, 1)

            def v_tok():
                pe.wait_ge(gk_out, 1)
                for k in range(NT):
                    for c in range(CT):
                        mm = pe.transpose(PS[:, 4 + k, c * P:(c + 1) * P], FM[:, 8 + c, k * P:(k + 1) * P], ident)
                    mm.then_inc(vtok_done, 1)

            def units():
                pe.wait_ge(ab_ready, 1)
                pe.wait_ge(vtok_out, 2)
                pe.wait_ge(gg_out, 2)
                for u in range(12):
                    k, h = divmod(u, NH)
                    c, r = h // 2, slice(64 * (h % 2), 64 * (h % 2) + 64)
                    if u >= 4:
                        pe.wait_ge(unit_out, u - 3)
                    for m, lhs in enumerate((BT, KT)):
                        mm = pe.matmul(PS[:, 4 + u % 4, m * 256:(m + 1) * 256], lhs[r, c, k * P:(k + 1) * P],
                                       AR[r, c, k, :, :], start=True, stop=True)
                    mm.then_inc(unit_done, 1)
                pe.wait_ge(proj_out, N_IN)
                for u in range(12):
                    k, h = divmod(u, NH)
                    c, r = h // 2, slice(64 * (h % 2), 64 * (h % 2) + 64)
                    e = u // 2
                    mm = pe.matmul(PS[:, 2 * (u % 2) + e // 4, (e % 4) * P:(e % 4 + 1) * P], AR[r, c, k, 0, :], BT[r, c, k * P:(k + 1) * P],
                                   start=True, stop=True)
                    if u in (6, 7, 10, 11):
                        mm.then_inc(mrow_done, 1)
                for i, src in enumerate((BT, KT)):
                    pe.wait_ge(unit_out, 12)
                    for c in range(CT):
                        mm = pe.transpose(PS[:, 4 + i, c * P:(c + 1) * P], src[:, c, 0:P], ident)
                    mm.then_inc(bk_done, 1)

            def invert():
                pe.wait_ge(mrow_out, 4 + 3)
                pe.wait_ge(bk_out, 2)
                for n, b in enumerate(LEVELS[1:]):
                    for k in range(NT):
                        if n >= 1:
                            pe.wait_ge(z_out, 2 * n - 1 + k)
                        for h in range(NH):
                            u = k * NH + h
                            mm = pe.matmul(PS[:, 2 * k + h // 4, (h % 4) * P:(h % 4 + 1) * P], MASKED[:, u, 0, :], TI[:, u, :],
                                           start=True, stop=True)
                        mm.then_inc(y_done, 1)
                    for k in range(NT):
                        pe.wait_ge(y_out, 2 * n + k + 1)
                        for h in range(NH):
                            u = k * NH + h
                            first = Y[:, u, :].rearrange("p (q a b) -> p q a b", a=2, b=b)[:, :, 0, :]
                            second = TT[:, u, :].rearrange("p (q a b) -> p q a b", a=2, b=b)[:, :, 1, :]
                            pe.matmul(PS[:, 4 + 2 * k, h * 64:(h + 1) * 64], TT[:, u, :], first, start=True, stop=True)
                            mm = pe.matmul(PS[:, 5 + 2 * k, h * 64:(h + 1) * 64], Y[:, u, :], second, start=True, stop=True)
                        mm.then_inc(z_done, 1)

            def chunks():
                pe.wait_ge(z_out, 2 * 6)
                for k in range(NT):
                    if k:
                        pe.wait_ge(state_out, 1)
                        pe.wait_ge(chunk_o_out, 1)
                    for h in range(NH):
                        c, r = h // 2, slice(64 * (h % 2), 64 * (h % 2) + 64)
                        o, v = PS[:, 4 * (h % 2), c * 64:(c + 1) * 64], VTOK[:, k, h * 64:(h + 1) * 64]
                        mm = pe.matmul(o, MASKED[:, k * NH + h, 2, :], v, start=True, stop=k == 0)
                        if k:
                            mm = pe.matmul(o, AR[r, c, k, 0, :], STATE[r, c, :], start=False, stop=True)
                    mm.then_inc(chunk_x, 1)
                    pe.wait_ge(chunk_x_out, k + 1)
                    for h in range(NH):
                        mm = pe.matmul(PS[:, 1, h * 64:(h + 1) * 64], TT[:, k * NH + h, :], XU[:, 0, h * 64:(h + 1) * 64],
                                       start=True, stop=True)
                    mm.then_inc(chunk_u, 1)
                    pe.wait_ge(chunk_u_out, k + 1)
                    for h in range(NH):
                        c, r = h // 2, slice(64 * (h % 2), 64 * (h % 2) + 64)
                        o = PS[:, 2 + 3 * (h % 2), c * 64:(c + 1) * 64]
                        pe.matmul(o, MASKED[:, k * NH + h, 1, :], XU[:, 1, h * 64:(h + 1) * 64], start=True, stop=False)
                        mm = pe.matmul(o, MASKED[:, k * NH + h, 3, :], VTOK[:, k, h * 64:(h + 1) * 64], start=False, stop=k == 0)
                        if k:
                            mm = pe.matmul(o, AR[r, c, k, 1, :], STATE[r, c, :], start=False, stop=True)
                    mm.then_inc(chunk_o, 1)
                    if k == 0:
                        for h in range(NH):
                            r = slice(64 * (h % 2), 64 * (h % 2) + 64)
                            o, hc = PS[r, 3, (h // 2) * 64:(h // 2 + 1) * 64], slice(h * 64, (h + 1) * 64)
                            pe.matmul(o, BTOK[:, hc], XU[:, 1, hc], start=True, stop=False)
                            mm = pe.matmul(o, KTOK[:, hc], VTOK[:, 0, hc], start=False, stop=True)
                        mm.then_inc(state_done, 1)

            def retention():
                pe.wait_ge(chunk_o_out, 2)
                for t in range(NT):
                    pe.wait_ge(rot_ready, t + 1)
                    for b in range(4):
                        mm = pe.transpose(PS[:, t, b * P:(b + 1) * P],
                                          ROT[:, t, 2 * b:2 * b + 2, :, :], ident)
                    mm.then_inc(rot_done, 1)
                pe.wait_ge(rot_out, 2)
                for h in range(RH):
                    r, b = slice(64 * (h % 2), 64 * (h % 2) + 64), h // 2
                    pe.matmul(PS[:, 4 + h, 0:256], QKT[r, 2 + b, 0:P], QKT[r, b, :], start=True, stop=True)
                    pe.matmul(PS[:, 4 + h, 256:384], QKT[r, 2 + b, P:S], QKT[r, b, P:S], start=True, stop=True).then_inc(score_done, 1)
                pe.wait_ge(score_out, RH)
                for t in range(NT):
                    for h in range(RH):
                        o = PS[:, 2 + t, h * 64:(h + 1) * 64]
                        v = [ZRET[:, j, 512 + h * 64:512 + (h + 1) * 64] for j in range(NT)]
                        if t == 0:
                            mm = pe.matmul(o, SCR[:, h, 0:P], v[0], start=True, stop=True)
                        else:
                            pe.matmul(o, SCR[:, h, P:256], v[0], start=True, stop=False)
                            mm = pe.matmul(o, SCR[:, h, 256:384], v[1], start=False, stop=True)
                    mm.then_inc(ret_o, 1)

            def gla():
                pe.wait_ge(score_out, RH)
                pe.wait_ge(gx_ready, 1)
                for n in range(9):
                    if n >= 1:
                        pe.wait_ge(gx_ready, n + 1)
                        if n < 8:
                            pe.wait_ge(gs_out, 2 * n)
                    for t in range(NT if n < 8 else 1):
                        for h in range(GH):
                            r, b = slice(64 * (h % 2), 64 * (h % 2) + 64), h // 2
                            bank = 4 + 2 * t + h % 2 if n < 8 else h % 2
                            if n == 0:
                                lhs, rhs = GQK[r, 2 + b, t * P:(t + 1) * P], GQK[r, b, t * P:(t + 1) * P]
                            elif n < 8:
                                lhs = rhs = GX[r, b, t * P:(t + 1) * P]
                            else:
                                lhs, rhs = GX[r, b, 0:P], GX[r, b, P:S]
                            mm = pe.matmul(PS[:, bank, b * P:(b + 1) * P], lhs, rhs, start=True, stop=True)
                        mm.then_inc(gs_done, 1)
                pe.wait_ge(gs_out, 17)
                for t in range(NT):
                    for h in range(GH):
                        o = PS[:, t, h * GDV:(h + 1) * GDV]
                        v = [ZGLA[:, j, h * GDV:(h + 1) * GDV] for j in range(NT)]
                        if t == 0:
                            mm = pe.matmul(o, GACC[:, 0, h, :], v[0], start=True, stop=True)
                        else:
                            pe.matmul(o, GACC[:, 2, h, :], v[0], start=True, stop=False)
                            mm = pe.matmul(o, GACC[:, 1, h, :], v[1], start=False, stop=True)
                    mm.then_inc(gla_o, 1)

            def project_out():
                pe.wait_ge(mix_ready, 1)
                for t in range(NT):
                    for c in range(DC):
                        mm = pe.transpose(PS[:, 2 * t + c // 4, (c % 4) * P:(c % 4 + 1) * P], HN[:, t, c * P:(c + 1) * P], ident)
                        if c % 4 == 3:
                            mm.then_inc(ot_done, 1)
                pe.wait_ge(ot_out, 4)
                for g in range(N_OUT):
                    n = N_IN + g
                    pe.wait_ge(ring_landed[n % 2], 16 * (n // 2 + 1))
                    w = RING[:, n % 2, :].rearrange("p (c n) -> p c n", c=2)
                    for i in range(2):
                        for t in range(NT):
                            for f in range(2):
                                mm = pe.matmul(PS[:, 4 + 2 * t + f, :], OT[:, 2 * g + i, t * P:(t + 1) * P], w[:, i, f * 512:(f + 1) * 512],
                                               start=g == 0 and i == 0, stop=g == N_OUT - 1 and i == 1, skip_group_check=True)
                    mm.then_inc(res_done, 1)
                    pe.wait_ge(res_done, g + 1)
                    pe.sem_inc(ring_free, 1)

            def queries():
                kn = N_IN + N_OUT
                for g in range(PH):
                    n = kn + 1 + g
                    if g == 0:
                        pe.wait_ge(ht_ready, 8)
                        pe.wait_ge(res_out, 4)
                    pe.wait_ge(ring_landed[n % 2], 16 * (n // 2 + 1))
                    if g >= 4:
                        pe.wait_ge(q_out, g - 3)
                    w = RING[:, n % 2, :].rearrange("p (c n) -> p c n", c=DC)
                    for b in range(2):
                        for c in range(DC):
                            mm = pe.matmul(PS[:, g % 4, b * 256:(b + 1) * 256], w[:, c, b * P:(b + 1) * P], HT[:, c, :],
                                           start=c == 0, stop=c == DC - 1)
                    mm.then_inc(q_done, 1)
                    pe.wait_ge(q_done, g + 1)
                    pe.sem_inc(ring_free, 1)
                for t in range(NT):
                    for m in range(4):
                        if t:
                            pe.wait_ge(sc_out, m + 1)
                        pe.wait_ge(q_out, 2 * m + 2 if t == 0 else PH)
                        for i in range(4):
                            b = 4 * m + i
                            mm = pe.matmul(PS[:, 4 + m, i * P:(i + 1) * P], QT[:, b, t * P:(t + 1) * P], KEYS[:, b, :],
                                           start=True, stop=True)
                        mm.then_inc(sc_done, 1)

            def turn_sel():
                pe.wait_ge(sel_ready, 1)
                for i, src in enumerate((I1F, I2F, GATE)):
                    for t in range(NT):
                        mm = pe.transpose(PS[:, i, t * P:(t + 1) * P], src[:, t * PH:(t + 1) * PH, :], ident)
                    mm.then_inc(sel_done, 1)

            def u_half(m, j, first, pool):
                e, f = m // 2, m % 2
                if pool:
                    pe.wait_ge(u_lo_pool, 8 * j + m + 1)
                else:
                    pe.wait_ge(u_lo, 8 * (j - POOL_BODIES) + m + 1)
                if f == 0:
                    if first and e < 2:
                        if e == 0:
                            pe.wait_ge(split_ready, 2)
                            pe.wait_ge(sc_out, 8)
                    else:
                        pe.wait_ge(u_act, 4 * j + e - 1)
                w_hi = EH[:, m % 4, :].rearrange("p (c n) -> p c n", c=4)
                w_lo = EL[:, m % 4, :].rearrange("p (c n) -> p c n", c=4)
                o = PS[:, 4 + e % 2, 0:S]
                for c in range(4):
                    d = 4 * f + c
                    pe.matmul(o, w_hi[:, c, :], HTH[:, d, :], start=d == 0, stop=False)
                    pe.matmul(o, w_hi[:, c, :], HTL[:, d, :], start=False, stop=False)
                    mm = pe.matmul(o, w_lo[:, c, :], HTH[:, d, :], start=False, stop=d == DC - 1)
                mm.then_inc(u_done, 1)

            def quad(i, q, first):
                pe.wait_ge(hot_gate, q + 1)
                pe.wait_ge(hot_pool, q + 1)
                if not first:
                    pe.wait_ge(quad_out, q - 2)
                for t in range(4):
                    mm = pe.matmul(PS[:, i, t * P:(t + 1) * P], HOT[i][:, 4 + t, :], HOT[i][:, t, :], start=True, stop=True)
                mm.then_inc(quad_done, 1)

            def v_half(m, j, first):
                e, f = m // 2, m % 2
                pe.wait_ge(v_lo, 8 * j + m + 1)
                pe.wait_ge(a_lo, 4 * j + e + 1)
                for t in range(NT):
                    o = PS[:, 2 * t + f, :]
                    a_hi_t, a_lo_t = AH[:, e % 2, t * P:(t + 1) * P], AL[:, e % 2, t * P:(t + 1) * P]
                    start = first and e == 0
                    pe.matmul(o, a_hi_t, EH[:, m % 4, :], start=start, stop=False, skip_group_check=True)
                    pe.matmul(o, a_hi_t, EL[:, m % 4, :], start=False, stop=False, skip_group_check=True)
                    mm = pe.matmul(o, a_lo_t, EH[:, m % 4, :], start=False, stop=True, skip_group_check=True)
                mm.then_inc(v_done, 1)

            with pe.Fori(0, L) as l:
                turn_h(HN, 0)
                for g in range(7):
                    group(g)
                lora()
                group(7)
                kk_norm()
                group(8)
                gk_up()
                group(9)
                gate_and_bonus()
                group(10)
                v_tok()
                for g in range(11, N_IN):
                    group(g)
                units()
                invert()
                chunks()
                retention()
                gla()
                project_out()
                turn_h(HNF, 1)
                queries()
                for m in range(8):
                    u_half(m, 0, True, True)
                with pe.Fori(1, POOL_BODIES) as j:
                    for m in range(8):
                        u_half(m, j, False, True)
                with pe.Fori(POOL_BODIES, SEL_BODY) as j:
                    for m in range(8):
                        u_half(m, j, False, False)
                turn_sel()
                with pe.Fori(SEL_BODY, N_BODY) as j:
                    for m in range(8):
                        u_half(m, j, False, False)
                pe.wait_ge(sel_out, 3)
                for i in range(3):
                    quad(i, i, True)
                with pe.Fori(1, 21) as q:
                    for i in range(3):
                        quad(i, 3 * q + i, False)
                quad(0, 63, False)
                for m in range(8):
                    v_half(m, 0, True)
                with pe.Fori(1, 32) as j:
                    for m in range(8):
                        v_half(m, j, False)
                pe.sem_inc(peer_done, 1)
                pe.wait_ge(v_done, 256)
                pe.sem_inc(arrived, 1)
                pe.wait_ge(go, l + 1)

        @block.scalar
        def _(act):
            act.wait_ge(const_landed, 32)
            steps = [0]

            def link(ins):
                steps[0] += 1
                ins.then_inc(act_step, 1)
                act.wait_ge(act_step, steps[0])

            def sumsq(k, dst):
                for t in range(NT):
                    act.activation(dst[:, t, :], X[:, t, :], ACT.Square, accum_out=STAT[:, 4 * k + t:4 * k + t + 1]).then_inc(sumsq_ready, 1)

            def root(k):
                act.wait_ge(rms_ready, k + 1)
                act.activation(STAT[:, 4 * k + 2:4 * k + 4], STAT[:, 4 * k:4 * k + 2], ACT.Sqrt).then_inc(rstd_ready, 1)

            def evac_h(col, k):
                for c in range(DC):
                    if c % 4 == 0:
                        act.wait_ge(h_turned, 4 * k + c // 4 + 1)
                    ins = act.activation(HT[:, c, 0:P], PS[:, c // 4, (c % 4) * P:(c % 4 + 1) * P], ACT.Identity, scale=COLS[:, col + c:col + c + 1])
                    if c % 4 == 3:
                        ins.then_inc(ht_ready, 1)

            def evac_group(g):
                act.wait_ge(proj_done, g + 1)
                ps = PS[:, g % 4, :].rearrange("p (b n) -> p b n", b=2)
                if g < 6:
                    if g == 0:
                        act.wait_ge(zeros_ready, 1)
                    if g >= 2:
                        act.wait_ge(mixed, g - 1)
                    ins = act.copy(RAW[:, g % 2, :, 1:257], ps)
                elif g == 6:
                    ins = act.mul(GQK[:, 0:2, :], ps, float(GDK) ** -0.5)
                elif g == 7:
                    ins = act.copy(GQK[:, 2:4, :], ps)
                elif g < 12:
                    ins = act.copy(ZRET[:, :, (g - 8) * 256:(g - 7) * 256], ps)
                else:
                    ins = act.copy(ZGLA[:, :, (g - 12) * 256:(g - 11) * 256], ps)
                ins.then_inc(proj_out, 1)

            def keys_out():
                n = N_IN + N_OUT
                act.wait_ge(ring_landed[n % 2], 16 * (n // 2 + 1))
                link(act.copy(KEYS, RING[:, n % 2, :].rearrange("p (b n) -> p b n", b=16)))
                act.sem_inc(keys_copied, 1)

            def u_split(m, j, first):
                if m % 4 == 0:
                    act.wait_ge(uring[m // 4], 16 * (j + 1))
                if first and m < 4:
                    if m == 0:
                        act.wait_ge(split_ready, 2)
                else:
                    act.wait_ge(u_done, 8 * j + m - 3)
                act.copy(EH[:, m % 4, :], RING[:, m // 4, (m % 4) * 512:(m % 4 + 1) * 512]).then_inc(u_hi, 1)

            def u_gelu(e, j):
                act.wait_ge(u_done, 8 * j + 2 * e + 2)
                act.activation(ACTS[:, 4 * j + e, :], PS[:, 4 + e % 2, 0:S], ACT.Gelu).then_inc(u_act, 1)

            def u_body(j, first):
                for m in range(8):
                    u_split(m, j, first)
                    if m == 1 and not first:
                        u_gelu(-1, j)
                    if m >= 3 and m % 2:
                        u_gelu(m // 2 - 1, j)

            def gate_rows(i, q):
                act.wait_ge(hot_eq, q + 1)
                for t in range(3):
                    ins = act.activation(HOT[i][:, 4 + t, :], HOT[i][:, 4 + t, :], ACT.Identity, scale=GATET[:, bass.ds(4 * q + t, 1)])
                ins.then_inc(hot_gate, 1)

            def v_split(m, j, first):
                if m % 4 == 0:
                    act.wait_ge(vring[m // 4], 16 * (j + 1))
                if first and m < 4:
                    if m == 0:
                        act.wait_ge(u_done, 256)
                else:
                    act.wait_ge(v_done, 8 * j + m - 3)
                act.copy(EH[:, m % 4, :], RING[:, m // 4, (m % 4) * 512:(m % 4 + 1) * 512]).then_inc(v_hi, 1)

            def a_split(e, j, first):
                if first and e < 2:
                    if e == 0:
                        act.wait_ge(quad_out, 64)
                else:
                    act.wait_ge(v_done, 8 * j + 2 * e - 2)
                act.copy(AH[:, e % 2, :], ACTS[:, 4 * j + e, :]).then_inc(a_hi, 1)

            with act.Fori(0, L) as l:
                steps[0] = 0
                act.wait_ge(params_landed, 64)
                sumsq(0, HN)
                root(0)
                evac_h(C_MIX, 0)
                for g in range(8):
                    evac_group(g)
                    if g == 6:
                        act.wait_ge(mixed, 6)
                        act.activation(FM[0:64, 0, :], FM[0:64, 0, :], ACT.Tanh).then_inc(tanh_ready, 1)
                        act.activation(FM[:, 1, :], FM[:, 1, :], ACT.Sigmoid).then_inc(sig_ready, 1)
                for c in range(CT):
                    act.wait_ge(lora_done, CT)
                    o = slice(c % 2 * 256, c % 2 * 256 + 256)
                    act.activation(SIGA[:, c, 0, :], PS[:, 4 + c // 2, o], ACT.Sigmoid, bias=COLS[:, C_WB + c:C_WB + c + 1]).then_inc(sig_ready, 1)
                    act.activation(SIGA[:, c, 1, :], PS[:, 6 + c // 2, o], ACT.Sigmoid, bias=COLS[:, C_AB + c:C_AB + c + 1]).then_inc(sig_ready, 1)
                evac_group(8)
                evac_group(9)
                act.wait_ge(cum_ready, 1)
                for c in range(CT):
                    for k in range(NT):
                        n = 16 + 2 * (c * NT + k)
                        act.activation(E1[:, c, k, :], CUM[:, c, k, :], ACT.Exp, bias=STAT[:, n:n + 1])
                        act.activation(E2[:, c, k * P:(k + 1) * P], CUM[:, c, k, 1:129], ACT.Exp, scale=-1.0, bias=STAT[:, n + 1:n + 2])
                act.activation(STAT[:, 28:31], CUM[:, :, 1, 64], ACT.Exp).then_inc(exp_ready, 1)
                act.wait_ge(kkmax_ready, 1)
                act.activation(KKN[:, :, :], KKN[:, :, :], ACT.Sqrt).then_inc(kksqrt_ready, 1)
                act.wait_ge(gk_out, 1)
                for b in range(2):
                    ins = act.activation(GE[:, b, :], GB[:, b, :], ACT.Abs)
                link(ins)
                link(act.activation(GE[:, :, :], GE[:, :, :], ACT.Exp, scale=-1.0))
                act.activation(GE[:, :, :], GE[:, :, :], ACT.Ln, bias=1.0).then_inc(gln_ready, 1)
                evac_group(10)
                for i in range(NT):
                    act.wait_ge(gg_done, i + 1)
                    act.copy(GG[:, i, :], PS[:, 6 + i, 0:390]).then_inc(gg_out, 1)
                for i in range(NT):
                    act.wait_ge(vtok_done, i + 1)
                    act.copy(VTOK[:, i, :], PS[:, 4 + i, 0:384]).then_inc(vtok_out, 1)
                for g in range(11, N_IN):
                    evac_group(g)
                for i in range(2):
                    act.wait_ge(bk_done, i + 1)
                    act.copy((BTOK, KTOK)[i], PS[:, 4 + i, 0:384]).then_inc(bk_out, 1)
                act.wait_ge(proj_out, N_IN)
                act.activation(ZRET[:, :, 768:1024], ZRET[:, :, 768:1024], ACT.Silu).then_inc(silu_ready, 1)
                act.activation(ZGLA[:, :, 384:768], ZGLA[:, :, 384:768], ACT.Silu).then_inc(silu_ready, 1)
                act.wait_ge(var_ready, 1)
                act.activation(STAT[:, 44:56], STAT[:, 32:44], ACT.Sqrt).then_inc(sd_ready, 1)
                act.wait_ge(var_ready, 2)
                act.activation(STAT[:, 44:52], STAT[:, 32:40], ACT.Sqrt).then_inc(sd_ready, 1)
                for n in range(8):
                    act.wait_ge(gd_ready, n + 1)
                    act.activation(GE[:, :, :], GE[:, :, :], ACT.Exp).then_inc(ge_ready, 1)
                act.wait_ge(var_ready, 3)
                act.activation(STAT[:, 44:52], STAT[:, 32:40], ACT.Sqrt).then_inc(sd_ready, 1)
                for t in range(NT):
                    for m in range(2):
                        act.wait_ge(ot_done, 2 * t + m + 1)
                        act.copy(OT[:, 4 * m:4 * m + 4, t * P:(t + 1) * P],
                                 PS[:, 2 * t + m, :].rearrange("p (c n) -> p c n", c=4)).then_inc(ot_out, 1)
                act.wait_ge(res_out, 4)
                sumsq(1, HNF)
                root(1)
                keys_out()
                evac_h(C_FFN, 1)
                act.wait_ge(ht_ready, 8)
                act.copy(HTH[:, :, :], HT[:, :, :]).then_inc(split_ready, 1)
                for g in range(PH):
                    act.wait_ge(q_done, g + 1)
                    act.copy(QT[:, 2 * g:2 * g + 2, :], PS[:, g % 4, :].rearrange("p (b n) -> p b n", b=2)).then_inc(q_out, 1)
                for t in range(NT):
                    for m in range(4):
                        act.wait_ge(sc_done, 4 * t + m + 1)
                        act.copy(SC[:, 16 * t + 4 * m:16 * t + 4 * m + 4, :], PS[:, 4 + m, :].rearrange("p (b n) -> p b n", b=4)).then_inc(sc_out, 1)
                u_body(0, True)
                with act.Fori(1, EXP_BODY) as j:
                    u_body(j, False)
                act.wait_ge(gdiff_ready, 1)
                act.activation(GATE[:, :, :], GATE[:, :, :], ACT.Exp).then_inc(gexp_ready, 1)
                with act.Fori(EXP_BODY, SEL_BODY) as j:
                    u_body(j, False)
                pair = IDXQ[:, :, :].rearrange("p q (m t) -> p m q t", m=2)
                for i in range(3):
                    act.wait_ge(sel_done, i + 1)
                    src = PS[:, i, 0:S]
                    if i < 2:
                        act.copy(pair[:, 1 - i], src.rearrange("p (q t) -> p q t", t=4)).then_inc(sel_out, 1)
                    else:
                        act.copy(GATET[:, :], src).then_inc(sel_out, 1)
                with act.Fori(SEL_BODY, N_BODY) as j:
                    u_body(j, False)
                u_gelu(-1, N_BODY)
                for i in range(3):
                    gate_rows(i, i)
                with act.Fori(1, 21) as q:
                    for i in range(3):
                        gate_rows(i, 3 * q + i)
                gate_rows(0, 63)
                act.wait_ge(quad_out, 64)
                for m in range(8):
                    if m % 2 == 0:
                        a_split(m // 2, 0, True)
                    v_split(m, 0, True)
                with act.Fori(1, 32) as j:
                    for m in range(8):
                        if m % 2 == 0:
                            a_split(m // 2, j, False)
                        v_split(m, j, False)
                act.wait_ge(v_hi, 256)
                act.sem_inc(arrived, 1)
                act.wait_ge(go, l + 1)
            for t in range(NT):
                act.activation(YOUT[:, t, :], X[:, t, :], ACT.Square, accum_out=STAT[:, t:t + 1]).then_inc(final_ss, 1)
            act.wait_ge(final_ms, 1)
            act.activation(STAT[:, 2:4], STAT[:, 0:2], ACT.Sqrt).then_inc(final_rt, 1)

        @block.vector
        def _(dve):
            dve.wait_ge(const_landed, 32)
            steps = [0]

            def link(ins):
                steps[0] += 1
                ins.then_inc(dve_step, 1)
                dve.wait_ge(dve_step, steps[0])

            def norm_rows(k, dst):
                dve.wait_ge(sumsq_ready, NT * (k + 1))
                a = 4 * k
                link(dve.tensor_scalar(STAT[:, a:a + 2], STAT[:, a:a + 2], 1.0 / D, NORM_EPS, ALU.mult, ALU.add))
                dve.sem_inc(rms_ready, 1)
                dve.wait_ge(rstd_ready, k + 1)
                link(dve.reciprocal(STAT[:, a:a + 2], STAT[:, a + 2:a + 4]))
                for t in range(NT):
                    dve.tensor_scalar(dst[:, t, :], X[:, t, :], STAT[:, a + t:a + t + 1], None, ALU.mult).then_inc(h_ready, 1)

            def evac_h(col, k):
                for c in range(DC):
                    if c % 4 == 0:
                        dve.wait_ge(h_turned, 4 * k + 3 + c // 4)
                    ins = dve.tensor_scalar(HT[:, c, P:S], PS[:, 2 + c // 4, (c % 4) * P:(c % 4 + 1) * P], COLS[:, col + c:col + c + 1], None, ALU.mult)
                    if c % 4 == 3:
                        ins.then_inc(ht_ready, 1)

            def mix(g):
                dve.wait_ge(proj_out, g + 1)
                r = RAW[:, g % 2, :, :]
                link(dve.tensor_tensor(TMP[:, 0:2, :], r[:, :, 0:256], r[:, :, 1:257], ALU.subtract))
                for b in range(2):
                    n = 2 * g + b
                    if n < 11:
                        ins = dve.scalar_tensor_tensor(FM[:, n, :], TMP[:, b, :], COLS[:, C_MU + n:C_MU + n + 1], r[:, b, 1:257], ALU.mult, ALU.add)
                    else:
                        ins = dve.tensor_copy(FM[:, n, :], r[:, b, 1:257])
                    link(ins)
                dve.sem_inc(mixed, 1)

            def col(n, c):
                return COLS[:, n + c:n + c + 1]

            def rwkv_prep():
                K, R = FM[:, 2:5, :], FM[:, 5:8, :]
                for c in range(CT):
                    ins = dve.tensor_scalar(BT[:, c, :], K[:, c, :], col(C_KK, c), None, ALU.mult)
                link(ins)
                dve.tensor_tensor(TMP[:, :, :], BT[:, :, :], BT[:, :, :], ALU.mult).then_inc(kksq_ready, 1)
                dve.wait_ge(sig_ready, 7)
                link(dve.tensor_scalar(E2[:, :, :], SIGA[:, :, 0, :], LOG_DECAY_SCALE, None, ALU.mult))
                dve.memset(CUM[:, :, :, 0:1], 0.0)
                for c in range(CT):
                    for k in range(NT):
                        ins = dve.tensor_tensor_scan(CUM[:, c, k, 1:129], XC[:, X_ONES:X_ONES + 1].broadcast_to([P, P]), E2[:, c, k * P:(k + 1) * P], 0.0, ALU.mult, ALU.add)
                link(ins)
                for c in range(CT):
                    for k in range(NT):
                        n = 16 + 2 * (c * NT + k)
                        dve.tensor_scalar(STAT[:, n:n + 1], CUM[:, c, k, 64:65], -1.0, None, ALU.mult)
                        ins = dve.tensor_copy(STAT[:, n + 1:n + 2], CUM[:, c, k, 64:65])
                link(ins)
                dve.sem_inc(cum_ready, 1)
                for c in range(CT):
                    ins = dve.tensor_scalar(KT[:, c, :], SIGA[:, c, 1, :], 1.0, col(C_KA, c), ALU.subtract, ALU.mult)
                link(ins)
                link(dve.scalar_tensor_tensor(KT[:, :, :], KT[:, :, :], 1.0, K, ALU.add, ALU.mult))
                dve.wait_ge(kknorm_done, 1)
                dve.tensor_scalar(KKN[:, 0:2, :], PS[:, 7, :].rearrange("p (c n) -> p c n", c=2), 1e-24, None, ALU.max)
                link(dve.tensor_scalar(KKN[:, 2, :], PS[:, 4, 0:256], 1e-24, None, ALU.max))
                dve.sem_inc(kkmax_ready, 1)
                for c in range(CT):
                    ins = dve.scalar_tensor_tensor(TMP[:, c, :], R[:, c, :], col(C_RK, c), KT[:, c, :], ALU.mult, ALU.mult)
                link(ins)
                dve.sem_inc(rk_ready, 1)
                dve.wait_ge(kksqrt_ready, 1)
                link(dve.reciprocal(KKN[:, :, :], KKN[:, :, :]))
                link(dve.tensor_tensor(KKN[:, :, :], KKN[:, :, :], BT[:, :, :], ALU.mult))
                dve.wait_ge(exp_ready, 1)
                for c in range(CT):
                    for k in range(NT):
                        s = slice(k * P, (k + 1) * P)
                        dve.scalar_tensor_tensor(AR[:, c, k, 0, :], KKN[:, c, s], -1.0, E1[:, c, k, 0:128], ALU.mult, ALU.mult)
                        dve.tensor_tensor(AR[:, c, k, 1, :], R[:, c, s], E1[:, c, k, 1:129], ALU.mult)
                link(dve.tensor_tensor(BT[:, :, :], KKN[:, :, :], SIGA[:, :, 1, :], ALU.mult))
                dve.tensor_tensor(BT[:, :, :], BT[:, :, :], E2[:, :, :], ALU.mult)
                link(dve.tensor_tensor(KT[:, :, :], KT[:, :, :], E2[:, :, :], ALU.mult))
                link(dve.tensor_tensor(STAT[:, 28:31], STAT[:, 28:31], E1[:, :, 0, 128], ALU.mult))
                dve.sem_inc(ab_ready, 1)

            def gla_gates_in():
                dve.wait_ge(gk_done, 1)
                for b in range(2):
                    ins = dve.tensor_scalar(GB[:, b, :], PS[:, 5, b * 256:(b + 1) * 256], col(C_GB, b), None, ALU.add)
                link(ins)
                dve.sem_inc(gk_out, 1)

            def gla_gates():
                dve.wait_ge(gln_ready, 1)
                link(dve.scalar_tensor_tensor(GX[:, :, :], GB[:, :, :], 0.0, GE[:, :, :], ALU.min, ALU.subtract))
                link(dve.tensor_scalar(GX[:, :, :], GX[:, :, :], 1.0 / 16.0, None, ALU.mult))
                for b in range(2):
                    ins = dve.tensor_tensor_scan(GB[:, b, :], XC[:, X_ONES:X_ONES + 1].broadcast_to([P, S]), GX[:, b, :], 0.0, ALU.mult, ALU.add)
                link(ins)

            def rwkv_units():
                mask2 = XC[:, X_MASK2:X_MASK2 + 256].unsqueeze(1).broadcast_to([P, 2, 256])
                for u in range(12):
                    dve.wait_ge(unit_done, u + 1)
                    dve.tensor_tensor(MASKED[:, u, :, :].rearrange("p (a b) n -> p a (b n)", a=2), PS[:, 4 + u % 4, :].rearrange("p (a n) -> p a n", a=2), mask2,
                                      ALU.mult).then_inc(unit_out, 1)
                low1 = XC[:, X_LOW:X_LOW + P].unsqueeze(1).broadcast_to([P, 4, P])
                up1 = XC[:, X_UP:X_UP + P].unsqueeze(1).broadcast_to([P, 12, P])
                id12 = ident.unsqueeze(1).broadcast_to([P, 12, P])
                ti_pairs = TI.rearrange("p (e r) n -> p r e n", r=2)
                for m in range(4):
                    n, e0, r = (4, 0, m) if m < 2 else (2, 4, m - 2)
                    dve.wait_ge(mrow_done, m + 1)
                    dve.tensor_tensor(ti_pairs[:, r, e0:e0 + n, :], PS[:, 2 * r + e0 // 4, 0:n * P].rearrange("p (u n) -> p u n", u=n), low1[:, 0:n, :],
                                      ALU.mult).then_inc(mrow_out, 1)
                dve.wait_ge(unit_out, 12)
                dve.wait_ge(mrow_out, 4)
                dve.tensor_tensor(TI[:, :, :], TI[:, :, :], id12, ALU.add).then_inc(mrow_out, 1)
                dve.tensor_tensor(TT[:, :, :], MASKED[:, :, 0, :], up1, ALU.mult).then_inc(mrow_out, 1)
                dve.wait_ge(mrow_out, 6)
                dve.tensor_tensor(TT[:, :, :], TT[:, :, :], id12, ALU.add).then_inc(mrow_out, 1)
                for n, b in enumerate(LEVELS[1:]):
                    low = XC[:, X_LOW + P * (n + 1):X_LOW + P * (n + 2)]
                    for k in range(NT):
                        dve.wait_ge(y_done, 2 * n + k + 1)
                        u0 = k * NH
                        dve.tensor_tensor(Y[:, u0:u0 + NH, :], PS[:, 2 * k:2 * k + 2, :].rearrange("p a n -> p (a n)")[:, 0:768].rearrange("p (u n) -> p u n", u=NH),
                                          low.unsqueeze(1).broadcast_to([P, NH, P]), ALU.mult).then_inc(y_out, 1)
                    for k in range(NT):
                        dve.wait_ge(z_done, 2 * n + k + 1)
                        u0 = k * NH
                        for i, dst in enumerate((TI, TT)):
                            z = PS[:, 4 + 2 * k + i, 0:384]
                            if b < 64:
                                half = dst[:, u0:u0 + NH, :].rearrange("p u (q a b) -> p (u q) a b", a=2, b=b)[:, :, i, :]
                                zz = z.rearrange("p (m b) -> p m b", b=b)
                            else:
                                half = dst[:, u0:u0 + NH, 64 * i:64 * i + 64]
                                zz = z.rearrange("p (m b) -> p m b", b=64)
                            ins = dve.tensor_tensor(half, half, zz, ALU.add)
                        ins.then_inc(z_out, 1)

            def rwkv_chunks():
                for k in range(NT):
                    dve.wait_ge(chunk_x, k + 1)
                    for r in range(2):
                        ins = dve.tensor_copy(XU[:, 0, :].rearrange("p (c r n) -> p r c n", c=CT, r=2)[:, r], PS[:, 4 * r, 0:192].rearrange("p (c n) -> p c n", c=CT))
                    ins.then_inc(chunk_x_out, 1)
                    dve.wait_ge(chunk_u, k + 1)
                    dve.tensor_copy(XU[:, 1, :], PS[:, 1, 0:384]).then_inc(chunk_u_out, 1)
                    if k == 0:
                        dve.wait_ge(state_done, 1)
                        dve.tensor_tensor(STATE[:, :, :], PS[:, 3, 0:192].rearrange("p (c n) -> p c n", c=CT),
                                          STAT[:, 28:31].unsqueeze(2).broadcast_to([P, CT, 64]), ALU.mult).then_inc(state_out, 1)
                    dve.wait_ge(chunk_o, k + 1)
                    for r in range(2):
                        ins = dve.tensor_copy(HN[:, k, 256:640].rearrange("p (c r n) -> p r c n", c=CT, r=2)[:, r], PS[:, 2 + 3 * r, 0:192].rearrange("p (c n) -> p c n", c=CT))
                    ins.then_inc(chunk_o_out, 1)

            def rwkv_out():
                dve.wait_ge(chunk_o_out, 2)
                O = HN[:, :, 256:640]
                for t in range(NT):
                    ins = dve.tensor_reduce(STAT[:, 32 + 6 * t:38 + 6 * t], O[:, t, :].rearrange("p (h n) -> p h n", h=NH), AX.X, ALU.add)
                link(ins)
                link(dve.tensor_scalar(STAT[:, 32:44], STAT[:, 32:44], 1.0 / 64, None, ALU.mult))
                for t in range(NT):
                    o = O[:, t, :].rearrange("p (h n) -> p h n", h=NH)
                    ins = dve.tensor_tensor(o, o, STAT[:, 32 + 6 * t:38 + 6 * t].unsqueeze(2).broadcast_to([P, NH, 64]), ALU.subtract)
                link(ins)
                link(dve.tensor_tensor(XB[:, :, :], O, O, ALU.mult))
                link(dve.tensor_reduce(STAT[:, 32:44], XB[:, :, :].rearrange("p t (h n) -> p (t h) n", h=NH), AX.X, ALU.add))
                link(dve.tensor_scalar(STAT[:, 32:44], STAT[:, 32:44], 1.0 / 64, GN_EPS, ALU.mult, ALU.add))
                dve.sem_inc(var_ready, 1)
                dve.wait_ge(sd_ready, 1)
                link(dve.reciprocal(STAT[:, 44:56], STAT[:, 44:56]))
                for t in range(NT):
                    o = O[:, t, :].rearrange("p (h n) -> p h n", h=NH)
                    link(dve.tensor_tensor(o, o, STAT[:, 44 + 6 * t:50 + 6 * t].unsqueeze(2).broadcast_to([P, NH, 64]), ALU.mult))
                    link(dve.tensor_tensor(O[:, t, :], O[:, t, :], ROWS[:, 0:384], ALU.mult))
                    link(dve.tensor_tensor(O[:, t, :], O[:, t, :], ROWS[:, 384:768], ALU.add))
                    link(dve.tensor_tensor(XB[:, t, :].rearrange("p (h n) -> p h n", h=NH), VTOK[:, t, :].rearrange("p (h n) -> p h n", h=NH),
                                           GG[:, t, 384:390].unsqueeze(2).broadcast_to([P, NH, 64]), ALU.mult))
                    link(dve.tensor_tensor(O[:, t, :], O[:, t, :], XB[:, t, :], ALU.add))
                    link(dve.tensor_tensor(O[:, t, :], O[:, t, :], GG[:, t, 0:384], ALU.mult))

            def head_rms(n, o, dst, heads, w, gate):
                for t in range(NT):
                    link(dve.tensor_copy(dst[:, t, :], o[t]))
                if n == 2:
                    dve.sem_inc(ret_o_out, 1)
                else:
                    dve.sem_inc(gla_o_out, 1)
                link(dve.tensor_tensor(XB[:, :, 0:heads * w], dst, dst, ALU.mult))
                for t in range(NT):
                    ins = dve.tensor_reduce(STAT[:, 32 + heads * t:32 + heads * (t + 1)],
                                            XB[:, t, 0:heads * w].rearrange("p (h n) -> p h n", h=heads), AX.X, ALU.add)
                link(ins)
                link(dve.tensor_scalar(STAT[:, 32:32 + 2 * heads], STAT[:, 32:32 + 2 * heads], 1.0 / w, HEAD_EPS, ALU.mult, ALU.add))
                dve.sem_inc(var_ready, 1)
                dve.wait_ge(sd_ready, n)
                link(dve.reciprocal(STAT[:, 44:44 + 2 * heads], STAT[:, 44:44 + 2 * heads]))
                for t in range(NT):
                    d = dst[:, t, :].rearrange("p (h n) -> p h n", h=heads)
                    link(dve.tensor_tensor(d, d, STAT[:, 44 + heads * t:44 + heads * (t + 1)].unsqueeze(2).broadcast_to([P, heads, w]), ALU.mult))
                link(dve.tensor_tensor(dst, dst, gate, ALU.mult))

            def retention():
                for t in range(NT):
                    z = ZRET[:, t, 0:512].rearrange("p (g h c) -> p g h c", g=8, h=2)
                    rope = XC[:, X_ROPE + 64 * t:X_ROPE + 64 * (t + 1)].rearrange("p (a c) -> p a c", a=2)
                    cos, sin = (rope[:, a, :].unsqueeze(1).broadcast_to([P, 8, 32]) for a in range(2))
                    tmp = XB[:, t, 0:256].rearrange("p (g c) -> p g c", g=8)
                    dve.tensor_tensor(ROT[:, t, :, 0, :], z[:, :, 0, :], cos, ALU.mult)
                    link(dve.tensor_tensor(tmp, z[:, :, 1, :], sin, ALU.mult))
                    link(dve.tensor_tensor(ROT[:, t, :, 0, :], ROT[:, t, :, 0, :], tmp, ALU.subtract))
                    dve.tensor_tensor(ROT[:, t, :, 1, :], z[:, :, 0, :], sin, ALU.mult)
                    link(dve.tensor_tensor(tmp, z[:, :, 1, :], cos, ALU.mult))
                    link(dve.tensor_tensor(ROT[:, t, :, 1, :], ROT[:, t, :, 1, :], tmp, ALU.add))
                    dve.sem_inc(rot_ready, 1)
                for t in range(NT):
                    dve.wait_ge(rot_done, t + 1)
                    dve.tensor_copy(QKT[:, :, t * P:(t + 1) * P], PS[:, t, :].rearrange("p (b n) -> p b n", b=4)).then_inc(rot_out, 1)
                for h in range(RH):
                    dm = XC[:, X_DM + 256 * h:X_DM + 256 * (h + 1)]
                    dve.wait_ge(score_done, h + 1)
                    dve.tensor_tensor(SCR[:, h, 0:256], PS[:, 4 + h, 0:256], dm, ALU.mult)
                    dve.tensor_tensor(SCR[:, h, 256:384], PS[:, 4 + h, 256:384], dm[:, 0:P], ALU.mult).then_inc(score_out, 1)

            def gla_levels():
                link(dve.memset(GACC[:, 0:2, :, :], 0.0))
                dve.sem_inc(gx_ready, 1)
                gacc = GACC.rearrange("p t (c r) n -> p t r c n", r=2)
                masks = [ident] + [XC[:, X_UP + P * n:X_UP + P * (n + 1)] for n in range(7)]
                for n in range(9):
                    if n >= 1:
                        b = 2 ** (n - 1)
                        B, E, XX = (v[:, :, :].rearrange("p b (q a n) -> p (b q) a n", a=2, n=b) for v in (GB, GE, GX))
                        Q, K = (v.rearrange("p b (q a n) -> p (b q) a n", a=2, n=b) for v in (GQK[:, 0:2, :], GQK[:, 2:4, :]))
                        nb = 2 * S // (2 * b)
                        ref = B[:, :, 0, b - 1:b].broadcast_to([P, nb, b])
                        if n >= 2:
                            dve.wait_ge(gs_done, 2 * n)
                        dve.tensor_tensor(E[:, :, 0, :], ref, B[:, :, 0, :], ALU.subtract)
                        link(dve.tensor_tensor(E[:, :, 1, :], B[:, :, 1, :], ref, ALU.subtract))
                        dve.sem_inc(gd_ready, 1)
                        dve.wait_ge(ge_ready, n)
                        dve.tensor_tensor(XX[:, :, 0, :], K[:, :, 0, :], E[:, :, 0, :], ALU.mult)
                        link(dve.tensor_tensor(XX[:, :, 1, :], Q[:, :, 1, :], E[:, :, 1, :], ALU.mult))
                        dve.sem_inc(gx_ready, 1)
                    if n < 8:
                        mask = masks[n].bitcast(U32).unsqueeze(1).broadcast_to([P, 2, P])
                        for t in range(NT):
                            dve.wait_ge(gs_done, 2 * n + t + 1)
                            for r in range(2):
                                ins = dve.copy_predicated(gacc[:, t, r], mask, PS[:, 4 + 2 * t + r, 0:256].rearrange("p (c n) -> p c n", c=2))
                            ins.then_inc(gs_out, 1)
                    else:
                        dve.wait_ge(gs_done, 17)
                        for r in range(2):
                            ins = dve.tensor_copy(gacc[:, 2, r], PS[:, r, 0:256].rearrange("p (c n) -> p c n", c=2))
                        ins.then_inc(gs_out, 1)

            def topk():
                for t in range(NT):
                    dve.wait_ge(sc_out, 4 * t + 4)
                    us = range(16 * t, 16 * t + 16)
                    for u in us:
                        ins = dve.max(VAL[:, u, 0:8], SC[:, u, :])
                    link(ins)
                    for u in us:
                        dve.max_index(IDX[:, u, 0:8].bitcast(U32), VAL[:, u, 0:8], SC[:, u, :])
                        ins = dve.match_replace(SC2[:, u % 16, :], VAL[:, u, 0:8], SC[:, u, :], NEG)
                    link(ins)
                    for u in us:
                        ins = dve.max(VAL[:, u, 8:16], SC2[:, u % 16, :])
                    link(ins)
                    for u in us:
                        ins = dve.max_index(IDX[:, u, 8:16].bitcast(U32), VAL[:, u, 8:16], SC2[:, u % 16, :])
                    link(ins)
                link(dve.tensor_copy(IDXF[:, :, :], IDX[:, :, :].bitcast(U32)))
                v = VAL[:, :, :].rearrange("p (u h) n -> p u h n", h=2)
                x = IDXF[:, :, :].rearrange("p (u h) n -> p u h n", h=2)
                o = 0
                for i in range(8):
                    n = CAND_ROWS[i]
                    dve.tensor_tensor(CAND[:, :, o:o + n], v[:, :, 0, i:i + 1].broadcast_to([P, 16, n]), v[:, :, 1, 0:n], ALU.add)
                    dve.scalar_tensor_tensor(CIDX[:, :, o:o + n], x[:, :, 0, i:i + 1].broadcast_to([P, 16, n]), float(NKEYS), x[:, :, 1, 0:n], ALU.mult, ALU.add)
                    o += n
                dve.tensor_tensor(CAND[:, :, o:o + 8], v[:, :, 0, 8:16], v[:, :, 1, 0:1].broadcast_to([P, 16, 8]), ALU.add)
                link(dve.scalar_tensor_tensor(CIDX[:, :, o:o + 8], x[:, :, 0, 8:16], float(NKEYS), x[:, :, 1, 0:1].broadcast_to([P, 16, 8]), ALU.mult, ALU.add))
                for u in range(16):
                    ins = dve.max(TOPV[:, u, 0:8], CAND[:, u, :])
                link(ins)
                for u in range(16):
                    dve.max_index(POS[:, u, 0:8].bitcast(U32), TOPV[:, u, 0:8], CAND[:, u, :])
                    ins = dve.match_replace(CAND2[:, u, :], TOPV[:, u, 0:8], CAND[:, u, :], NEG)
                link(ins)
                for u in range(16):
                    ins = dve.max(TOPV[:, u, 8:16], CAND2[:, u, :])
                link(ins)
                for u in range(16):
                    ins = dve.max_index(POS[:, u, 8:16].bitcast(U32), TOPV[:, u, 8:16], CAND2[:, u, :])
                link(ins)
                link(dve.tensor_tensor(GATE[:, :, :], TOPV[:, :, :], TOPV[:, :, 0:1].broadcast_to([P, 16, 16]), ALU.subtract))
                dve.sem_inc(gdiff_ready, 1)
                link(dve.tensor_copy(POSF[:, :, :], POS[:, :, :].bitcast(U32)))
                cpos = iota[:, 0:NC].unsqueeze(1).broadcast_to([P, 16, NC])
                for u in range(16):
                    e = EQ[:, u % 2, :, :]
                    link(dve.tensor_tensor(e, POSF[:, u, :].unsqueeze(2).broadcast_to([P, 16, NC]), cpos, ALU.is_equal))
                    link(dve.tensor_tensor(e, e, CIDX[:, u, :].unsqueeze(1).broadcast_to([P, 16, NC]), ALU.mult))
                    ins = dve.tensor_reduce(EIDX[:, u, :], e, AX.X, ALU.add)
                link(ins)
                link(dve.tensor_copy(POS[:, :, :].bitcast(I32), EIDX[:, :, :]))
                dve.tensor_scalar(I1F[:, :, :].bitcast(I32), POS[:, :, :].bitcast(I32), 7, None, ALU.logical_shift_right)
                link(dve.tensor_scalar(I2F[:, :, :].bitcast(I32), POS[:, :, :].bitcast(I32), NKEYS - 1, None, ALU.bitwise_and))
                dve.tensor_copy(I1F[:, :, :], I1F[:, :, :].bitcast(I32))
                dve.tensor_copy(I2F[:, :, :], I2F[:, :, :].bitcast(I32))

            def gates():
                dve.wait_ge(gexp_ready, 1)
                link(dve.tensor_reduce(STAT[:, 16:32], GATE[:, :, :], AX.X, ALU.add))
                link(dve.reciprocal(STAT[:, 32:48], STAT[:, 16:32]))
                link(dve.tensor_tensor(GATE[:, :, :], GATE[:, :, :], STAT[:, 32:48].unsqueeze(2).broadcast_to([P, 16, 16]), ALU.mult))
                dve.sem_inc(sel_ready, 1)

            def u_lows(m, j):
                dve.wait_ge(u_hi, 8 * j + m + 1)
                dve.tensor_tensor(EL[:, m % 4, :], RING[:, m // 4, (m % 4) * 512:(m % 4 + 1) * 512], EH[:, m % 4, :].bitcast(F32), ALU.subtract).then_inc(u_lo, 1)

            def v_lows(m, j):
                dve.wait_ge(v_hi, 8 * j + m + 1)
                dve.tensor_tensor(EL[:, m % 4, :], RING[:, m // 4, (m % 4) * 512:(m % 4 + 1) * 512], EH[:, m % 4, :].bitcast(F32), ALU.subtract).then_inc(v_lo, 1)

            def a_lows(e, j):
                dve.wait_ge(a_hi, 4 * j + e + 1)
                dve.tensor_tensor(AL[:, e % 2, :], ACTS[:, 4 * j + e, :], AH[:, e % 2, :].bitcast(F32), ALU.subtract).then_inc(a_lo, 1)

            def hots(i, q, first):
                if not first:
                    dve.wait_ge(quad_done, q - 2)
                dve.tensor_tensor(HOT[i][:, 0:7, :], iota.unsqueeze(1).broadcast_to([P, 7, P]),
                                  IDXQ[:, bass.ds(q, 1), 0:7].rearrange("p a m -> p (a m)").unsqueeze(2).broadcast_to([P, 7, P]), ALU.is_equal).then_inc(hot_eq, 1)

            def gated(i, q):
                dve.wait_ge(quad_done, q + 1)
                a = ACTS[:, :, bass.ds(4 * q, 4)]
                dve.tensor_tensor(a, a, PS[:, i, :].rearrange("p (t e) -> p e t", t=4), ALU.mult).then_inc(quad_out, 1)

            with dve.Fori(0, L) as l:
                steps[0] = 0
                norm_rows(0, HN)
                dve.wait_ge(params_landed, 64)
                evac_h(C_MIX, 0)
                for g in range(6):
                    mix(g)
                rwkv_prep()
                gla_gates_in()
                gla_gates()
                rwkv_units()
                rwkv_chunks()
                rwkv_out()
                retention()
                dve.wait_ge(ret_o, 2)
                dve.wait_ge(silu_ready, 2)
                head_rms(2, [PS[:, 2 + t, 0:256] for t in range(NT)], HN[:, :, 0:256], RH, 64, ZRET[:, :, 768:1024])
                gla_levels()
                dve.wait_ge(gla_o, 2)
                gdst = HN[:, :, 640:1024]
                head_rms(3, [PS[:, t, 0:384] for t in range(NT)], gdst, GH, GDV, ZGLA[:, :, 384:768])
                for t in range(NT):
                    link(dve.tensor_tensor(gdst[:, t, :], gdst[:, t, :], ROWS[:, 768:1152], ALU.mult))
                dve.sem_inc(mix_ready, 1)
                dve.wait_ge(res_done, N_OUT)
                for t in range(NT):
                    for f in range(2):
                        xs = X[:, t, f * 512:(f + 1) * 512]
                        dve.tensor_tensor(xs, xs, PS[:, 4 + 2 * t + f, :], ALU.add).then_inc(res_out, 1)
                dve.wait_ge(res_out, 4)
                norm_rows(1, HNF)
                evac_h(C_FFN, 1)
                dve.wait_ge(split_ready, 1)
                dve.tensor_tensor(HTL[:, :, :], HT[:, :, :], HTH[:, :, :].bitcast(F32), ALU.subtract).then_inc(split_ready, 1)
                topk()
                with dve.Fori(POOL_BODIES, GATE_BODY) as j:
                    for m in range(8):
                        u_lows(m, j)
                gates()
                with dve.Fori(GATE_BODY, N_BODY) as j:
                    for m in range(8):
                        u_lows(m, j)
                dve.wait_ge(u_act, 128)
                dve.wait_ge(sel_out, 3)
                for i in range(3):
                    hots(i, i, True)
                gated(0, 0)
                with dve.Fori(1, 21) as q:
                    for i in range(3):
                        hots(i, 3 * q + i, False)
                        gated((i + 1) % 3, 3 * q + i - 2)
                hots(0, 63, False)
                for q in range(61, 64):
                    gated(q % 3, q)
                for m in range(8):
                    if m % 2 == 0:
                        a_lows(m // 2, 0)
                    v_lows(m, 0)
                with dve.Fori(1, 32) as j:
                    for m in range(8):
                        if m % 2 == 0:
                            a_lows(m // 2, j)
                        v_lows(m, j)
                dve.wait_ge(v_done, 256)
                for t in range(NT):
                    for f in range(2):
                        xs = X[:, t, f * 512:(f + 1) * 512]
                        link(dve.tensor_tensor(xs, xs, PS[:, 2 * t + f, :], ALU.add))
                dve.sem_inc(peer_out, 1)
                dve.sem_inc(arrived, 1)
                dve.wait_ge(go, l + 1)
            dve.wait_ge(final_ss, NT)
            dve.tensor_scalar(STAT[:, 0:2], STAT[:, 0:2], 1.0 / D, NORM_EPS, ALU.mult, ALU.add).then_inc(final_ms, 1)
            dve.wait_ge(final_rt, 1)
            dve.reciprocal(STAT[:, 0:2], STAT[:, 2:4]).then_inc(final_ms, 1)
            dve.wait_ge(final_ms, 2)
            dve.wait_ge(final_row, 16)
            for t in range(NT):
                dve.scalar_tensor_tensor(YOUT[:, t, :], X[:, t, :], STAT[:, t:t + 1], FROW, ALU.mult, ALU.mult).then_inc(y_ready, 1)

        @block.gpsimd
        def _(pool):
            pool.wait_ge(const_landed, 32)

            def u_lows(m, j):
                pool.wait_ge(u_hi, 8 * j + m + 1)
                pool.tensor_tensor(EL[:, m % 4, :], RING[:, m // 4, (m % 4) * 512:(m % 4 + 1) * 512], EH[:, m % 4, :].bitcast(F32), ALU.subtract).then_inc(u_lo_pool, 1)

            def last_row(i, q, first):
                if not first:
                    pool.wait_ge(quad_done, q - 2)
                pool.tensor_copy(PQ[:, i, 0:1], IDXQ[:, bass.ds(q, 1), 7])
                pool.tensor_copy(PQ[:, i, 1:2], GATET[:, bass.ds(4 * q + 3, 1)]).then_inc(pool_copied, 1)
                pool.wait_ge(pool_copied, q + 1)
                pool.sem_inc(pool_seen, 1)
                pool.tensor_scalar(HOT[i][:, 7, :], iota, PQ[:, i, 0:1], PQ[:, i, 1:2], ALU.is_equal, ALU.mult).then_inc(hot_pool, 1)

            with pool.Fori(0, L) as l:
                pool.memset(RAW[:, :, :, 0:1], 0.0).then_inc(zeros_ready, 1)
                for m in range(8):
                    u_lows(m, 0)
                with pool.Fori(1, POOL_BODIES) as j:
                    for m in range(8):
                        u_lows(m, j)
                pool.wait_ge(u_act, 128)
                pool.wait_ge(sel_out, 3)
                for i in range(3):
                    last_row(i, i, True)
                with pool.Fori(1, 21) as q:
                    for i in range(3):
                        last_row(i, 3 * q + i, False)
                last_row(0, 63, False)
                pool.sem_inc(arrived, 1)
                pool.wait_ge(go, l + 1)


def constants():
    const = np.zeros((P, N_CONST), np.float32)
    const[:, K_ID:K_ID + P] = np.eye(P)
    const[:, K_IOTA:K_IOTA + P] = np.arange(P)
    x = np.zeros((P, N_XCONST), np.float32)
    i = np.arange(P)
    x[:, X_MASK2:X_MASK2 + P] = i[:, None] < i[None, :]
    x[:, X_MASK2 + P:X_MASK2 + 256] = i[:, None] <= i[None, :]
    for n, b in enumerate(LEVELS):
        low = (i[:, None] // (2 * b) == i[None, :] // (2 * b)) & ((i[:, None] // b) % 2 == 1) & ((i[None, :] // b) % 2 == 0)
        x[:, X_LOW + P * n:X_LOW + P * (n + 1)] = low
        x[:, X_UP + P * n:X_UP + P * (n + 1)] = low.T
    x[:, X_ONES:X_ONES + 2] = 1
    x[:, X_BLK:X_BLK + P] = i[:, None] // 64 == i[None, :] // 64
    x[:, X_HEAD:X_HEAD + 2] = i[:, None] // 64 == np.arange(2)[None, :]
    lg = np.log1p(-np.exp(np.linspace(np.log(1 / 32), np.log(1 / 512), RH)))
    for h in range(RH):
        diff = (i[None, :] - i[:, None]).astype(np.float64)
        x[:, X_DM + 256 * h:X_DM + 256 * h + P] = np.where(diff >= 0, np.exp(lg[h] * np.maximum(diff, 0)), 0) * RDK ** -0.5
        x[:, X_DM + 256 * h + P:X_DM + 256 * (h + 1)] = np.exp(lg[h] * (diff + P)) * RDK ** -0.5
    inv = (10000.0 ** (-np.arange(32, dtype=np.float32) / 32)).astype(np.float32)
    ang = np.arange(S, dtype=np.float32)[:, None] * inv[None, :]
    for t in range(NT):
        a = ang[t * P:(t + 1) * P]
        x[:, X_ROPE + 64 * t:X_ROPE + 64 * t + 32] = np.cos(a)
        x[:, X_ROPE + 64 * t + 32:X_ROPE + 64 * (t + 1)] = np.sin(a)
    return const, x


def lay_out(a):
    f = np.float32

    def chunked(w):
        g = w.shape[2] // GC
        return np.ascontiguousarray(w.reshape(L, DC, P, g, GC).transpose(0, 3, 2, 1, 4)).reshape(L, g, P, DC * GC)

    def head_pad(w):
        w = w.reshape(*w.shape[:-1], GH, GDK)
        return np.concatenate([w, np.zeros((*w.shape[:-1], 64 - GDK), f)], -1).reshape(*w.shape[:-2], GH * 64)

    w = a["w_in"]
    r0 = 1024
    g0 = r0 + 1408
    rwkv = w[:, :, r0:g0]
    rw = [rwkv[:, :, 1152:1280], rwkv[:, :, 1280:1408], rwkv[:, :, 384:768], rwkv[:, :, 0:384], rwkv[:, :, 768:1152]]
    gkd = w[:, :, g0 + 768:g0 + 784]
    w_in = chunked(np.concatenate([*rw, gkd, np.zeros((L, D, 112), f), head_pad(w[:, :, g0:g0 + 192]), head_pad(w[:, :, g0 + 192:g0 + 384]),
                                   w[:, :, 0:1024], w[:, :, g0 + 384:g0 + 768], w[:, :, g0 + 784:g0 + 1168]], -1))
    w_out = np.ascontiguousarray(a["w_out"].reshape(L, N_OUT, 2, P, D).transpose(0, 1, 3, 2, 4)).reshape(L, N_OUT, P, 2 * D)
    mu = a["rwkv_mu"]
    mu = np.concatenate([mu[:, 1152:1280], mu[:, 1280:1408], mu[:, 384:768], mu[:, 0:384], mu[:, 768:1152]], -1)

    def column(v):
        return v.reshape(L, -1, P).transpose(0, 2, 1)

    cols = np.concatenate([column(v) for v in (a["norm_mix"], a["norm_ffn"], mu, a["rwkv_w_bias"], a["rwkv_a_bias"], a["rwkv_k_k"],
                                               a["rwkv_k_a"], a["rwkv_r_k"].reshape(L, -1), head_pad(a["gla_gk_bias"]))], -1)
    small = np.zeros((L, P, N_SMALL), f)
    small[:, 0:64, W_WA:W_WA + 384] = a["rwkv_w_up"]
    small[:, 64:128, W_WA:W_WA + 384] = a["rwkv_a_up"]
    small[:, :, W_G:W_G + 384] = a["rwkv_g_up"]
    small[:, 0:16, W_GK:W_GK + 256] = head_pad(a["gla_gk_up"])
    rows = np.concatenate([a["rwkv_ln_w"], a["rwkv_ln_b"], a["gla_norm_w"]], -1)
    keys = np.ascontiguousarray(a["peer_sub_keys"].reshape(L, 16, P, P).transpose(0, 3, 1, 2)).reshape(L, P, 2048)
    u_t = a["peer_u"].reshape(L, P, 64, 2, DC, P).transpose(0, 2, 5, 3, 4, 1)
    v_t = a["peer_v"].reshape(L, P, 64, 2, D).transpose(0, 2, 1, 3, 4)
    const, xconst = constants()
    return {"x_in": a["x"], "w_in": w_in, "w_out": w_out, "cols": cols, "small": small, "rows": rows, "norm_final": a["norm_final"],
            "w_q": chunked(a["peer_w_q"]), "keys": keys, "u_t": u_t.reshape(L, 64, P, 2048), "v_t": v_t.reshape(L, 64, P, 2048),
            "const": const, "xconst": xconst}


def kernel(**inputs):
    import concourse.bacc as _bacc
    from concourse.bass_utils import run_bass_kernel_spmd as _run

    arrays = {k: np.ascontiguousarray(v) for k, v in lay_out({k: np.asarray(v) for k, v in inputs.items()}).items()}
    nc = _bacc.Bacc("TRN2", target_bir_lowering=False, num_devices=1)
    args = {k: nc.dram_tensor(k, v.shape, F32, kind="ExternalInput").ap() for k, v in arrays.items()}
    out = nc.dram_tensor("y_out", (1, S, D), F32, kind="ExternalOutput").ap()
    trunk(nc, *args.values(), out)
    r = _run(nc, [arrays], core_ids=[0])
    return r.results[0]["y_out"]
```

```python
from contextlib import ExitStack

import numpy as np

import concourse.bass as bass
from concourse import mybir

F32 = mybir.dt.float32
F32R = mybir.dt.float32r
U32 = mybir.dt.uint32
I32 = mybir.dt.int32
ALU = mybir.AluOpType
ACT = mybir.ActivationFunctionType
AX = mybir.AxisListType

P = 128
S = 256
NT = S // P
D = 1024
DC = D // P
L = 2
NH = 6
CT = 3
GH, GDK, GDV = 4, 48, 96
RH, RDK = 4, 64
GC = 256
N_IN = 15
N_CH = 8
N_OUT = 4
OUT_CHUNKS = [0, 1, 5, 6, 7, 2, 3, 4]
N_EARLY = 5
PH, TOPK, NKEYS = 8, 16, 128
NEG = -3.0e38
N_BODY, POOL_BODIES, EXP_BODY, GATE_BODY, SEL_BODY = 32, 9, 10, 11, 14
LOG_DECAY_SCALE = -float(np.exp(-0.5))
NORM_EPS, HEAD_EPS, GN_EPS = 1e-6, 1e-5, 64e-5
CAND_ROWS = [TOPK // (i + 1) for i in range(TOPK)]
NC = sum(CAND_ROWS)

C_MIX, C_FFN, C_MU, C_WB, C_AB, C_KK, C_KA, C_RK, C_GB = 0, 8, 16, 27, 30, 33, 36, 39, 42
N_COLS = 44
W_WA, W_G, W_GK = 0, 384, 768
N_SMALL = 1024
K_ID, K_IOTA = 0, 128
N_CONST = 256
LEVELS = [1, 2, 4, 8, 16, 32, 64]
X_MASK2 = 0
X_LOW = 256
X_UP = X_LOW + 128 * 7
X_ONES = X_UP + 128 * 7
X_BLK = X_ONES + 2
X_HEAD = X_BLK + 128
X_DM = X_HEAD + 2
X_ROPE = X_DM + RH * 256
N_XCONST = X_ROPE + NT * 64


def trunk(nc, x_in, w_in, w_out, cols, small, rows, norm_final, w_q, keys, u_t, v_t, const, xconst, out):
    with ExitStack() as ctx:
        def sb(name, shape, dt=F32):
            return ctx.enter_context(nc.sbuf_tensor(name, shape, dt))

        layer_sems = []

        def sem(name, per_layer=True):
            s = ctx.enter_context(nc.semaphore(name))
            if per_layer:
                layer_sems.append(s)
            return s

        X = sb("x_res", [P, NT, D])
        HT = sb("h_t", [P, DC, S])
        HTH = sb("h_t_hi", [P, DC, S], F32R)
        HTL = sb("h_t_lo", [P, DC, S], F32R)
        RING = sb("w_ring", [P, 2, 2048])
        EH = sb("expert_hi", [P, 4, 512], F32R)
        EL = sb("expert_lo", [P, 4, 512], F32R)
        AH = sb("act_hi", [P, 2, S], F32R)
        AL = sb("act_lo", [P, 2, S], F32R)
        KONST = sb("const_sb", [P, N_CONST])
        COLS = sb("cols_sb", [P, N_COLS])
        IDXQ = sb("idx_quads", [P, S // 4, 8])
        GATET = sb("gate_t", [P, S])
        HOTX = sb("hot_extra", [P, 1024])
        STAT = sb("stat", [P, 96])
        PQ = sb("pool_scalars", [P, 3, 2])
        BIGW = 128 * S
        BIG = sb("big", [P, BIGW])
        PS = ctx.enter_context(nc.psum_tensor("ps", [P, 8, 512], F32))

        ident = KONST[:, K_ID:K_ID + 128]
        iota = KONST[:, K_IOTA:K_IOTA + 128]

        used = [0]

        def big(n):
            a = used[0]
            used[0] += n
            assert used[0] <= BIGW, used[0]
            return BIG[:, a:a + n]

        XC = big(N_XCONST)
        HN = big(NT * D).rearrange("p (t d) -> p t d", t=NT)
        SM = big(N_SMALL)
        ROWS = big(1152)
        RAW = big(2 * 2 * 257).rearrange("p (s b n) -> p s b n", s=2, b=2)
        FM = big(12 * S).rearrange("p (b n) -> p b n", b=12)
        SIGA = big(CT * 2 * S).rearrange("p (c k n) -> p c k n", c=CT, k=2)
        decays = used[0]
        CUM = big(CT * NT * 129).rearrange("p (c k n) -> p c k n", c=CT, k=NT)
        E1 = big(CT * NT * 129).rearrange("p (c k n) -> p c k n", c=CT, k=NT)
        E2 = big(CT * S).rearrange("p (c n) -> p c n", c=CT)
        BTOK = BIG[:, decays:decays + 384]
        KTOK = BIG[:, decays + 384:decays + 768]
        XU = BIG[:, decays + 768:decays + 1536].rearrange("p (a n) -> p a n", a=2)
        STATE = BIG[:, decays + 1536:decays + 1728].rearrange("p (c n) -> p c n", c=CT)
        AR = big(CT * NT * 256).rearrange("p (c k m n) -> p c k m n", c=CT, k=NT, m=2)
        BT = big(CT * S).rearrange("p (c n) -> p c n", c=CT)
        KT = big(CT * S).rearrange("p (c n) -> p c n", c=CT)
        KKN = big(CT * S).rearrange("p (c n) -> p c n", c=CT)
        TMP = big(CT * S).rearrange("p (c n) -> p c n", c=CT)
        MASKED = big(12 * 512).rearrange("p (u m n) -> p u m n", u=12, m=4)
        fm_flat = FM.rearrange("p b n -> p (b n)")
        TI = fm_flat[:, 0:1536].rearrange("p (u n) -> p u n", u=12)
        TT = fm_flat[:, 1536:3072].rearrange("p (u n) -> p u n", u=12)
        Y = SIGA.rearrange("p c k n -> p (c k n)").rearrange("p (u n) -> p u n", u=12)
        VTOK = KKN.rearrange("p c n -> p (c n)").rearrange("p (k n) -> p k n", k=NT)
        GG = RAW.rearrange("p s b n -> p (s b n)")[:, 0:780].rearrange("p (k n) -> p k n", k=NT)
        ZRET = big(NT * 1024).rearrange("p (t n) -> p t n", t=NT)
        ZGLA = big(NT * 768).rearrange("p (t n) -> p t n", t=NT)
        GQK = big(4 * S).rearrange("p (b n) -> p b n", b=4)
        GB = big(2 * S).rearrange("p (b n) -> p b n", b=2)
        GX = big(2 * 2 * S).rearrange("p (s b n) -> p s b n", s=2, b=2)
        mflat = MASKED.rearrange("p u m n -> p (u m n)")
        ROT = mflat[:, 0:1024].rearrange("p (t g h c) -> p t g h c", t=NT, g=8, h=2)
        QKT = mflat[:, 1024:2048].rearrange("p (b n) -> p b n", b=4)
        SCR = mflat[:, 2048:3584].rearrange("p (h n) -> p h n", h=RH)
        RTMP = mflat[:, 3584:4096].rearrange("p (t n) -> p t n", t=NT)
        GE = mflat[:, 4096:5120].rearrange("p (s b n) -> p s b n", s=2, b=2)
        GACC = BIG[:, decays:decays + 1536].rearrange("p (t h n) -> p t h n", t=3, h=GH)
        RSQ = HOTX[:, 0:512].rearrange("p (t n) -> p t n", t=NT)
        GSQ = GX.rearrange("p s b n -> p (s b n)")[:, 0:768].rearrange("p (t n) -> p t n", t=NT)
        XB = TT.rearrange("p u n -> p (u n)")[:, 0:768].rearrange("p (k n) -> p k n", k=NT)
        OT = HT
        used[0] = 0
        QT = big(16 * S).rearrange("p (b n) -> p b n", b=16)
        HNF = big(NT * D).rearrange("p (t d) -> p t d", t=NT)
        KEYS = big(16 * P).rearrange("p (b n) -> p b n", b=16)
        used[0] = 4 * (SEL_BODY + 1) * S
        SC = big(NT * 2048).rearrange("p (u n) -> p u n", u=32)
        SC2 = big(2048).rearrange("p (u n) -> p u n", u=16)
        VAL = big(32 * 16).rearrange("p (u n) -> p u n", u=32)
        IDX = big(32 * 16).rearrange("p (u n) -> p u n", u=32)
        IDXF = big(32 * 16).rearrange("p (u n) -> p u n", u=32)
        CAND = big(16 * NC).rearrange("p (u n) -> p u n", u=16)
        CAND2 = big(16 * NC).rearrange("p (u n) -> p u n", u=16)
        CIDX = big(16 * NC).rearrange("p (u n) -> p u n", u=16)
        TOPV, POS, POSF, EIDX, GATE, I1F, I2F = (big(256).rearrange("p (u n) -> p u n", u=16) for _ in range(7))
        EQ = big(2 * 16 * NC).rearrange("p (s k n) -> p s k n", s=2, k=16)
        ACTS = BIG[:, :].rearrange("p (e t) -> p e t", t=S)
        ht_flat = HT[:, :, :].rearrange("p c n -> p (c n)")
        HOT = [v.rearrange("p (m n) -> p m n", m=8) for v in (ht_flat[:, 0:1024], ht_flat[:, 1024:2048], HOTX[:, :])]
        FROW = BIG[:, 0:D]
        YOUT = BIG[:, D:D + NT * D].rearrange("p (t d) -> p t d", t=NT)

        const_landed = sem("const_landed", False)
        go = sem("layer_go", False)
        arrived = sem("layer_arrived")
        dve_step, act_step, pool_step = sem("dve_step"), sem("act_step"), sem("pool_step")
        params_landed, ring0_landed, ring1_landed = sem("params_landed"), sem("ring0_landed"), sem("ring1_landed")
        ring_free, keys_copied = sem("ring_free"), sem("keys_copied")
        sumsq_ready, rms_ready, rstd_ready = sem("sumsq_ready"), sem("rms_ready"), sem("rstd_ready")
        h_ready, h_turned, ht_ready = sem("h_ready"), sem("h_turned"), sem("ht_ready")
        proj_done, proj_out = sem("proj_done"), sem("proj_out")
        mixed = sem("mixed")
        zeros_ready = sem("zeros_ready")
        tanh_ready, lora_done, sig_ready = sem("tanh_ready"), sem("lora_done"), sem("sig_ready")
        cum_ready, exp_ready = sem("cum_ready"), sem("exp_ready")
        kksq_ready, kknorm_done, kkmax_ready, kksqrt_ready = sem("kksq_ready"), sem("kknorm_done"), sem("kkmax_ready"), sem("kksqrt_ready")
        gg_done, gg_out = sem("gg_done"), sem("gg_out")
        rk_ready, ab_ready = sem("rk_ready"), sem("ab_ready")
        vtok_done, vtok_out = sem("vtok_done"), sem("vtok_out")
        unit_done, unit_out = sem("unit_done"), sem("unit_out")
        mrow_done, mrow_out = sem("mrow_done"), sem("mrow_out")
        y_done, y_out, z_done, z_out = sem("y_done"), sem("y_out"), sem("z_done"), sem("z_out")
        bk_done, bk_out = sem("bk_done"), sem("bk_out")
        chunk_x, chunk_x_out, chunk_u, chunk_u_out = sem("chunk_x"), sem("chunk_x_out"), sem("chunk_u"), sem("chunk_u_out")
        chunk_o, chunk_o_out, state_done, state_out = sem("chunk_o"), sem("chunk_o_out"), sem("state_done"), sem("state_out")
        var_ready, sd_ready = sem("var_ready"), sem("sd_ready")
        rot_ready, rot_done, rot_out = sem("rot_ready"), sem("rot_done"), sem("rot_out")
        score_done, score_out, ret_o, ret_o_out = sem("score_done"), sem("score_out"), sem("ret_o"), sem("ret_o_out")
        gk_done, gk_out, gabs_ready, gln_ready = sem("gk_done"), sem("gk_out"), sem("gabs_ready"), sem("gln_ready")
        gd_ready, ge_ready, gx_ready, gs_done, gs_out = sem("gd_ready"), sem("ge_ready"), sem("gx_ready"), sem("gs_done"), sem("gs_out")
        gla_o, gla_o_out = sem("gla_o"), sem("gla_o_out")
        silu_ready, gcum_ready, sq_ready = sem("silu_ready"), sem("gcum_ready"), sem("sq_ready")
        hvar_ready, hsd_ready, hrstd_ready = sem("hvar_ready"), sem("hsd_ready"), sem("hrstd_ready")
        mix_ready, rwkv_ready = sem("mix_ready"), sem("rwkv_ready")
        ot_done, ot_out = sem("ot_done"), sem("ot_out")
        res_done, res_out = sem("res_done"), sem("res_out")
        split_ready = sem("split_ready")
        q_done, q_out, sc_done, sc_out = sem("q_done"), sem("q_out"), sem("sc_done"), sem("sc_out")
        gdiff_ready, gexp_ready, sel_ready, sel_done, sel_out = sem("gdiff_ready"), sem("gexp_ready"), sem("sel_ready"), sem("sel_done"), sem("sel_out")
        uring = [sem("u0_landed"), sem("u1_landed")]
        u_lo_pool = sem("u_lo_pool")
        u_hi, u_lo, u_done, u_act = sem("u_hi"), sem("u_lo"), sem("u_done"), sem("u_act")
        hot_eq, hot_gate, hot_pool, quad_done, quad_out = (sem(n) for n in ("hot_eq", "hot_gate", "hot_pool", "quad_done", "quad_out"))
        pool_copied, pool_seen = sem("pool_copied"), sem("pool_seen")
        vring = [sem("v0_landed"), sem("v1_landed")]
        v_hi, v_lo, a_hi, a_lo, v_done = sem("v_hi"), sem("v_lo"), sem("a_hi"), sem("a_lo"), sem("v_done")
        peer_done, peer_out = sem("peer_done"), sem("peer_out")
        final_row, y_ready, stored = sem("final_row", False), sem("y_ready", False), sem("stored", False)
        final_ss, final_ms, final_rt = sem("final_ss", False), sem("final_ms", False), sem("final_rt", False)
        ring_landed = [ring0_landed, ring1_landed]
        N_RING = N_IN + N_OUT + 1 + PH

        block = ctx.enter_context(nc.Block())

        @block.sync
        def _(sp):
            sp.dma_start(X[:, :, :], x_in.rearrange("a (t p) d -> p (a t) d", p=P)).then_inc(const_landed, 16)
            sp.dma_start(KONST[:, :], const).then_inc(const_landed, 16)
            with sp.Fori(0, L) as l:
                sp.dma_start(COLS[:, :], cols[l]).then_inc(params_landed, 16)
                sp.dma_start(XC, xconst).then_inc(params_landed, 16)
                sp.dma_start(SM, small[l]).then_inc(params_landed, 16)
                sp.dma_start(ROWS, rows[l].partition_broadcast(P)).then_inc(params_landed, 16)
                src = ([w_in[l, g] for g in range(N_IN)] + [w_out[l, g] for g in range(N_OUT)] + [keys[l]]
                       + [w_q[l, g] for g in range(PH)])
                for n in range(N_RING):
                    if n == N_IN + N_OUT + 2:
                        sp.wait_ge(keys_copied, 1)
                    elif n >= 2:
                        sp.wait_ge(ring_free, n - 1 - (n > N_IN + N_OUT + 2))
                    sp.dma_start(RING[:, n % 2, :], src[n]).then_inc(ring_landed[n % 2], 16)
                for i in range(2):
                    sp.wait_ge(ring_free, N_RING - 2 + i)
                    sp.dma_start(RING[:, i, :], u_t[l, i]).then_inc(uring[i], 16)
                with sp.Fori(1, POOL_BODIES + 1) as j:
                    for i in range(2):
                        sp.wait_ge(u_lo_pool, 8 * j + 4 * i - 4)
                        sp.dma_start(RING[:, i, :], u_t[l, 2 * j + i]).then_inc(uring[i], 16)
                with sp.Fori(1, N_BODY - POOL_BODIES) as j:
                    for i in range(2):
                        sp.wait_ge(u_lo, 8 * j + 4 * i - 4)
                        sp.dma_start(RING[:, i, :], u_t[l, 2 * (j + POOL_BODIES) + i]).then_inc(uring[i], 16)
                for i in range(2):
                    sp.wait_ge(u_lo, 8 * (N_BODY - POOL_BODIES) - 4 + 4 * i)
                    sp.dma_start(RING[:, i, :], v_t[l, i]).then_inc(vring[i], 16)
                with sp.Fori(1, 32) as j:
                    for i in range(2):
                        sp.wait_ge(v_lo, 8 * j + 4 * i - 4)
                        sp.dma_start(RING[:, i, :], v_t[l, 2 * j + i]).then_inc(vring[i], 16)
                sp.wait_ge(arrived, 4)
                for s in layer_sems:
                    sp.sem_clear(s)
                sp.sem_inc(go, 1)
            sp.dma_start(FROW, norm_final.partition_broadcast(P)).then_inc(final_row, 16)
            for t in range(NT):
                sp.wait_ge(y_ready, t + 1)
                sp.dma_start(out[0, t * P:(t + 1) * P, :], YOUT[:, t, :]).then_inc(stored, 16)
            sp.wait_ge(stored, 16 * NT)

        @block.tensor
        def _(pe):
            pe.wait_ge(const_landed, 32)

            def turn_h(src, k):
                for t in range(NT):
                    pe.wait_ge(h_ready, NT * k + t + 1)
                    for c in range(DC):
                        mm = pe.transpose(PS[:, 2 * t + c // 4, (c % 4) * P:(c % 4 + 1) * P], src[:, t, c * P:(c + 1) * P], ident)
                        if c % 4 == 3:
                            mm.then_inc(h_turned, 1)

            def group(g):
                pe.wait_ge(ring_landed[g % 2], 16 * (g // 2 + 1))
                if g == 0:
                    pe.wait_ge(ht_ready, 4)
                if g >= 4:
                    pe.wait_ge(proj_out, g - 3)
                w = RING[:, g % 2, :].rearrange("p (c n) -> p c n", c=DC)
                for b in range(2):
                    o = PS[:, g % 4, b * 256:(b + 1) * 256]
                    for c in range(DC):
                        if g < N_CH:
                            mm = pe.matmul(o, w[:, c, b * P:(b + 1) * P], HT[:, c, :], start=c == 0, stop=c == DC - 1)
                        else:
                            mm = pe.matmul(o, HT[:, c, b * P:(b + 1) * P], w[:, c, :], start=c == 0, stop=c == DC - 1)
                mm.then_inc(proj_done, 1)
                pe.wait_ge(proj_done, g + 1)
                pe.sem_inc(ring_free, 1)

            def lora():
                pe.wait_ge(tanh_ready, 1)
                pe.wait_ge(gk_out, 1)
                for c in range(CT):
                    o = slice(c % 2 * 256, c % 2 * 256 + 256)
                    pe.matmul(PS[:, 4 + c // 2, o], SM[0:64, W_WA + c * P:W_WA + (c + 1) * P], FM[0:64, 0, :], start=True, stop=True)
                    pe.matmul(PS[:, 6 + c // 2, o], SM[64:128, W_WA + c * P:W_WA + (c + 1) * P], FM[64:128, 0, :],
                              start=True, stop=True).then_inc(lora_done, 1)

            def gk_up():
                pe.wait_ge(params_landed, 64)
                pe.wait_ge(mixed, 6)
                for b in range(2):
                    mm = pe.matmul(PS[:, 5, b * 256:(b + 1) * 256], SM[0:16, W_GK + b * P:W_GK + (b + 1) * P], FM[0:16, 11, :],
                                   start=True, stop=True)
                mm.then_inc(gk_done, 1)

            def kk_norm():
                pe.wait_ge(kksq_ready, 1)
                pe.wait_ge(sig_ready, 7)
                for c in range(CT):
                    o = PS[:, 7, c * 256:(c + 1) * 256] if c < 2 else PS[:, 4, 0:256]
                    mm = pe.matmul(o, XC[:, X_BLK:X_BLK + P], TMP[:, c, :], start=True, stop=True)
                mm.then_inc(kknorm_done, 1)

            def gate_and_bonus():
                pe.wait_ge(rk_ready, 1)
                pe.wait_ge(sig_ready, 7)
                pe.wait_ge(kkmax_ready, 1)
                for t in range(NT):
                    pe.matmul(PS[:, 6 + t, 0:384], FM[:, 1, t * P:(t + 1) * P], SM[:, W_G:W_G + 384], start=True, stop=True)
                    for c in range(CT):
                        mm = pe.matmul(PS[:, 6 + t, 384 + 2 * c:386 + 2 * c], TMP[:, c, t * P:(t + 1) * P],
                                       XC[:, X_HEAD:X_HEAD + 2], start=True, stop=True)
                    mm.then_inc(gg_done, 1)

            def v_tok():
                pe.wait_ge(kkmax_ready, 1)
                for k in range(NT):
                    for c in range(CT):
                        mm = pe.transpose(PS[:, 4 + k, c * P:(c + 1) * P], FM[:, 8 + c, k * P:(k + 1) * P], ident)
                    mm.then_inc(vtok_done, 1)

            def units():
                pe.wait_ge(ab_ready, 1)
                pe.wait_ge(gs_out, 9)
                for u in range(12):
                    if u == 6:
                        gla_outputs()
                    k, h = divmod(u, NH)
                    c, r = h // 2, slice(64 * (h % 2), 64 * (h % 2) + 64)
                    if u >= 4:
                        pe.wait_ge(unit_out, u - 3)
                    for m, lhs in enumerate((BT, KT)):
                        mm = pe.matmul(PS[:, 4 + u % 4, m * 256:(m + 1) * 256], lhs[r, c, k * P:(k + 1) * P],
                                       AR[r, c, k, :, :], start=True, stop=True)
                    mm.then_inc(unit_done, 1)
                pe.wait_ge(proj_out, N_IN)
                pe.wait_ge(gla_o_out, 2)
                for u in range(12):
                    k, h = divmod(u, NH)
                    c, r = h // 2, slice(64 * (h % 2), 64 * (h % 2) + 64)
                    e = u // 2
                    mm = pe.matmul(PS[:, 2 * (u % 2) + e // 4, (e % 4) * P:(e % 4 + 1) * P], AR[r, c, k, 0, :], BT[r, c, k * P:(k + 1) * P],
                                   start=True, stop=True)
                    if u in (6, 7, 10, 11):
                        mm.then_inc(mrow_done, 1)
                for i, src in enumerate((BT, KT)):
                    pe.wait_ge(unit_out, 12)
                    for c in range(CT):
                        mm = pe.transpose(PS[:, 4 + i, c * P:(c + 1) * P], src[:, c, 0:P], ident)
                    mm.then_inc(bk_done, 1)

            def invert():
                pe.wait_ge(mrow_out, 4 + 3)
                pe.wait_ge(bk_out, 2)
                for n, b in enumerate(LEVELS[1:]):
                    for k in range(NT):
                        if n >= 1:
                            pe.wait_ge(z_out, 2 * n - 1 + k)
                        for h in range(NH):
                            u = k * NH + h
                            mm = pe.matmul(PS[:, 2 * k + h // 4, (h % 4) * P:(h % 4 + 1) * P], MASKED[:, u, 0, :], TI[:, u, :],
                                           start=True, stop=True)
                        mm.then_inc(y_done, 1)
                    for k in range(NT):
                        pe.wait_ge(y_out, 2 * n + k + 1)
                        for h in range(NH):
                            u = k * NH + h
                            first = Y[:, u, :].rearrange("p (q a b) -> p q a b", a=2, b=b)[:, :, 0, :]
                            second = TT[:, u, :].rearrange("p (q a b) -> p q a b", a=2, b=b)[:, :, 1, :]
                            pe.matmul(PS[:, 4 + 2 * k, h * 64:(h + 1) * 64], TT[:, u, :], first, start=True, stop=True)
                            mm = pe.matmul(PS[:, 5 + 2 * k, h * 64:(h + 1) * 64], Y[:, u, :], second, start=True, stop=True)
                        mm.then_inc(z_done, 1)

            def chunks():
                pe.wait_ge(z_out, 2 * 6)
                for k in range(NT):
                    if k:
                        pe.wait_ge(state_out, 1)
                        pe.wait_ge(chunk_o_out, 1)
                    for h in range(NH):
                        c, r = h // 2, slice(64 * (h % 2), 64 * (h % 2) + 64)
                        o, v = PS[:, 4 * (h % 2), c * 64:(c + 1) * 64], VTOK[:, k, h * 64:(h + 1) * 64]
                        mm = pe.matmul(o, MASKED[:, k * NH + h, 2, :], v, start=True, stop=k == 0)
                        if k:
                            mm = pe.matmul(o, AR[r, c, k, 0, :], STATE[r, c, :], start=False, stop=True)
                    mm.then_inc(chunk_x, 1)
                    pe.wait_ge(chunk_x_out, k + 1)
                    for h in range(NH):
                        mm = pe.matmul(PS[:, 1, h * 64:(h + 1) * 64], TT[:, k * NH + h, :], XU[:, 0, h * 64:(h + 1) * 64],
                                       start=True, stop=True)
                    mm.then_inc(chunk_u, 1)
                    pe.wait_ge(chunk_u_out, k + 1)
                    for h in range(NH):
                        c, r = h // 2, slice(64 * (h % 2), 64 * (h % 2) + 64)
                        o = PS[:, 2 + 3 * (h % 2), c * 64:(c + 1) * 64]
                        pe.matmul(o, MASKED[:, k * NH + h, 1, :], XU[:, 1, h * 64:(h + 1) * 64], start=True, stop=False)
                        mm = pe.matmul(o, MASKED[:, k * NH + h, 3, :], VTOK[:, k, h * 64:(h + 1) * 64], start=False, stop=k == 0)
                        if k:
                            mm = pe.matmul(o, AR[r, c, k, 1, :], STATE[r, c, :], start=False, stop=True)
                    mm.then_inc(chunk_o, 1)
                    if k == 0:
                        for h in range(NH):
                            r = slice(64 * (h % 2), 64 * (h % 2) + 64)
                            o, hc = PS[r, 3, (h // 2) * 64:(h // 2 + 1) * 64], slice(h * 64, (h + 1) * 64)
                            pe.matmul(o, BTOK[:, hc], XU[:, 1, hc], start=True, stop=False)
                            mm = pe.matmul(o, KTOK[:, hc], VTOK[:, 0, hc], start=False, stop=True)
                        mm.then_inc(state_done, 1)

            def turn_qk():
                pe.wait_ge(gg_out, 2)
                for t in range(NT):
                    pe.wait_ge(rot_ready, t + 1)
                    for b in range(4):
                        mm = pe.transpose(PS[:, 6 + t, b * P:(b + 1) * P],
                                          ROT[:, t, 2 * b:2 * b + 2, :, :], ident)
                    mm.then_inc(rot_done, 1)

            def scores(b, bank):
                for i in range(2):
                    r = slice(64 * i, 64 * i + 64)
                    pe.matmul(PS[:, bank + i, 0:256], QKT[r, 2 + b, 0:P], QKT[r, b, :], start=True, stop=True)
                    pe.matmul(PS[:, bank + i, 256:384], QKT[r, 2 + b, P:S], QKT[r, b, P:S], start=True, stop=True).then_inc(score_done, 1)

            def retention_outputs():
                pe.wait_ge(score_out, RH)
                pe.wait_ge(proj_out, 11)
                for t in range(NT):
                    for h in range(RH):
                        o = PS[:, 4 + t, h * 64:(h + 1) * 64]
                        v = [ZRET[:, j, 512 + h * 64:512 + (h + 1) * 64] for j in range(NT)]
                        if t == 0:
                            mm = pe.matmul(o, SCR[:, h, 0:P], v[0], start=True, stop=True)
                        else:
                            pe.matmul(o, SCR[:, h, P:256], v[0], start=True, stop=False)
                            mm = pe.matmul(o, SCR[:, h, 256:384], v[1], start=False, stop=True)
                    mm.then_inc(ret_o, 1)

            def level(n, bank):
                if n:
                    pe.wait_ge(gx_ready, n)
                for t in range(NT if n < 8 else 1):
                    for h in range(GH):
                        r, b = slice(64 * (h % 2), 64 * (h % 2) + 64), h // 2
                        if n == 0:
                            lhs, rhs = GQK[r, 2 + b, t * P:(t + 1) * P], GQK[r, b, t * P:(t + 1) * P]
                        elif n < 8:
                            lhs = rhs = GX[r, n % 2, b, t * P:(t + 1) * P]
                        else:
                            lhs, rhs = GX[r, n % 2, b, 0:P], GX[r, n % 2, b, P:S]
                        o = PS[:, bank + h % 2, (2 * t + b) * P:(2 * t + b + 1) * P]
                        mm = pe.matmul(o, lhs, rhs, start=True, stop=True)
                mm.then_inc(gs_done, 1)

            def gla_outputs():
                pe.wait_ge(proj_out, N_IN)
                for t in range(NT):
                    for h in range(GH):
                        o = PS[:, t, h * GDV:(h + 1) * GDV]
                        v = [ZGLA[:, j, h * GDV:(h + 1) * GDV] for j in range(NT)]
                        if t == 0:
                            mm = pe.matmul(o, GACC[:, 0, h, :], v[0], start=True, stop=True)
                        else:
                            pe.matmul(o, GACC[:, 2, h, :], v[0], start=True, stop=False)
                            mm = pe.matmul(o, GACC[:, 1, h, :], v[1], start=False, stop=True)
                    mm.then_inc(gla_o, 1)

            def turn_out(first, last):
                for t in range(NT):
                    for i, c in enumerate(OUT_CHUNKS[first:last]):
                        mm = pe.transpose(PS[:, 2 * t + i // 4, (i % 4) * P:(i % 4 + 1) * P], HN[:, t, c * P:(c + 1) * P], ident)
                    mm.then_inc(ot_done, 1)

            def out_chunk(i):
                g = i // 2
                n = N_IN + g
                pe.wait_ge(ring_landed[n % 2], 16 * (n // 2 + 1))
                w = RING[:, n % 2, :].rearrange("p (c n) -> p c n", c=2)
                for t in range(NT):
                    for f in range(2):
                        mm = pe.matmul(PS[:, 4 + 2 * t + f, :], OT[:, i, t * P:(t + 1) * P], w[:, i % 2, f * 512:(f + 1) * 512],
                                       start=i == 0, stop=i == DC - 1, skip_group_check=True)
                if i % 2:
                    mm.then_inc(res_done, 1)
                    pe.wait_ge(res_done, g + 1)
                    pe.sem_inc(ring_free, 1)

            def project_out():
                pe.wait_ge(chunk_o_out, 2)
                pe.wait_ge(mix_ready, 2)
                turn_out(0, N_EARLY)
                pe.wait_ge(ot_out, 2)
                for i in range(N_EARLY):
                    out_chunk(i)
                pe.wait_ge(rwkv_ready, 1)
                turn_out(N_EARLY, DC)
                pe.wait_ge(ot_out, 4)
                for i in range(N_EARLY, DC):
                    out_chunk(i)

            def queries():
                kn = N_IN + N_OUT
                for g in range(PH):
                    n = kn + 1 + g
                    if g == 0:
                        pe.wait_ge(ht_ready, 8)
                        pe.wait_ge(res_out, 4)
                    pe.wait_ge(ring_landed[n % 2], 16 * (n // 2 + 1))
                    if g >= 4:
                        pe.wait_ge(q_out, g - 3)
                    w = RING[:, n % 2, :].rearrange("p (c n) -> p c n", c=DC)
                    for b in range(2):
                        for c in range(DC):
                            mm = pe.matmul(PS[:, g % 4, b * 256:(b + 1) * 256], w[:, c, b * P:(b + 1) * P], HT[:, c, :],
                                           start=c == 0, stop=c == DC - 1)
                    mm.then_inc(q_done, 1)
                    pe.wait_ge(q_done, g + 1)
                    pe.sem_inc(ring_free, 1)
                for t in range(NT):
                    for m in range(4):
                        if t:
                            pe.wait_ge(sc_out, m + 1)
                        pe.wait_ge(q_out, 2 * m + 2 if t == 0 else PH)
                        for i in range(4):
                            b = 4 * m + i
                            mm = pe.matmul(PS[:, 4 + m, i * P:(i + 1) * P], QT[:, b, t * P:(t + 1) * P], KEYS[:, b, :],
                                           start=True, stop=True)
                        mm.then_inc(sc_done, 1)

            def turn_sel():
                pe.wait_ge(sel_ready, 1)
                for i, src in enumerate((I1F, I2F, GATE)):
                    for t in range(NT):
                        mm = pe.transpose(PS[:, i, t * P:(t + 1) * P], src[:, t * PH:(t + 1) * PH, :], ident)
                    mm.then_inc(sel_done, 1)

            def u_half(m, j, first, pool):
                e, f = m // 2, m % 2
                if pool:
                    pe.wait_ge(u_lo_pool, 8 * j + m + 1)
                else:
                    pe.wait_ge(u_lo, 8 * (j - POOL_BODIES) + m + 1)
                if f == 0:
                    if first and e < 2:
                        if e == 0:
                            pe.wait_ge(split_ready, 2)
                            pe.wait_ge(sc_out, 8)
                    else:
                        pe.wait_ge(u_act, 4 * j + e - 1)
                w_hi = EH[:, m % 4, :].rearrange("p (c n) -> p c n", c=4)
                w_lo = EL[:, m % 4, :].rearrange("p (c n) -> p c n", c=4)
                o = PS[:, 4 + e % 2, 0:S]
                for c in range(4):
                    d = 4 * f + c
                    pe.matmul(o, w_hi[:, c, :], HTH[:, d, :], start=d == 0, stop=False)
                    pe.matmul(o, w_hi[:, c, :], HTL[:, d, :], start=False, stop=False)
                    mm = pe.matmul(o, w_lo[:, c, :], HTH[:, d, :], start=False, stop=d == DC - 1)
                mm.then_inc(u_done, 1)

            def quad(i, q, first):
                pe.wait_ge(hot_gate, q + 1)
                pe.wait_ge(hot_pool, q + 1)
                if not first:
                    pe.wait_ge(quad_out, q - 2)
                for t in range(4):
                    mm = pe.matmul(PS[:, i, t * P:(t + 1) * P], HOT[i][:, 4 + t, :], HOT[i][:, t, :], start=True, stop=True)
                mm.then_inc(quad_done, 1)

            def v_half(m, j, first):
                e, f = m // 2, m % 2
                pe.wait_ge(v_lo, 8 * j + m + 1)
                pe.wait_ge(a_lo, 4 * j + e + 1)
                for t in range(NT):
                    o = PS[:, 2 * t + f, :]
                    a_hi_t, a_lo_t = AH[:, e % 2, t * P:(t + 1) * P], AL[:, e % 2, t * P:(t + 1) * P]
                    start = first and e == 0
                    pe.matmul(o, a_hi_t, EH[:, m % 4, :], start=start, stop=False, skip_group_check=True)
                    pe.matmul(o, a_hi_t, EL[:, m % 4, :], start=False, stop=False, skip_group_check=True)
                    mm = pe.matmul(o, a_lo_t, EH[:, m % 4, :], start=False, stop=True, skip_group_check=True)
                mm.then_inc(v_done, 1)

            with pe.Fori(0, L) as l:
                turn_h(HN, 0)
                for g in range(7):
                    group(g)
                gk_up()
                group(7)
                lora()
                group(8)
                kk_norm()
                group(9)
                gate_and_bonus()
                group(10)
                v_tok()
                turn_qk()
                group(11)
                pe.wait_ge(vtok_out, 2)
                level(0, 4)
                pe.wait_ge(rot_out, 2)
                level(1, 6)
                pe.wait_ge(gs_out, 1)
                scores(0, 4)
                group(12)
                pe.wait_ge(gs_out, 2)
                level(2, 6)
                pe.wait_ge(score_out, 2)
                level(3, 4)
                pe.wait_ge(gs_out, 3)
                scores(1, 6)
                group(13)
                pe.wait_ge(gs_out, 4)
                level(4, 4)
                pe.wait_ge(score_out, 4)
                level(5, 6)
                pe.wait_ge(gs_out, 5)
                retention_outputs()
                pe.wait_ge(gs_out, 6)
                level(6, 6)
                group(14)
                pe.wait_ge(ret_o_out, 1)
                level(7, 4)
                pe.wait_ge(gs_out, 7)
                level(8, 6)
                units()
                invert()
                chunks()
                project_out()
                turn_h(HNF, 1)
                queries()
                for m in range(8):
                    u_half(m, 0, True, True)
                with pe.Fori(1, POOL_BODIES) as j:
                    for m in range(8):
                        u_half(m, j, False, True)
                with pe.Fori(POOL_BODIES, SEL_BODY) as j:
                    for m in range(8):
                        u_half(m, j, False, False)
                turn_sel()
                with pe.Fori(SEL_BODY, N_BODY) as j:
                    for m in range(8):
                        u_half(m, j, False, False)
                pe.wait_ge(sel_out, 3)
                for i in range(3):
                    quad(i, i, True)
                with pe.Fori(1, 21) as q:
                    for i in range(3):
                        quad(i, 3 * q + i, False)
                quad(0, 63, False)
                for m in range(8):
                    v_half(m, 0, True)
                with pe.Fori(1, 32) as j:
                    for m in range(8):
                        v_half(m, j, False)
                pe.sem_inc(peer_done, 1)
                pe.wait_ge(v_done, 256)
                pe.sem_inc(arrived, 1)
                pe.wait_ge(go, l + 1)

        @block.scalar
        def _(act):
            act.wait_ge(const_landed, 32)
            steps = [0]

            def link(ins):
                steps[0] += 1
                ins.then_inc(act_step, 1)
                act.wait_ge(act_step, steps[0])

            def sumsq(k, dst):
                for t in range(NT):
                    act.activation(dst[:, t, :], X[:, t, :], ACT.Square, accum_out=STAT[:, 4 * k + t:4 * k + t + 1]).then_inc(sumsq_ready, 1)

            def root(k):
                act.wait_ge(rms_ready, k + 1)
                act.activation(STAT[:, 4 * k + 2:4 * k + 4], STAT[:, 4 * k:4 * k + 2], ACT.Sqrt).then_inc(rstd_ready, 1)

            def evac_h(col, k):
                for c in range(DC):
                    if c % 4 == 0:
                        act.wait_ge(h_turned, 4 * k + c // 4 + 1)
                    ins = act.activation(HT[:, c, 0:P], PS[:, c // 4, (c % 4) * P:(c % 4 + 1) * P], ACT.Identity, scale=COLS[:, col + c:col + c + 1])
                    if c % 4 == 3:
                        ins.then_inc(ht_ready, 1)

            def evac_group(g):
                act.wait_ge(proj_done, g + 1)
                ps = PS[:, g % 4, :].rearrange("p (b n) -> p b n", b=2)
                if g < 6:
                    if g == 0:
                        act.wait_ge(zeros_ready, 1)
                    if g >= 2:
                        act.wait_ge(mixed, g - 1)
                    ins = act.copy(RAW[:, g % 2, :, 1:257], ps)
                elif g == 6:
                    ins = act.mul(GQK[:, 0:2, :], ps, float(GDK) ** -0.5)
                elif g == 7:
                    ins = act.copy(GQK[:, 2:4, :], ps)
                elif g < 12:
                    ins = act.copy(ZRET[:, :, (g - 8) * 256:(g - 7) * 256], ps)
                else:
                    ins = act.copy(ZGLA[:, :, (g - 12) * 256:(g - 11) * 256], ps)
                ins.then_inc(proj_out, 1)

            def keys_out():
                n = N_IN + N_OUT
                act.wait_ge(ring_landed[n % 2], 16 * (n // 2 + 1))
                link(act.copy(KEYS, RING[:, n % 2, :].rearrange("p (b n) -> p b n", b=16)))
                act.sem_inc(keys_copied, 1)

            def u_split(m, j, first):
                if m % 4 == 0:
                    act.wait_ge(uring[m // 4], 16 * (j + 1))
                if first and m < 4:
                    if m == 0:
                        act.wait_ge(split_ready, 2)
                else:
                    act.wait_ge(u_done, 8 * j + m - 3)
                act.copy(EH[:, m % 4, :], RING[:, m // 4, (m % 4) * 512:(m % 4 + 1) * 512]).then_inc(u_hi, 1)

            def u_gelu(e, j):
                act.wait_ge(u_done, 8 * j + 2 * e + 2)
                act.activation(ACTS[:, 4 * j + e, :], PS[:, 4 + e % 2, 0:S], ACT.Gelu).then_inc(u_act, 1)

            def u_body(j, first):
                for m in range(8):
                    u_split(m, j, first)
                    if m == 1 and not first:
                        u_gelu(-1, j)
                    if m >= 3 and m % 2:
                        u_gelu(m // 2 - 1, j)

            def gate_rows(i, q):
                act.wait_ge(hot_eq, q + 1)
                for t in range(3):
                    ins = act.activation(HOT[i][:, 4 + t, :], HOT[i][:, 4 + t, :], ACT.Identity, scale=GATET[:, bass.ds(4 * q + t, 1)])
                ins.then_inc(hot_gate, 1)

            def v_split(m, j, first):
                if m % 4 == 0:
                    act.wait_ge(vring[m // 4], 16 * (j + 1))
                if first and m < 4:
                    if m == 0:
                        act.wait_ge(u_done, 256)
                else:
                    act.wait_ge(v_done, 8 * j + m - 3)
                act.copy(EH[:, m % 4, :], RING[:, m // 4, (m % 4) * 512:(m % 4 + 1) * 512]).then_inc(v_hi, 1)

            def a_split(e, j, first):
                if first and e < 2:
                    if e == 0:
                        act.wait_ge(quad_out, 64)
                else:
                    act.wait_ge(v_done, 8 * j + 2 * e - 2)
                act.copy(AH[:, e % 2, :], ACTS[:, 4 * j + e, :]).then_inc(a_hi, 1)

            with act.Fori(0, L) as l:
                steps[0] = 0
                act.wait_ge(params_landed, 64)
                sumsq(0, HN)
                root(0)
                evac_h(C_MIX, 0)
                for g in range(7):
                    evac_group(g)
                act.wait_ge(mixed, 6)
                act.activation(FM[0:64, 0, :], FM[0:64, 0, :], ACT.Tanh).then_inc(tanh_ready, 1)
                act.activation(FM[:, 1, :], FM[:, 1, :], ACT.Sigmoid).then_inc(sig_ready, 1)
                act.wait_ge(gk_out, 1)
                link(act.activation(GE[:, 0, :, :], GB[:, :, :], ACT.Abs))
                link(act.activation(GE[:, 0, :, :], GE[:, 0, :, :], ACT.Exp, scale=-1.0))
                act.activation(GE[:, 0, :, :], GE[:, 0, :, :], ACT.Ln, bias=1.0).then_inc(gln_ready, 1)
                evac_group(7)
                for c in range(CT):
                    act.wait_ge(lora_done, CT)
                    o = slice(c % 2 * 256, c % 2 * 256 + 256)
                    act.activation(SIGA[:, c, 0, :], PS[:, 4 + c // 2, o], ACT.Sigmoid, bias=COLS[:, C_WB + c:C_WB + c + 1]).then_inc(sig_ready, 1)
                    act.activation(SIGA[:, c, 1, :], PS[:, 6 + c // 2, o], ACT.Sigmoid, bias=COLS[:, C_AB + c:C_AB + c + 1]).then_inc(sig_ready, 1)
                evac_group(8)
                act.wait_ge(cum_ready, 1)
                for c in range(CT):
                    for k in range(NT):
                        n = 16 + 2 * (c * NT + k)
                        act.activation(E1[:, c, k, :], CUM[:, c, k, :], ACT.Exp, bias=STAT[:, n:n + 1])
                        act.activation(E2[:, c, k * P:(k + 1) * P], CUM[:, c, k, 1:129], ACT.Exp, scale=-1.0, bias=STAT[:, n + 1:n + 2])
                act.activation(STAT[:, 28:31], CUM[:, :, 1, 64], ACT.Exp).then_inc(exp_ready, 1)
                act.wait_ge(kkmax_ready, 1)
                act.activation(KKN[:, :, :], KKN[:, :, :], ACT.Sqrt).then_inc(kksqrt_ready, 1)
                evac_group(9)
                evac_group(10)
                for i in range(NT):
                    act.wait_ge(gg_done, i + 1)
                    act.copy(GG[:, i, :], PS[:, 6 + i, 0:390]).then_inc(gg_out, 1)
                act.wait_ge(ab_ready, 1)
                for i in range(NT):
                    act.wait_ge(vtok_done, i + 1)
                    act.copy(VTOK[:, i, :], PS[:, 4 + i, 0:384]).then_inc(vtok_out, 1)
                for t in range(NT):
                    act.wait_ge(rot_done, t + 1)
                    act.copy(QKT[:, :, t * P:(t + 1) * P], PS[:, 6 + t, :].rearrange("p (b n) -> p b n", b=4)).then_inc(rot_out, 1)

                def level_exp(n):
                    act.wait_ge(gd_ready, n)
                    act.activation(GE[:, n % 2, :, :], GE[:, n % 2, :, :], ACT.Exp).then_inc(ge_ready, 1)

                level_exp(1)
                level_exp(2)
                evac_group(11)
                level_exp(3)
                evac_group(12)
                level_exp(4)
                level_exp(5)
                evac_group(13)
                act.wait_ge(ret_o, 2)
                act.copy(HN[:, :, 0:256], PS[:, 4:6, 0:256]).then_inc(ret_o_out, 1)
                level_exp(6)
                level_exp(7)
                evac_group(14)
                level_exp(8)
                for t in range(NT):
                    act.wait_ge(gla_o, t + 1)
                    act.copy(HN[:, t, 640:1024], PS[:, t, 0:384]).then_inc(gla_o_out, 1)
                for i in range(2):
                    act.wait_ge(bk_done, i + 1)
                    act.copy((BTOK, KTOK)[i], PS[:, 4 + i, 0:384]).then_inc(bk_out, 1)
                act.wait_ge(ret_o_out, 1)
                act.wait_ge(gla_o_out, 2)
                for t in range(NT):
                    for h in range(RH):
                        act.activation(RSQ[:, t, h * 64:(h + 1) * 64], HN[:, t, h * 64:(h + 1) * 64], ACT.Square, accum_out=STAT[:, 64 + 4 * t + h:65 + 4 * t + h])
                    for h in range(GH):
                        o = 640 + h * GDV
                        ins = act.activation(GSQ[:, t, o - 640:o - 640 + GDV], HN[:, t, o:o + GDV], ACT.Square, accum_out=STAT[:, 72 + 4 * t + h:73 + 4 * t + h])
                ins.then_inc(sq_ready, 1)
                act.wait_ge(proj_out, N_IN)
                act.activation(ZRET[:, :, 768:1024], ZRET[:, :, 768:1024], ACT.Silu).then_inc(silu_ready, 1)
                act.activation(ZGLA[:, :, 384:768], ZGLA[:, :, 384:768], ACT.Silu).then_inc(silu_ready, 1)
                act.wait_ge(hvar_ready, 1)
                act.activation(STAT[:, 80:96], STAT[:, 64:80], ACT.Sqrt).then_inc(hsd_ready, 1)
                act.wait_ge(var_ready, 1)
                act.activation(STAT[:, 44:56], STAT[:, 32:44], ACT.Sqrt).then_inc(sd_ready, 1)
                for t in range(NT):
                    act.wait_ge(ot_done, t + 1)
                    act.copy(OT[:, 0:4, t * P:(t + 1) * P], PS[:, 2 * t, :].rearrange("p (c n) -> p c n", c=4))
                    act.copy(OT[:, 4, t * P:(t + 1) * P], PS[:, 2 * t + 1, 0:P]).then_inc(ot_out, 1)
                for t in range(NT):
                    act.wait_ge(ot_done, NT + t + 1)
                    act.copy(OT[:, N_EARLY:DC, t * P:(t + 1) * P], PS[:, 2 * t, 0:384].rearrange("p (c n) -> p c n", c=3)).then_inc(ot_out, 1)
                act.wait_ge(res_out, 4)
                sumsq(1, HNF)
                root(1)
                keys_out()
                evac_h(C_FFN, 1)
                act.wait_ge(ht_ready, 8)
                act.copy(HTH[:, :, :], HT[:, :, :]).then_inc(split_ready, 1)
                for g in range(PH):
                    act.wait_ge(q_done, g + 1)
                    act.copy(QT[:, 2 * g:2 * g + 2, :], PS[:, g % 4, :].rearrange("p (b n) -> p b n", b=2)).then_inc(q_out, 1)
                for t in range(NT):
                    for m in range(4):
                        act.wait_ge(sc_done, 4 * t + m + 1)
                        act.copy(SC[:, 16 * t + 4 * m:16 * t + 4 * m + 4, :], PS[:, 4 + m, :].rearrange("p (b n) -> p b n", b=4)).then_inc(sc_out, 1)
                u_body(0, True)
                with act.Fori(1, EXP_BODY) as j:
                    u_body(j, False)
                act.wait_ge(gdiff_ready, 1)
                act.activation(GATE[:, :, :], GATE[:, :, :], ACT.Exp).then_inc(gexp_ready, 1)
                with act.Fori(EXP_BODY, SEL_BODY) as j:
                    u_body(j, False)
                pair = IDXQ[:, :, :].rearrange("p q (m t) -> p m q t", m=2)
                for i in range(3):
                    act.wait_ge(sel_done, i + 1)
                    src = PS[:, i, 0:S]
                    if i < 2:
                        act.copy(pair[:, 1 - i], src.rearrange("p (q t) -> p q t", t=4)).then_inc(sel_out, 1)
                    else:
                        act.copy(GATET[:, :], src).then_inc(sel_out, 1)
                with act.Fori(SEL_BODY, N_BODY) as j:
                    u_body(j, False)
                u_gelu(-1, N_BODY)
                for i in range(3):
                    gate_rows(i, i)
                with act.Fori(1, 21) as q:
                    for i in range(3):
                        gate_rows(i, 3 * q + i)
                gate_rows(0, 63)
                act.wait_ge(quad_out, 64)
                for m in range(8):
                    if m % 2 == 0:
                        a_split(m // 2, 0, True)
                    v_split(m, 0, True)
                with act.Fori(1, 32) as j:
                    for m in range(8):
                        if m % 2 == 0:
                            a_split(m // 2, j, False)
                        v_split(m, j, False)
                act.wait_ge(v_hi, 256)
                act.sem_inc(arrived, 1)
                act.wait_ge(go, l + 1)
            for t in range(NT):
                act.activation(YOUT[:, t, :], X[:, t, :], ACT.Square, accum_out=STAT[:, t:t + 1]).then_inc(final_ss, 1)
            act.wait_ge(final_ms, 1)
            act.activation(STAT[:, 2:4], STAT[:, 0:2], ACT.Sqrt).then_inc(final_rt, 1)

        @block.vector
        def _(dve):
            dve.wait_ge(const_landed, 32)
            steps = [0]

            def link(ins):
                steps[0] += 1
                ins.then_inc(dve_step, 1)
                dve.wait_ge(dve_step, steps[0])

            def norm_rows(k, dst):
                dve.wait_ge(sumsq_ready, NT * (k + 1))
                a = 4 * k
                link(dve.tensor_scalar(STAT[:, a:a + 2], STAT[:, a:a + 2], 1.0 / D, NORM_EPS, ALU.mult, ALU.add))
                dve.sem_inc(rms_ready, 1)
                dve.wait_ge(rstd_ready, k + 1)
                link(dve.reciprocal(STAT[:, a:a + 2], STAT[:, a + 2:a + 4]))
                for t in range(NT):
                    dve.tensor_scalar(dst[:, t, :], X[:, t, :], STAT[:, a + t:a + t + 1], None, ALU.mult).then_inc(h_ready, 1)

            def evac_h(col, k):
                for c in range(DC):
                    if c % 4 == 0:
                        dve.wait_ge(h_turned, 4 * k + 3 + c // 4)
                    ins = dve.tensor_scalar(HT[:, c, P:S], PS[:, 2 + c // 4, (c % 4) * P:(c % 4 + 1) * P], COLS[:, col + c:col + c + 1], None, ALU.mult)
                    if c % 4 == 3:
                        ins.then_inc(ht_ready, 1)

            def mix(g):
                dve.wait_ge(proj_out, g + 1)
                r = RAW[:, g % 2, :, :]
                link(dve.tensor_tensor(TMP[:, 0:2, :], r[:, :, 0:256], r[:, :, 1:257], ALU.subtract))
                for b in range(2):
                    n = 2 * g + b
                    if n < 11:
                        ins = dve.scalar_tensor_tensor(FM[:, n, :], TMP[:, b, :], COLS[:, C_MU + n:C_MU + n + 1], r[:, b, 1:257], ALU.mult, ALU.add)
                    else:
                        ins = dve.tensor_copy(FM[:, n, :], r[:, b, 1:257])
                    link(ins)
                dve.sem_inc(mixed, 1)

            def col(n, c):
                return COLS[:, n + c:n + c + 1]

            def rwkv_prep():
                K, R = FM[:, 2:5, :], FM[:, 5:8, :]
                for c in range(CT):
                    ins = dve.tensor_scalar(BT[:, c, :], K[:, c, :], col(C_KK, c), None, ALU.mult)
                link(ins)
                dve.tensor_tensor(TMP[:, :, :], BT[:, :, :], BT[:, :, :], ALU.mult).then_inc(kksq_ready, 1)
                gla_gates()
                dve.wait_ge(sig_ready, 7)
                link(dve.tensor_scalar(E2[:, :, :], SIGA[:, :, 0, :], LOG_DECAY_SCALE, None, ALU.mult))
                dve.memset(CUM[:, :, :, 0:1], 0.0)
                for c in range(CT):
                    for k in range(NT):
                        ins = dve.tensor_tensor_scan(CUM[:, c, k, 1:129], XC[:, X_ONES:X_ONES + 1].broadcast_to([P, P]), E2[:, c, k * P:(k + 1) * P], 0.0, ALU.mult, ALU.add)
                link(ins)
                for c in range(CT):
                    for k in range(NT):
                        n = 16 + 2 * (c * NT + k)
                        dve.tensor_scalar(STAT[:, n:n + 1], CUM[:, c, k, 64:65], -1.0, None, ALU.mult)
                        ins = dve.tensor_copy(STAT[:, n + 1:n + 2], CUM[:, c, k, 64:65])
                link(ins)
                dve.sem_inc(cum_ready, 1)
                for c in range(CT):
                    ins = dve.tensor_scalar(KT[:, c, :], SIGA[:, c, 1, :], 1.0, col(C_KA, c), ALU.subtract, ALU.mult)
                link(ins)
                link(dve.scalar_tensor_tensor(KT[:, :, :], KT[:, :, :], 1.0, K, ALU.add, ALU.mult))
                dve.wait_ge(kknorm_done, 1)
                dve.tensor_scalar(KKN[:, 0:2, :], PS[:, 7, :].rearrange("p (c n) -> p c n", c=2), 1e-24, None, ALU.max)
                link(dve.tensor_scalar(KKN[:, 2, :], PS[:, 4, 0:256], 1e-24, None, ALU.max))
                dve.sem_inc(kkmax_ready, 1)
                for c in range(CT):
                    ins = dve.scalar_tensor_tensor(TMP[:, c, :], R[:, c, :], col(C_RK, c), KT[:, c, :], ALU.mult, ALU.mult)
                link(ins)
                dve.sem_inc(rk_ready, 1)
                dve.wait_ge(kksqrt_ready, 1)
                link(dve.reciprocal(KKN[:, :, :], KKN[:, :, :]))
                link(dve.tensor_tensor(KKN[:, :, :], KKN[:, :, :], BT[:, :, :], ALU.mult))
                dve.wait_ge(exp_ready, 1)
                for c in range(CT):
                    for k in range(NT):
                        s = slice(k * P, (k + 1) * P)
                        dve.scalar_tensor_tensor(AR[:, c, k, 0, :], KKN[:, c, s], -1.0, E1[:, c, k, 0:128], ALU.mult, ALU.mult)
                        dve.tensor_tensor(AR[:, c, k, 1, :], R[:, c, s], E1[:, c, k, 1:129], ALU.mult)
                link(dve.tensor_tensor(BT[:, :, :], KKN[:, :, :], SIGA[:, :, 1, :], ALU.mult))
                dve.tensor_tensor(BT[:, :, :], BT[:, :, :], E2[:, :, :], ALU.mult)
                link(dve.tensor_tensor(KT[:, :, :], KT[:, :, :], E2[:, :, :], ALU.mult))
                link(dve.tensor_tensor(STAT[:, 28:31], STAT[:, 28:31], E1[:, :, 0, 128], ALU.mult))
                dve.sem_inc(ab_ready, 1)

            def gla_gates():
                dve.wait_ge(gk_done, 1)
                for b in range(2):
                    ins = dve.tensor_scalar(GB[:, b, :], PS[:, 5, b * 256:(b + 1) * 256], col(C_GB, b), None, ALU.add)
                link(ins)
                dve.sem_inc(gk_out, 1)
                dve.wait_ge(gln_ready, 1)
                link(dve.scalar_tensor_tensor(GX[:, 0, :, :], GB[:, :, :], 0.0, GE[:, 0, :, :], ALU.min, ALU.subtract))
                link(dve.tensor_scalar(GX[:, 0, :, :], GX[:, 0, :, :], 1.0 / 16.0, None, ALU.mult))
                for b in range(2):
                    ins = dve.tensor_tensor_scan(GB[:, b, :], XC[:, X_ONES:X_ONES + 1].broadcast_to([P, S]), GX[:, 0, b, :], 0.0, ALU.mult, ALU.add)
                ins.then_inc(gcum_ready, 1)

            def rwkv_units():
                mask2 = XC[:, X_MASK2:X_MASK2 + 256].unsqueeze(1).broadcast_to([P, 2, 256])
                for u in range(12):
                    dve.wait_ge(unit_done, u + 1)
                    dve.tensor_tensor(MASKED[:, u, :, :].rearrange("p (a b) n -> p a (b n)", a=2), PS[:, 4 + u % 4, :].rearrange("p (a n) -> p a n", a=2), mask2,
                                      ALU.mult).then_inc(unit_out, 1)
                low1 = XC[:, X_LOW:X_LOW + P].unsqueeze(1).broadcast_to([P, 4, P])
                up1 = XC[:, X_UP:X_UP + P].unsqueeze(1).broadcast_to([P, 12, P])
                id12 = ident.unsqueeze(1).broadcast_to([P, 12, P])
                ti_pairs = TI.rearrange("p (e r) n -> p r e n", r=2)
                for m in range(4):
                    n, e0, r = (4, 0, m) if m < 2 else (2, 4, m - 2)
                    dve.wait_ge(mrow_done, m + 1)
                    dve.tensor_tensor(ti_pairs[:, r, e0:e0 + n, :], PS[:, 2 * r + e0 // 4, 0:n * P].rearrange("p (u n) -> p u n", u=n), low1[:, 0:n, :],
                                      ALU.mult).then_inc(mrow_out, 1)
                dve.wait_ge(unit_out, 12)
                dve.wait_ge(mrow_out, 4)
                dve.tensor_tensor(TI[:, :, :], TI[:, :, :], id12, ALU.add).then_inc(mrow_out, 1)
                dve.tensor_tensor(TT[:, :, :], MASKED[:, :, 0, :], up1, ALU.mult).then_inc(mrow_out, 1)
                dve.wait_ge(mrow_out, 6)
                dve.tensor_tensor(TT[:, :, :], TT[:, :, :], id12, ALU.add).then_inc(mrow_out, 1)
                for n, b in enumerate(LEVELS[1:]):
                    if n == 3:
                        dve.wait_ge(sq_ready, 1)
                        dve.tensor_scalar(STAT[:, 64:72], STAT[:, 64:72], 1.0 / RDK, HEAD_EPS, ALU.mult, ALU.add)
                        dve.tensor_scalar(STAT[:, 72:80], STAT[:, 72:80], 1.0 / GDV, HEAD_EPS, ALU.mult, ALU.add).then_inc(hvar_ready, 1)
                    if n == 4:
                        dve.wait_ge(hsd_ready, 1)
                        dve.reciprocal(STAT[:, 80:96], STAT[:, 80:96]).then_inc(hrstd_ready, 1)
                    low = XC[:, X_LOW + P * (n + 1):X_LOW + P * (n + 2)]
                    for k in range(NT):
                        dve.wait_ge(y_done, 2 * n + k + 1)
                        u0 = k * NH
                        dve.tensor_tensor(Y[:, u0:u0 + NH, :], PS[:, 2 * k:2 * k + 2, :].rearrange("p a n -> p (a n)")[:, 0:768].rearrange("p (u n) -> p u n", u=NH),
                                          low.unsqueeze(1).broadcast_to([P, NH, P]), ALU.mult).then_inc(y_out, 1)
                    for k in range(NT):
                        dve.wait_ge(z_done, 2 * n + k + 1)
                        u0 = k * NH
                        for i, dst in enumerate((TI, TT)):
                            z = PS[:, 4 + 2 * k + i, 0:384]
                            if b < 64:
                                half = dst[:, u0:u0 + NH, :].rearrange("p u (q a b) -> p (u q) a b", a=2, b=b)[:, :, i, :]
                                zz = z.rearrange("p (m b) -> p m b", b=b)
                            else:
                                half = dst[:, u0:u0 + NH, 64 * i:64 * i + 64]
                                zz = z.rearrange("p (m b) -> p m b", b=64)
                            ins = dve.tensor_tensor(half, half, zz, ALU.add)
                        ins.then_inc(z_out, 1)

            def rwkv_chunks():
                for k in range(NT):
                    dve.wait_ge(chunk_x, k + 1)
                    for r in range(2):
                        ins = dve.tensor_copy(XU[:, 0, :].rearrange("p (c r n) -> p r c n", c=CT, r=2)[:, r], PS[:, 4 * r, 0:192].rearrange("p (c n) -> p c n", c=CT))
                    ins.then_inc(chunk_x_out, 1)
                    dve.wait_ge(chunk_u, k + 1)
                    dve.tensor_copy(XU[:, 1, :], PS[:, 1, 0:384]).then_inc(chunk_u_out, 1)
                    if k == 0:
                        dve.wait_ge(state_done, 1)
                        dve.tensor_tensor(STATE[:, :, :], PS[:, 3, 0:192].rearrange("p (c n) -> p c n", c=CT),
                                          STAT[:, 28:31].unsqueeze(2).broadcast_to([P, CT, 64]), ALU.mult).then_inc(state_out, 1)
                    dve.wait_ge(chunk_o, k + 1)
                    for r in range(2):
                        ins = dve.tensor_copy(HN[:, k, 256:640].rearrange("p (c r n) -> p r c n", c=CT, r=2)[:, r], PS[:, 2 + 3 * r, 0:192].rearrange("p (c n) -> p c n", c=CT))
                    ins.then_inc(chunk_o_out, 1)

            def rwkv_out():
                dve.wait_ge(chunk_o_out, 2)
                O = HN[:, :, 256:640]
                for t in range(NT):
                    ins = dve.tensor_reduce(STAT[:, 32 + 6 * t:38 + 6 * t], O[:, t, :].rearrange("p (h n) -> p h n", h=NH), AX.X, ALU.add)
                link(ins)
                link(dve.tensor_scalar(STAT[:, 32:44], STAT[:, 32:44], 1.0 / 64, None, ALU.mult))
                for t in range(NT):
                    o = O[:, t, :].rearrange("p (h n) -> p h n", h=NH)
                    ins = dve.tensor_tensor(o, o, STAT[:, 32 + 6 * t:38 + 6 * t].unsqueeze(2).broadcast_to([P, NH, 64]), ALU.subtract)
                link(ins)
                link(dve.tensor_tensor(XB[:, :, :], O, O, ALU.mult))
                link(dve.tensor_reduce(STAT[:, 32:44], XB[:, :, :].rearrange("p t (h n) -> p (t h) n", h=NH), AX.X, ALU.add))
                link(dve.tensor_scalar(STAT[:, 32:44], STAT[:, 32:44], 1.0 / 64, GN_EPS, ALU.mult, ALU.add))
                dve.sem_inc(var_ready, 1)
                dve.wait_ge(sd_ready, 1)
                link(dve.reciprocal(STAT[:, 44:56], STAT[:, 44:56]))
                for t in range(NT):
                    o = O[:, t, :].rearrange("p (h n) -> p h n", h=NH)
                    link(dve.tensor_tensor(o, o, STAT[:, 44 + 6 * t:50 + 6 * t].unsqueeze(2).broadcast_to([P, NH, 64]), ALU.mult))
                    link(dve.tensor_tensor(O[:, t, :], O[:, t, :], ROWS[:, 0:384], ALU.mult))
                    link(dve.tensor_tensor(O[:, t, :], O[:, t, :], ROWS[:, 384:768], ALU.add))
                    link(dve.tensor_tensor(XB[:, t, :].rearrange("p (h n) -> p h n", h=NH), VTOK[:, t, :].rearrange("p (h n) -> p h n", h=NH),
                                           GG[:, t, 384:390].unsqueeze(2).broadcast_to([P, NH, 64]), ALU.mult))
                    link(dve.tensor_tensor(O[:, t, :], O[:, t, :], XB[:, t, :], ALU.add))
                    link(dve.tensor_tensor(O[:, t, :], O[:, t, :], GG[:, t, 0:384], ALU.mult))

            def rotate():
                dve.wait_ge(proj_out, 10)
                for t in range(NT):
                    z = ZRET[:, t, 0:512].rearrange("p (g h c) -> p g h c", g=8, h=2)
                    rope = XC[:, X_ROPE + 64 * t:X_ROPE + 64 * (t + 1)].rearrange("p (a c) -> p a c", a=2)
                    cos, sin = (rope[:, a, :].unsqueeze(1).broadcast_to([P, 8, 32]) for a in range(2))
                    tmp = RTMP[:, t, :].rearrange("p (g c) -> p g c", g=8)
                    dve.tensor_tensor(ROT[:, t, :, 0, :], z[:, :, 0, :], cos, ALU.mult)
                    link(dve.tensor_tensor(tmp, z[:, :, 1, :], sin, ALU.mult))
                    link(dve.tensor_tensor(ROT[:, t, :, 0, :], ROT[:, t, :, 0, :], tmp, ALU.subtract))
                    dve.tensor_tensor(ROT[:, t, :, 1, :], z[:, :, 0, :], sin, ALU.mult)
                    link(dve.tensor_tensor(tmp, z[:, :, 1, :], cos, ALU.mult))
                    link(dve.tensor_tensor(ROT[:, t, :, 1, :], ROT[:, t, :, 1, :], tmp, ALU.add))
                    dve.sem_inc(rot_ready, 1)

            def decayed(b, bank):
                for i in range(2):
                    h = 2 * b + i
                    dm = XC[:, X_DM + 256 * h:X_DM + 256 * (h + 1)]
                    dve.wait_ge(score_done, h + 1)
                    dve.tensor_tensor(SCR[:, h, 0:256], PS[:, bank + i, 0:256], dm, ALU.mult)
                    dve.tensor_tensor(SCR[:, h, 256:384], PS[:, bank + i, 256:384], dm[:, 0:P], ALU.mult).then_inc(score_out, 1)

            gacc = GACC.rearrange("p t (c r) n -> p t r c n", r=2)
            masks = [ident] + [XC[:, X_UP + P * n:X_UP + P * (n + 1)] for n in range(7)]

            def level(n, bank):
                dve.wait_ge(gs_done, n + 1)
                if 1 <= n < 8:
                    dve.wait_ge(gs_out, n)
                for r in range(2):
                    if n < 8:
                        mask = masks[n].bitcast(U32).unsqueeze(1).unsqueeze(1).broadcast_to([P, NT, 2, P])
                        ins = dve.copy_predicated(gacc[:, 0:2, r], mask, PS[:, bank + r, :].rearrange("p (t c n) -> p t c n", t=NT, c=2))
                    else:
                        ins = dve.tensor_copy(gacc[:, 2, r], PS[:, bank + r, 0:256].rearrange("p (c n) -> p c n", c=2))
                ins.then_inc(gs_out, 1)

            def topk():
                for t in range(NT):
                    dve.wait_ge(sc_out, 4 * t + 4)
                    us = range(16 * t, 16 * t + 16)
                    for u in us:
                        ins = dve.max(VAL[:, u, 0:8], SC[:, u, :])
                    link(ins)
                    for u in us:
                        dve.max_index(IDX[:, u, 0:8].bitcast(U32), VAL[:, u, 0:8], SC[:, u, :])
                        ins = dve.match_replace(SC2[:, u % 16, :], VAL[:, u, 0:8], SC[:, u, :], NEG)
                    link(ins)
                    for u in us:
                        ins = dve.max(VAL[:, u, 8:16], SC2[:, u % 16, :])
                    link(ins)
                    for u in us:
                        ins = dve.max_index(IDX[:, u, 8:16].bitcast(U32), VAL[:, u, 8:16], SC2[:, u % 16, :])
                    link(ins)
                link(dve.tensor_copy(IDXF[:, :, :], IDX[:, :, :].bitcast(U32)))
                v = VAL[:, :, :].rearrange("p (u h) n -> p u h n", h=2)
                x = IDXF[:, :, :].rearrange("p (u h) n -> p u h n", h=2)
                o = 0
                for i in range(8):
                    n = CAND_ROWS[i]
                    dve.tensor_tensor(CAND[:, :, o:o + n], v[:, :, 0, i:i + 1].broadcast_to([P, 16, n]), v[:, :, 1, 0:n], ALU.add)
                    dve.scalar_tensor_tensor(CIDX[:, :, o:o + n], x[:, :, 0, i:i + 1].broadcast_to([P, 16, n]), float(NKEYS), x[:, :, 1, 0:n], ALU.mult, ALU.add)
                    o += n
                dve.tensor_tensor(CAND[:, :, o:o + 8], v[:, :, 0, 8:16], v[:, :, 1, 0:1].broadcast_to([P, 16, 8]), ALU.add)
                link(dve.scalar_tensor_tensor(CIDX[:, :, o:o + 8], x[:, :, 0, 8:16], float(NKEYS), x[:, :, 1, 0:1].broadcast_to([P, 16, 8]), ALU.mult, ALU.add))
                for u in range(16):
                    ins = dve.max(TOPV[:, u, 0:8], CAND[:, u, :])
                link(ins)
                for u in range(16):
                    dve.max_index(POS[:, u, 0:8].bitcast(U32), TOPV[:, u, 0:8], CAND[:, u, :])
                    ins = dve.match_replace(CAND2[:, u, :], TOPV[:, u, 0:8], CAND[:, u, :], NEG)
                link(ins)
                for u in range(16):
                    ins = dve.max(TOPV[:, u, 8:16], CAND2[:, u, :])
                link(ins)
                for u in range(16):
                    ins = dve.max_index(POS[:, u, 8:16].bitcast(U32), TOPV[:, u, 8:16], CAND2[:, u, :])
                link(ins)
                link(dve.tensor_tensor(GATE[:, :, :], TOPV[:, :, :], TOPV[:, :, 0:1].broadcast_to([P, 16, 16]), ALU.subtract))
                dve.sem_inc(gdiff_ready, 1)
                link(dve.tensor_copy(POSF[:, :, :], POS[:, :, :].bitcast(U32)))
                cpos = iota[:, 0:NC].unsqueeze(1).broadcast_to([P, 16, NC])
                for u in range(16):
                    e = EQ[:, u % 2, :, :]
                    link(dve.tensor_tensor(e, POSF[:, u, :].unsqueeze(2).broadcast_to([P, 16, NC]), cpos, ALU.is_equal))
                    link(dve.tensor_tensor(e, e, CIDX[:, u, :].unsqueeze(1).broadcast_to([P, 16, NC]), ALU.mult))
                    ins = dve.tensor_reduce(EIDX[:, u, :], e, AX.X, ALU.add)
                link(ins)
                link(dve.tensor_copy(POS[:, :, :].bitcast(I32), EIDX[:, :, :]))
                dve.tensor_scalar(I1F[:, :, :].bitcast(I32), POS[:, :, :].bitcast(I32), 7, None, ALU.logical_shift_right)
                link(dve.tensor_scalar(I2F[:, :, :].bitcast(I32), POS[:, :, :].bitcast(I32), NKEYS - 1, None, ALU.bitwise_and))
                dve.tensor_copy(I1F[:, :, :], I1F[:, :, :].bitcast(I32))
                dve.tensor_copy(I2F[:, :, :], I2F[:, :, :].bitcast(I32))

            def gates():
                dve.wait_ge(gexp_ready, 1)
                link(dve.tensor_reduce(STAT[:, 16:32], GATE[:, :, :], AX.X, ALU.add))
                link(dve.reciprocal(STAT[:, 32:48], STAT[:, 16:32]))
                link(dve.tensor_tensor(GATE[:, :, :], GATE[:, :, :], STAT[:, 32:48].unsqueeze(2).broadcast_to([P, 16, 16]), ALU.mult))
                dve.sem_inc(sel_ready, 1)

            def u_lows(m, j):
                dve.wait_ge(u_hi, 8 * j + m + 1)
                dve.tensor_tensor(EL[:, m % 4, :], RING[:, m // 4, (m % 4) * 512:(m % 4 + 1) * 512], EH[:, m % 4, :].bitcast(F32), ALU.subtract).then_inc(u_lo, 1)

            def v_lows(m, j):
                dve.wait_ge(v_hi, 8 * j + m + 1)
                dve.tensor_tensor(EL[:, m % 4, :], RING[:, m // 4, (m % 4) * 512:(m % 4 + 1) * 512], EH[:, m % 4, :].bitcast(F32), ALU.subtract).then_inc(v_lo, 1)

            def a_lows(e, j):
                dve.wait_ge(a_hi, 4 * j + e + 1)
                dve.tensor_tensor(AL[:, e % 2, :], ACTS[:, 4 * j + e, :], AH[:, e % 2, :].bitcast(F32), ALU.subtract).then_inc(a_lo, 1)

            def hots(i, q, first):
                if not first:
                    dve.wait_ge(quad_done, q - 2)
                dve.tensor_tensor(HOT[i][:, 0:7, :], iota.unsqueeze(1).broadcast_to([P, 7, P]),
                                  IDXQ[:, bass.ds(q, 1), 0:7].rearrange("p a m -> p (a m)").unsqueeze(2).broadcast_to([P, 7, P]), ALU.is_equal).then_inc(hot_eq, 1)

            def gated(i, q):
                dve.wait_ge(quad_done, q + 1)
                a = ACTS[:, :, bass.ds(4 * q, 4)]
                dve.tensor_tensor(a, a, PS[:, i, :].rearrange("p (t e) -> p e t", t=4), ALU.mult).then_inc(quad_out, 1)

            with dve.Fori(0, L) as l:
                steps[0] = 0
                norm_rows(0, HN)
                dve.wait_ge(params_landed, 64)
                evac_h(C_MIX, 0)
                for g in range(6):
                    mix(g)
                rwkv_prep()
                rotate()
                link(dve.memset(GACC[:, 0:2, :, :], 0.0))
                level(0, 4)
                level(1, 6)
                decayed(0, 4)
                level(2, 6)
                level(3, 4)
                decayed(1, 6)
                level(4, 4)
                level(5, 6)
                level(6, 6)
                level(7, 4)
                level(8, 6)
                rwkv_units()
                rwkv_chunks()
                rwkv_out()
                dve.sem_inc(rwkv_ready, 1)
                dve.wait_ge(res_done, N_OUT)
                for t in range(NT):
                    for f in range(2):
                        xs = X[:, t, f * 512:(f + 1) * 512]
                        dve.tensor_tensor(xs, xs, PS[:, 4 + 2 * t + f, :], ALU.add).then_inc(res_out, 1)
                dve.wait_ge(res_out, 4)
                norm_rows(1, HNF)
                evac_h(C_FFN, 1)
                dve.wait_ge(split_ready, 1)
                dve.tensor_tensor(HTL[:, :, :], HT[:, :, :], HTH[:, :, :].bitcast(F32), ALU.subtract).then_inc(split_ready, 1)
                topk()
                with dve.Fori(POOL_BODIES, GATE_BODY) as j:
                    for m in range(8):
                        u_lows(m, j)
                gates()
                with dve.Fori(GATE_BODY, N_BODY) as j:
                    for m in range(8):
                        u_lows(m, j)
                dve.wait_ge(u_act, 128)
                dve.wait_ge(sel_out, 3)
                for i in range(3):
                    hots(i, i, True)
                gated(0, 0)
                with dve.Fori(1, 21) as q:
                    for i in range(3):
                        hots(i, 3 * q + i, False)
                        gated((i + 1) % 3, 3 * q + i - 2)
                hots(0, 63, False)
                for q in range(61, 64):
                    gated(q % 3, q)
                for m in range(8):
                    if m % 2 == 0:
                        a_lows(m // 2, 0)
                    v_lows(m, 0)
                with dve.Fori(1, 32) as j:
                    for m in range(8):
                        if m % 2 == 0:
                            a_lows(m // 2, j)
                        v_lows(m, j)
                dve.wait_ge(v_done, 256)
                for t in range(NT):
                    for f in range(2):
                        xs = X[:, t, f * 512:(f + 1) * 512]
                        link(dve.tensor_tensor(xs, xs, PS[:, 2 * t + f, :], ALU.add))
                dve.sem_inc(peer_out, 1)
                dve.sem_inc(arrived, 1)
                dve.wait_ge(go, l + 1)
            dve.wait_ge(final_ss, NT)
            dve.tensor_scalar(STAT[:, 0:2], STAT[:, 0:2], 1.0 / D, NORM_EPS, ALU.mult, ALU.add).then_inc(final_ms, 1)
            dve.wait_ge(final_rt, 1)
            dve.reciprocal(STAT[:, 0:2], STAT[:, 2:4]).then_inc(final_ms, 1)
            dve.wait_ge(final_ms, 2)
            dve.wait_ge(final_row, 16)
            for t in range(NT):
                dve.scalar_tensor_tensor(YOUT[:, t, :], X[:, t, :], STAT[:, t:t + 1], FROW, ALU.mult, ALU.mult).then_inc(y_ready, 1)

        @block.gpsimd
        def _(pool):
            pool.wait_ge(const_landed, 32)

            def u_lows(m, j):
                pool.wait_ge(u_hi, 8 * j + m + 1)
                pool.tensor_tensor(EL[:, m % 4, :], RING[:, m // 4, (m % 4) * 512:(m % 4 + 1) * 512], EH[:, m % 4, :].bitcast(F32), ALU.subtract).then_inc(u_lo_pool, 1)

            steps = [0]

            def link(ins):
                steps[0] += 1
                ins.then_inc(pool_step, 1)
                pool.wait_ge(pool_step, steps[0])

            def blocks(v, n):
                return v.rearrange("p b (q a n) -> p (b q) a n", a=2, n=2 ** (n - 1))

            def level_gates(n):
                b = 2 ** (n - 1)
                B, E = blocks(GB[:, :, :], n), blocks(GE[:, n % 2, :, :], n)
                ref = B[:, :, 0, b - 1:b].broadcast_to([P, S // b, b])
                pool.tensor_tensor(E[:, :, 0, :], ref, B[:, :, 0, :], ALU.subtract)
                pool.tensor_tensor(E[:, :, 1, :], B[:, :, 1, :], ref, ALU.subtract).then_inc(gd_ready, 1)

            def level_operand(n):
                E, XX, Q, K = (blocks(v, n) for v in (GE[:, n % 2, :, :], GX[:, n % 2, :, :], GQK[:, 0:2, :], GQK[:, 2:4, :]))
                if n >= 2:
                    pool.wait_ge(gs_done, n - 1)
                pool.wait_ge(ge_ready, n)
                pool.tensor_tensor(XX[:, :, 0, :], K[:, :, 0, :], E[:, :, 0, :], ALU.mult)
                link(pool.tensor_tensor(XX[:, :, 1, :], Q[:, :, 1, :], E[:, :, 1, :], ALU.mult))
                pool.sem_inc(gx_ready, 1)

            def finish_heads(dst, heads, w, at, gate):
                for t in range(NT):
                    d = dst[:, t, :].rearrange("p (h n) -> p h n", h=heads)
                    link(pool.tensor_tensor(d, d, STAT[:, at + heads * t:at + heads * (t + 1)].unsqueeze(2).broadcast_to([P, heads, w]), ALU.mult))
                link(pool.tensor_tensor(dst, dst, gate, ALU.mult))

            def last_row(i, q, first):
                if not first:
                    pool.wait_ge(quad_done, q - 2)
                pool.tensor_copy(PQ[:, i, 0:1], IDXQ[:, bass.ds(q, 1), 7])
                pool.tensor_copy(PQ[:, i, 1:2], GATET[:, bass.ds(4 * q + 3, 1)]).then_inc(pool_copied, 1)
                pool.wait_ge(pool_copied, q + 1)
                pool.sem_inc(pool_seen, 1)
                pool.tensor_scalar(HOT[i][:, 7, :], iota, PQ[:, i, 0:1], PQ[:, i, 1:2], ALU.is_equal, ALU.mult).then_inc(hot_pool, 1)

            with pool.Fori(0, L) as l:
                pool.memset(RAW[:, :, :, 0:1], 0.0).then_inc(zeros_ready, 1)
                steps[0] = 0
                pool.wait_ge(gcum_ready, 1)
                pool.wait_ge(proj_out, 8)
                level_gates(1)
                for n in range(1, 9):
                    if n < 8:
                        level_gates(n + 1)
                    level_operand(n)
                pool.wait_ge(hrstd_ready, 1)
                pool.wait_ge(silu_ready, 2)
                finish_heads(HN[:, :, 0:256], RH, RDK, 80, ZRET[:, :, 768:1024])
                pool.sem_inc(mix_ready, 1)
                finish_heads(HN[:, :, 640:1024], GH, GDV, 88, ZGLA[:, :, 384:768])
                for t in range(NT):
                    link(pool.tensor_tensor(HN[:, t, 640:1024], HN[:, t, 640:1024], ROWS[:, 768:1152], ALU.mult))
                pool.sem_inc(mix_ready, 1)
                for m in range(8):
                    u_lows(m, 0)
                with pool.Fori(1, POOL_BODIES) as j:
                    for m in range(8):
                        u_lows(m, j)
                pool.wait_ge(u_act, 128)
                pool.wait_ge(sel_out, 3)
                for i in range(3):
                    last_row(i, i, True)
                with pool.Fori(1, 21) as q:
                    for i in range(3):
                        last_row(i, 3 * q + i, False)
                last_row(0, 63, False)
                pool.sem_inc(arrived, 1)
                pool.wait_ge(go, l + 1)


def constants():
    const = np.zeros((P, N_CONST), np.float32)
    const[:, K_ID:K_ID + P] = np.eye(P)
    const[:, K_IOTA:K_IOTA + P] = np.arange(P)
    x = np.zeros((P, N_XCONST), np.float32)
    i = np.arange(P)
    x[:, X_MASK2:X_MASK2 + P] = i[:, None] < i[None, :]
    x[:, X_MASK2 + P:X_MASK2 + 256] = i[:, None] <= i[None, :]
    for n, b in enumerate(LEVELS):
        low = (i[:, None] // (2 * b) == i[None, :] // (2 * b)) & ((i[:, None] // b) % 2 == 1) & ((i[None, :] // b) % 2 == 0)
        x[:, X_LOW + P * n:X_LOW + P * (n + 1)] = low
        x[:, X_UP + P * n:X_UP + P * (n + 1)] = low.T
    x[:, X_ONES:X_ONES + 2] = 1
    x[:, X_BLK:X_BLK + P] = i[:, None] // 64 == i[None, :] // 64
    x[:, X_HEAD:X_HEAD + 2] = i[:, None] // 64 == np.arange(2)[None, :]
    lg = np.log1p(-np.exp(np.linspace(np.log(1 / 32), np.log(1 / 512), RH)))
    for h in range(RH):
        diff = (i[None, :] - i[:, None]).astype(np.float64)
        x[:, X_DM + 256 * h:X_DM + 256 * h + P] = np.where(diff >= 0, np.exp(lg[h] * np.maximum(diff, 0)), 0) * RDK ** -0.5
        x[:, X_DM + 256 * h + P:X_DM + 256 * (h + 1)] = np.exp(lg[h] * (diff + P)) * RDK ** -0.5
    inv = (10000.0 ** (-np.arange(32, dtype=np.float32) / 32)).astype(np.float32)
    ang = np.arange(S, dtype=np.float32)[:, None] * inv[None, :]
    for t in range(NT):
        a = ang[t * P:(t + 1) * P]
        x[:, X_ROPE + 64 * t:X_ROPE + 64 * t + 32] = np.cos(a)
        x[:, X_ROPE + 64 * t + 32:X_ROPE + 64 * (t + 1)] = np.sin(a)
    return const, x


def lay_out(a):
    f = np.float32

    def chunked(w):
        g = w.shape[2] // GC
        return np.ascontiguousarray(w.reshape(L, DC, P, g, GC).transpose(0, 3, 2, 1, 4)).reshape(L, g, P, DC * GC)

    def head_pad(w):
        w = w.reshape(*w.shape[:-1], GH, GDK)
        return np.concatenate([w, np.zeros((*w.shape[:-1], 64 - GDK), f)], -1).reshape(*w.shape[:-2], GH * 64)

    w = a["w_in"]
    r0 = 1024
    g0 = r0 + 1408
    rwkv = w[:, :, r0:g0]
    rw = [rwkv[:, :, 1152:1280], rwkv[:, :, 1280:1408], rwkv[:, :, 384:768], rwkv[:, :, 0:384], rwkv[:, :, 768:1152]]
    gkd = w[:, :, g0 + 768:g0 + 784]
    w_in = chunked(np.concatenate([*rw, gkd, np.zeros((L, D, 112), f), head_pad(w[:, :, g0:g0 + 192]), head_pad(w[:, :, g0 + 192:g0 + 384]),
                                   w[:, :, 0:1024], w[:, :, g0 + 384:g0 + 768], w[:, :, g0 + 784:g0 + 1168]], -1))
    w_out = a["w_out"].reshape(L, DC, P, D)[:, OUT_CHUNKS].reshape(L, N_OUT, 2, P, D)
    w_out = np.ascontiguousarray(w_out.transpose(0, 1, 3, 2, 4)).reshape(L, N_OUT, P, 2 * D)
    mu = a["rwkv_mu"]
    mu = np.concatenate([mu[:, 1152:1280], mu[:, 1280:1408], mu[:, 384:768], mu[:, 0:384], mu[:, 768:1152]], -1)

    def column(v):
        return v.reshape(L, -1, P).transpose(0, 2, 1)

    cols = np.concatenate([column(v) for v in (a["norm_mix"], a["norm_ffn"], mu, a["rwkv_w_bias"], a["rwkv_a_bias"], a["rwkv_k_k"],
                                               a["rwkv_k_a"], a["rwkv_r_k"].reshape(L, -1), head_pad(a["gla_gk_bias"]))], -1)
    small = np.zeros((L, P, N_SMALL), f)
    small[:, 0:64, W_WA:W_WA + 384] = a["rwkv_w_up"]
    small[:, 64:128, W_WA:W_WA + 384] = a["rwkv_a_up"]
    small[:, :, W_G:W_G + 384] = a["rwkv_g_up"]
    small[:, 0:16, W_GK:W_GK + 256] = head_pad(a["gla_gk_up"])
    rows = np.concatenate([a["rwkv_ln_w"], a["rwkv_ln_b"], a["gla_norm_w"]], -1)
    keys = np.ascontiguousarray(a["peer_sub_keys"].reshape(L, 16, P, P).transpose(0, 3, 1, 2)).reshape(L, P, 2048)
    u_t = a["peer_u"].reshape(L, P, 64, 2, DC, P).transpose(0, 2, 5, 3, 4, 1)
    v_t = a["peer_v"].reshape(L, P, 64, 2, D).transpose(0, 2, 1, 3, 4)
    const, xconst = constants()
    return {"x_in": a["x"], "w_in": w_in, "w_out": w_out, "cols": cols, "small": small, "rows": rows, "norm_final": a["norm_final"],
            "w_q": chunked(a["peer_w_q"]), "keys": keys, "u_t": u_t.reshape(L, 64, P, 2048), "v_t": v_t.reshape(L, 64, P, 2048),
            "const": const, "xconst": xconst}


def kernel(**inputs):
    import concourse.bacc as _bacc
    from concourse.bass_utils import run_bass_kernel_spmd as _run

    arrays = {k: np.ascontiguousarray(v) for k, v in lay_out({k: np.asarray(v) for k, v in inputs.items()}).items()}
    nc = _bacc.Bacc("TRN2", target_bir_lowering=False, num_devices=1)
    args = {k: nc.dram_tensor(k, v.shape, F32, kind="ExternalInput").ap() for k, v in arrays.items()}
    out = nc.dram_tensor("y_out", (1, S, D), F32, kind="ExternalOutput").ap()
    trunk(nc, *args.values(), out)
    r = _run(nc, [arrays], core_ids=[0])
    return r.results[0]["y_out"]
```

```python
from contextlib import ExitStack

import numpy as np

import concourse.bass as bass
from concourse import mybir

F32 = mybir.dt.float32
F32R = mybir.dt.float32r
U32 = mybir.dt.uint32
I32 = mybir.dt.int32
ALU = mybir.AluOpType
ACT = mybir.ActivationFunctionType
AX = mybir.AxisListType

P = 128
S = 256
NT = S // P
D = 1024
DC = D // P
L = 2
NH = 6
CT = 3
GH, GDK, GDV = 4, 48, 96
RH, RDK = 4, 64
GC = 256
N_IN = 15
N_CH = 8
N_OUT = 4
OUT_CHUNKS = [0, 1, 5, 6, 7, 2, 3, 4]
N_EARLY = 5
PH, TOPK, NKEYS = 8, 16, 128
NEG = -3.0e38
N_BODY, POOL_BODIES, EXP_BODY, GATE_BODY, SEL_BODY = 32, 9, 10, 11, 14
KEY_LOAD = N_IN + N_OUT
N_RING = KEY_LOAD + 1 + PH
IN_SPLIT, Q_SPLIT = range(1, N_IN), range(1, PH)
POOL_SPLIT = 10
SPLIT = [*IN_SPLIT, *(KEY_LOAD + 1 + g for g in Q_SPLIT)]
WHOLE = [n for n in range(N_RING) if n not in SPLIT and n != KEY_LOAD]
N_EQ = [5, 6, 6]
LOG_DECAY_SCALE = -float(np.exp(-0.5))
NORM_EPS, HEAD_EPS, GN_EPS = 1e-6, 1e-5, 64e-5
CAND_ROWS = [TOPK // (i + 1) for i in range(TOPK)]
NC = sum(CAND_ROWS)

C_MIX, C_FFN, C_MU, C_WB, C_AB, C_KK, C_KA, C_RK, C_GB = 0, 8, 16, 27, 30, 33, 36, 39, 42
N_COLS = 44
W_WA, W_G, W_GK = 0, 384, 768
N_SMALL = 1024
K_ID, K_IOTA = 0, 128
N_CONST = 256
LEVELS = [1, 2, 4, 8, 16, 32, 64]
X_MASK2 = 0
X_LOW = 256
X_UP = X_LOW + 128 * 7
X_ONES = X_UP + 128 * 7
X_BLK = X_ONES + 2
X_HEAD = X_BLK + 128
X_DM = X_HEAD + 2
X_ROPE = X_DM + RH * 256
N_XCONST = X_ROPE + NT * 64


def trunk(nc, x_in, w_in, w_out, cols, small, rows, norm_final, w_q, keys, u_t, v_t, const, xconst, out):
    with ExitStack() as ctx:
        def sb(name, shape, dt=F32):
            return ctx.enter_context(nc.sbuf_tensor(name, shape, dt))

        layer_sems = []

        def sem(name, per_layer=True):
            s = ctx.enter_context(nc.semaphore(name))
            if per_layer:
                layer_sems.append(s)
            return s

        X = sb("x_res", [P, NT, D])
        HT = sb("h_t", [P, DC, S])
        HTH = sb("h_t_hi", [P, DC, S], F32R)
        HTL = sb("h_t_lo", [P, DC, S], F32R)
        RING = sb("w_ring", [P, 2, 2048])
        EH = sb("expert_hi", [P, 4, 512], F32R)
        EL = sb("expert_lo", [P, 4, 512], F32R)
        AH = sb("act_hi", [P, 2, S], F32R)
        AL = sb("act_lo", [P, 2, S], F32R)
        KONST = sb("const_sb", [P, N_CONST])
        COLS = sb("cols_sb", [P, N_COLS])
        IDXQ = sb("idx_quads", [P, S // 4, 8])
        GATET = sb("gate_t", [P, S])
        NEGI1 = sb("neg_i1", [P, S])
        NEGATE = sb("neg_gate", [P, S])
        HOTX = sb("hot_extra", [P, 1024])
        STAT = sb("stat", [P, 96])
        PQ = sb("pool_scalars", [P, 3, 2])
        BIGW = 128 * S
        BIG = sb("big", [P, BIGW])
        PS = ctx.enter_context(nc.psum_tensor("ps", [P, 8, 512], F32))

        ident = KONST[:, K_ID:K_ID + 128]
        iota = KONST[:, K_IOTA:K_IOTA + 128]

        used = [0]

        def big(n):
            a = used[0]
            used[0] += n
            assert used[0] <= BIGW, used[0]
            return BIG[:, a:a + n]

        XC = big(N_XCONST)
        HN = big(NT * D).rearrange("p (t d) -> p t d", t=NT)
        SM = big(N_SMALL)
        ROWS = big(1152)
        RAW = big(2 * 2 * 257).rearrange("p (s b n) -> p s b n", s=2, b=2)
        FM = big(12 * S).rearrange("p (b n) -> p b n", b=12)
        SIGA = big(CT * 2 * S).rearrange("p (c k n) -> p c k n", c=CT, k=2)
        decays = used[0]
        CUM = big(CT * NT * 129).rearrange("p (c k n) -> p c k n", c=CT, k=NT)
        E1 = big(CT * NT * 129).rearrange("p (c k n) -> p c k n", c=CT, k=NT)
        E2 = big(CT * S).rearrange("p (c n) -> p c n", c=CT)
        BTOK = BIG[:, decays:decays + 384]
        KTOK = BIG[:, decays + 384:decays + 768]
        XU = BIG[:, decays + 768:decays + 1536].rearrange("p (a n) -> p a n", a=2)
        STATE = BIG[:, decays + 1536:decays + 1728].rearrange("p (c n) -> p c n", c=CT)
        AR = big(CT * NT * 256).rearrange("p (c k m n) -> p c k m n", c=CT, k=NT, m=2)
        BT = big(CT * S).rearrange("p (c n) -> p c n", c=CT)
        KT = big(CT * S).rearrange("p (c n) -> p c n", c=CT)
        KKN = big(CT * S).rearrange("p (c n) -> p c n", c=CT)
        TMP = big(CT * S).rearrange("p (c n) -> p c n", c=CT)
        MASKED = big(12 * 512).rearrange("p (u m n) -> p u m n", u=12, m=4)
        fm_flat = FM.rearrange("p b n -> p (b n)")
        TI = fm_flat[:, 0:1536].rearrange("p (u n) -> p u n", u=12)
        TT = fm_flat[:, 1536:3072].rearrange("p (u n) -> p u n", u=12)
        Y = SIGA.rearrange("p c k n -> p (c k n)").rearrange("p (u n) -> p u n", u=12)
        VTOK = KKN.rearrange("p c n -> p (c n)").rearrange("p (k n) -> p k n", k=NT)
        GG = RAW.rearrange("p s b n -> p (s b n)")[:, 0:780].rearrange("p (k n) -> p k n", k=NT)
        ZRET = big(NT * 1024).rearrange("p (t n) -> p t n", t=NT)
        ZGLA = big(NT * 768).rearrange("p (t n) -> p t n", t=NT)
        GBIAS = ZRET[:, :, 0:384]
        GQK = big(4 * S).rearrange("p (b n) -> p b n", b=4)
        GB = big(2 * S).rearrange("p (b n) -> p b n", b=2)
        GX = big(2 * 2 * S).rearrange("p (s b n) -> p s b n", s=2, b=2)
        mflat = MASKED.rearrange("p u m n -> p (u m n)")
        ROT = mflat[:, 0:1024].rearrange("p (t g h c) -> p t g h c", t=NT, g=8, h=2)
        QKT = mflat[:, 1024:2048].rearrange("p (b n) -> p b n", b=4)
        SCR = mflat[:, 2048:3584].rearrange("p (h n) -> p h n", h=RH)
        RTMP = mflat[:, 3584:4096].rearrange("p (t n) -> p t n", t=NT)
        GE = mflat[:, 4096:5120].rearrange("p (s b n) -> p s b n", s=2, b=2)
        GACC = BIG[:, decays:decays + 1536].rearrange("p (t h n) -> p t h n", t=3, h=GH)
        RSQ = HOTX[:, 0:512].rearrange("p (t n) -> p t n", t=NT)
        GSQ = GX.rearrange("p s b n -> p (s b n)")[:, 0:768].rearrange("p (t n) -> p t n", t=NT)
        XB = TT.rearrange("p u n -> p (u n)")[:, 0:768].rearrange("p (k n) -> p k n", k=NT)
        OT = HT
        used[0] = 0
        QT = big(16 * S).rearrange("p (b n) -> p b n", b=16)
        HNF = big(NT * D).rearrange("p (t d) -> p t d", t=NT)
        KEYS = big(16 * P).rearrange("p (b n) -> p b n", b=16)
        used[0] = 4 * (SEL_BODY + 1) * S
        SC = big(NT * 2048).rearrange("p (u n) -> p u n", u=32)
        SC2 = big(2048).rearrange("p (u n) -> p u n", u=16)
        VAL = big(32 * 16).rearrange("p (u n) -> p u n", u=32)
        IDX = big(32 * 16).rearrange("p (u n) -> p u n", u=32)
        IDXF = big(32 * 16).rearrange("p (u n) -> p u n", u=32)
        CAND = big(16 * NC).rearrange("p (u n) -> p u n", u=16)
        CAND2 = big(16 * NC).rearrange("p (u n) -> p u n", u=16)
        CIDX = big(16 * NC).rearrange("p (u n) -> p u n", u=16)
        TOPV, POS, POSF, EIDX, GATE, I1F, I2F = (big(256).rearrange("p (u n) -> p u n", u=16) for _ in range(7))
        EQ = big(2 * 16 * NC).rearrange("p (s k n) -> p s k n", s=2, k=16)
        ACTS = BIG[:, :].rearrange("p (e t) -> p e t", t=S)
        ht_flat = HT[:, :, :].rearrange("p c n -> p (c n)")
        HOT = [v.rearrange("p (m n) -> p m n", m=8) for v in (ht_flat[:, 0:1024], ht_flat[:, 1024:2048], HOTX[:, :])]
        FROW = BIG[:, 0:D]
        YOUT = BIG[:, D:D + NT * D].rearrange("p (t d) -> p t d", t=NT)

        const_landed = sem("const_landed", False)
        x_landed = [sem("x0_landed", False), sem("x1_landed", False)]
        go = sem("layer_go", False)
        first_landed = sem("first_landed", False)
        params_landed, ring0_landed, ring1_landed = sem("params_landed"), sem("ring0_landed"), sem("ring1_landed")
        ring_free, keys_copied = sem("ring_free"), sem("keys_copied")
        sumsq_ready, rms_ready, rstd_ready, rstd_turned = sem("sumsq_ready"), sem("rms_ready"), sem("rstd_ready"), sem("rstd_turned")
        h_ready, h_turned, ht_ready = sem("h_ready"), sem("h_turned"), sem("ht_ready")
        proj_done, proj_out = sem("proj_done"), sem("proj_out")
        mixed = sem("mixed")
        zeros_ready = sem("zeros_ready")
        tanh_ready, lora_done, sig_ready = sem("tanh_ready"), sem("lora_done"), sem("sig_ready")
        cum_ready, exp_ready = sem("cum_ready"), sem("exp_ready")
        kksq_ready, kknorm_done, kkmax_ready, kksqrt_ready = sem("kksq_ready"), sem("kknorm_done"), sem("kkmax_ready"), sem("kksqrt_ready")
        gg_done, gg_out = sem("gg_done"), sem("gg_out")
        rk_ready, ab_ready = sem("rk_ready"), sem("ab_ready")
        vtok_done, vtok_out = sem("vtok_done"), sem("vtok_out")
        unit_done, unit_out = sem("unit_done"), sem("unit_out")
        mrow_done, mrow_out = sem("mrow_done"), sem("mrow_out")
        ti_ready, tt_ready = sem("ti_ready"), sem("tt_ready")
        y_done, y_out, z_done, z_out = sem("y_done"), sem("y_out"), sem("z_done"), sem("z_out")
        bk_done, bk_out = sem("bk_done"), sem("bk_out")
        chunk_x, chunk_x_out, chunk_u, chunk_u_out = sem("chunk_x"), sem("chunk_x_out"), sem("chunk_u"), sem("chunk_u_out")
        chunk_o, chunk_o_out, state_done, state_out = sem("chunk_o"), sem("chunk_o_out"), sem("state_done"), sem("state_out")
        var_ready, sd_ready = sem("var_ready"), sem("sd_ready")
        rot_ready, rot_done, rot_out = sem("rot_ready"), sem("rot_done"), sem("rot_out")
        score_done, score_out, ret_o, ret_o_out = sem("score_done"), sem("score_out"), sem("ret_o"), sem("ret_o_out")
        gk_done, gk_out, gln_ready = sem("gk_done"), sem("gk_out"), sem("gln_ready")
        gd_ready, ge_ready, gx_ready, gs_done, gs_out = sem("gd_ready"), sem("ge_ready"), sem("gx_ready"), sem("gs_done"), sem("gs_out")
        gla_o, gla_o_out = sem("gla_o"), sem("gla_o_out")
        gacc_zero = sem("gacc_zero")
        silu_ready, gcum_ready, sq_ready = sem("silu_ready"), sem("gcum_ready"), sem("sq_ready")
        hvar_ready, hsd_ready, hrstd_ready = sem("hvar_ready"), sem("hsd_ready"), sem("hrstd_ready")
        rwkv_affine = sem("rwkv_affine")
        mix_ready, rwkv_ready = sem("mix_ready"), sem("rwkv_ready")
        ot_done, ot_out = sem("ot_done"), sem("ot_out")
        res_done, res_out = sem("res_done"), sem("res_out")
        split_ready = sem("split_ready")
        w_hi, w_lo_pool, w_lo, w_done = sem("w_hi"), sem("w_lo_pool"), sem("w_lo"), sem("w_done")
        q_done, q_out, sc_done, sc_out = sem("q_done"), sem("q_out"), sem("sc_done"), sem("sc_out")
        passed, arrived = sem("passed"), sem("layer_arrived")
        dve_step, act_step, pool_step = sem("dve_step"), sem("act_step"), sem("pool_step")
        gdiff_ready, gexp_ready, sel_ready, sel_done, sel_out = sem("gdiff_ready"), sem("gexp_ready"), sem("sel_ready"), sem("sel_done"), sem("sel_out")
        uring = [sem("u0_landed"), sem("u1_landed")]
        u_lo_pool = sem("u_lo_pool")
        u_hi, u_lo, u_done, u_act = sem("u_hi"), sem("u_lo"), sem("u_done"), sem("u_act")
        hot_eq, hot_gate, hot_pool, quad_done, quad_out = (sem(n) for n in ("hot_eq", "hot_gate", "hot_pool", "quad_done", "quad_out"))
        hot_dist = sem("hot_dist")
        pool_copied, pool_seen = sem("pool_copied"), sem("pool_seen")
        vring = [sem("v0_landed"), sem("v1_landed")]
        v_hi, v_lo, a_hi, a_lo, v_done = sem("v_hi"), sem("v_lo"), sem("a_hi"), sem("a_lo"), sem("v_done")
        peer_out = sem("peer_out")
        final_row, y_ready, stored = sem("final_row", False), sem("y_ready", False), sem("stored", False)
        ring_landed = [ring0_landed, ring1_landed]

        def lows_made(i, m):
            return (w_lo_pool, 4 * i + m + 1) if i < POOL_SPLIT else (w_lo, 4 * (i - POOL_SPLIT) + m + 1)

        def freed(n):
            if n in SPLIT:
                return lows_made(SPLIT.index(n), 3)
            if n == KEY_LOAD:
                return keys_copied, 1
            return ring_free, WHOLE.index(n) + 1

        def in_group_done(g):
            return (w_done, 4 * SPLIT.index(g) + 4) if g in IN_SPLIT else (proj_done, WHOLE.index(g) + 1)

        def q_group_done(g):
            return (w_done, 4 * SPLIT.index(KEY_LOAD + 1 + g) + 4) if g in Q_SPLIT else (q_done, 1)


        block = ctx.enter_context(nc.Block())

        early = layer_sems[:layer_sems.index(sc_out) + 1]

        @block.sync
        def _(sp):
            def first_loads(l):
                sp.dma_start(COLS[:, :], cols[l]).then_inc(first_landed, 16)
                for i in range(2):
                    sp.dma_start(RING[:, i, :], w_in[l, i]).then_inc(first_landed, 16)

            for t in range(NT):
                sp.dma_start(X[:, t, :], x_in[0, t * P:(t + 1) * P, :]).then_inc(x_landed[t], 16)
            sp.dma_start(KONST[:, :], const).then_inc(const_landed, 16)
            first_loads(0)
            with sp.Fori(0, L) as l:
                sp.dma_start(XC, xconst).then_inc(params_landed, 16)
                sp.dma_start(SM, small[l]).then_inc(params_landed, 16)
                sp.dma_start(ROWS, rows[l].partition_broadcast(P)).then_inc(params_landed, 16)
                src = ([w_in[l, g] for g in range(N_IN)] + [w_out[l, g] for g in range(N_OUT)] + [keys[l]]
                       + [w_q[l, g] for g in range(PH)])
                for n in range(2, N_RING):
                    sp.wait_ge(*freed(n - 2))
                    sp.dma_start(RING[:, n % 2, :], src[n]).then_inc(ring_landed[n % 2], 16)
                for i in range(2):
                    sp.wait_ge(*freed(N_RING - 2 + i))
                    sp.dma_start(RING[:, i, :], u_t[l, i]).then_inc(uring[i], 16)
                with sp.Fori(1, POOL_BODIES + 1) as j:
                    for i in range(2):
                        sp.wait_ge(u_lo_pool, 8 * j + 4 * i - 4)
                        sp.dma_start(RING[:, i, :], u_t[l, 2 * j + i]).then_inc(uring[i], 16)
                with sp.Fori(1, N_BODY - POOL_BODIES) as j:
                    for i in range(2):
                        sp.wait_ge(u_lo, 8 * j + 4 * i - 4)
                        sp.dma_start(RING[:, i, :], u_t[l, 2 * (j + POOL_BODIES) + i]).then_inc(uring[i], 16)
                sp.wait_ge(passed, 4)
                for s in early:
                    sp.sem_clear(s)
                for i in range(2):
                    sp.wait_ge(u_lo, 8 * (N_BODY - POOL_BODIES) - 4 + 4 * i)
                    sp.dma_start(RING[:, i, :], v_t[l, i]).then_inc(vring[i], 16)
                with sp.Fori(1, 32) as j:
                    for i in range(2):
                        sp.wait_ge(v_lo, 8 * j + 4 * i - 4)
                        sp.dma_start(RING[:, i, :], v_t[l, 2 * j + i]).then_inc(vring[i], 16)
                for i in range(2):
                    sp.wait_ge(v_lo, 252 + 4 * i)
                first_loads(L - 1)
                sp.wait_ge(arrived, 4)
                for s in layer_sems:
                    if s not in early:
                        sp.sem_clear(s)
                sp.sem_inc(go, 1)
            sp.dma_start(FROW, norm_final.partition_broadcast(P)).then_inc(final_row, 16)
            for t in range(NT):
                sp.wait_ge(y_ready, t + 1)
                sp.dma_start(out[0, t * P:(t + 1) * P, :], YOUT[:, t, :]).then_inc(stored, 16)
            sp.wait_ge(stored, 16 * NT)

        @block.tensor
        def _(pe):
            pe.wait_ge(const_landed, 16)

            def turn_h(src, k):
                for t in range(NT):
                    pe.wait_ge(h_ready, NT * k + t + 1)
                    for c in range(DC):
                        mm = pe.transpose(PS[:, 2 * t + c // 4, (c % 4) * P:(c % 4 + 1) * P], src[:, t, c * P:(c + 1) * P], ident)
                        if c % 4 == 3:
                            mm.then_inc(h_turned, 1)

            def split_products(i, bank):
                for m in range(4):
                    pe.wait_ge(*lows_made(i, m))
                    w_hi_m = EH[:, m, :].rearrange("p (c n) -> p c n", c=4)
                    w_lo_m = EL[:, m, :].rearrange("p (c n) -> p c n", c=4)
                    o = PS[:, bank, m // 2 * 256:(m // 2 + 1) * 256]
                    for c in range(4):
                        d = 4 * (m % 2) + c
                        pe.matmul(o, w_hi_m[:, c, :], HTH[:, d, :], start=d == 0, stop=False)
                        pe.matmul(o, w_hi_m[:, c, :], HTL[:, d, :], start=False, stop=False)
                        mm = pe.matmul(o, w_lo_m[:, c, :], HTH[:, d, :], start=False, stop=d == DC - 1)
                    mm.then_inc(w_done, 1)

            def split_rows(i, bank, half):
                for t in range(NT) if half is None else [half]:
                    o = PS[:, bank, t * 256:(t + 1) * 256]
                    for m in range(4):
                        pe.wait_ge(*lows_made(i, m))
                        w_hi_m = EH[:, m, :].rearrange("p (c n) -> p c n", c=2)
                        w_lo_m = EL[:, m, :].rearrange("p (c n) -> p c n", c=2)
                        for c in range(2):
                            d = 2 * m + c
                            h_hi, h_lo = HTH[:, d, t * P:(t + 1) * P], HTL[:, d, t * P:(t + 1) * P]
                            pe.matmul(o, h_hi, w_hi_m[:, c, :], start=d == 0, stop=False)
                            pe.matmul(o, h_hi, w_lo_m[:, c, :], start=False, stop=False)
                            mm = pe.matmul(o, h_lo, w_hi_m[:, c, :], start=False, stop=d == DC - 1)
                        if t == NT - 1:
                            mm.then_inc(w_done, 1)

            def group(g, half=None):
                if g >= 4 and half != 1:
                    pe.wait_ge(proj_out, g - 3)
                if g in IN_SPLIT:
                    if g == IN_SPLIT[0]:
                        pe.wait_ge(split_ready, 2)
                    if g < N_CH:
                        split_products(SPLIT.index(g), g % 4)
                    else:
                        split_rows(SPLIT.index(g), g % 4, half)
                    return
                pe.wait_ge(ht_ready, 4)
                w = RING[:, g % 2, :].rearrange("p (b c n) -> p b c n", b=2, c=DC)
                for b in range(2):
                    for c in range(DC):
                        mm = pe.matmul(PS[:, g % 4, b * 256:(b + 1) * 256], w[:, b, c, :], HT[:, c, :], start=c == 0, stop=c == DC - 1)
                mm.then_inc(proj_done, 1)
                pe.wait_ge(proj_done, 1)
                pe.sem_inc(ring_free, 1)

            def lora():
                pe.wait_ge(tanh_ready, 1)
                pe.wait_ge(gk_out, 1)
                for c in range(CT):
                    o = slice(c % 2 * 256, c % 2 * 256 + 256)
                    pe.matmul(PS[:, 4 + c // 2, o], SM[0:64, W_WA + c * P:W_WA + (c + 1) * P], FM[0:64, 0, :], start=True, stop=True)
                    pe.matmul(PS[:, 6 + c // 2, o], SM[64:128, W_WA + c * P:W_WA + (c + 1) * P], FM[64:128, 0, :],
                              start=True, stop=True).then_inc(lora_done, 1)

            def gk_up():
                pe.wait_ge(params_landed, 48)
                pe.wait_ge(mixed, 6)
                for b in range(2):
                    mm = pe.matmul(PS[:, 5, b * 256:(b + 1) * 256], SM[0:16, W_GK + b * P:W_GK + (b + 1) * P], FM[0:16, 11, :],
                                   start=True, stop=True)
                mm.then_inc(gk_done, 1)

            def kk_norm():
                pe.wait_ge(kksq_ready, 1)
                pe.wait_ge(sig_ready, 7)
                for c in range(CT):
                    o = PS[:, 7, c * 256:(c + 1) * 256] if c < 2 else PS[:, 4, 0:256]
                    mm = pe.matmul(o, XC[:, X_BLK:X_BLK + P], TMP[:, c, :], start=True, stop=True)
                mm.then_inc(kknorm_done, 1)

            def gate_and_bonus():
                pe.wait_ge(rk_ready, 1)
                pe.wait_ge(sig_ready, 7)
                pe.wait_ge(kkmax_ready, 1)
                for t in range(NT):
                    pe.matmul(PS[:, 6 + t, 0:384], FM[:, 1, t * P:(t + 1) * P], SM[:, W_G:W_G + 384], start=True, stop=True)
                    for c in range(CT):
                        mm = pe.matmul(PS[:, 6 + t, 384 + 2 * c:386 + 2 * c], TMP[:, c, t * P:(t + 1) * P],
                                       XC[:, X_HEAD:X_HEAD + 2], start=True, stop=True)
                    mm.then_inc(gg_done, 1)

            def v_tok():
                pe.wait_ge(kkmax_ready, 1)
                for k in range(NT):
                    for c in range(CT):
                        mm = pe.transpose(PS[:, 4 + k, c * P:(c + 1) * P], FM[:, 8 + c, k * P:(k + 1) * P], ident)
                    mm.then_inc(vtok_done, 1)

            def units():
                pe.wait_ge(ab_ready, 1)
                pe.wait_ge(gs_out, 9)
                for u in range(12):
                    if u == 6:
                        gla_outputs()
                    k, h = divmod(u, NH)
                    c, r = h // 2, slice(64 * (h % 2), 64 * (h % 2) + 64)
                    if u >= 4:
                        pe.wait_ge(unit_out, u - 3)
                    for m, lhs in enumerate((BT, KT)):
                        mm = pe.matmul(PS[:, 4 + u % 4, m * 256:(m + 1) * 256], lhs[r, c, k * P:(k + 1) * P],
                                       AR[r, c, k, :, :], start=True, stop=True)
                    mm.then_inc(unit_done, 1)
                pe.wait_ge(proj_out, N_IN)
                pe.wait_ge(gla_o_out, 2)
                for u in range(12):
                    k, h = divmod(u, NH)
                    c, r = h // 2, slice(64 * (h % 2), 64 * (h % 2) + 64)
                    e = u // 2
                    mm = pe.matmul(PS[:, 2 * (u % 2) + e // 4, (e % 4) * P:(e % 4 + 1) * P], AR[r, c, k, 0, :], BT[r, c, k * P:(k + 1) * P],
                                   start=True, stop=True)
                    if u in (6, 7, 10, 11):
                        mm.then_inc(mrow_done, 1)
                for i, src in enumerate((BT, KT)):
                    pe.wait_ge(unit_out, 12)
                    for c in range(CT):
                        mm = pe.transpose(PS[:, 4 + i, c * P:(c + 1) * P], src[:, c, 0:P], ident)
                    mm.then_inc(bk_done, 1)

            def invert():
                pe.wait_ge(mrow_out, 4)
                for n, b in enumerate(LEVELS[1:]):
                    for k in range(NT):
                        if n == 0:
                            pe.wait_ge(ti_ready, k + 1)
                        if n >= 1:
                            pe.wait_ge(z_out, 2 * n - 1 + k)
                        for h in range(NH):
                            u = k * NH + h
                            mm = pe.matmul(PS[:, 2 * k + h // 4, (h % 4) * P:(h % 4 + 1) * P], MASKED[:, u, 0, :], TI[:, u, :],
                                           start=True, stop=True)
                        mm.then_inc(y_done, 1)
                    for k in range(NT):
                        if n == 0:
                            pe.wait_ge(bk_out, 2)
                            pe.wait_ge(tt_ready, k + 1)
                        pe.wait_ge(y_out, 2 * n + k + 1)
                        for h in range(NH):
                            u = k * NH + h
                            first = Y[:, u, :].rearrange("p (q a b) -> p q a b", a=2, b=b)[:, :, 0, :]
                            second = TT[:, u, :].rearrange("p (q a b) -> p q a b", a=2, b=b)[:, :, 1, :]
                            pe.matmul(PS[:, 4 + 2 * k, h * 64:(h + 1) * 64], TT[:, u, :], first, start=True, stop=True)
                            mm = pe.matmul(PS[:, 5 + 2 * k, h * 64:(h + 1) * 64], Y[:, u, :], second, start=True, stop=True)
                        mm.then_inc(z_done, 1)

            def chunks():
                pe.wait_ge(mix_ready, 2)
                turn_out(0, N_EARLY)
                pe.wait_ge(ot_out, 2)
                pe.wait_ge(z_out, 2 * 6)
                for k in range(NT):
                    if k:
                        pe.wait_ge(state_out, 1)
                        pe.wait_ge(chunk_o_out, 1)
                    for h in range(NH):
                        c, r = h // 2, slice(64 * (h % 2), 64 * (h % 2) + 64)
                        o, v = PS[:, 4 * (h % 2), c * 64:(c + 1) * 64], VTOK[:, k, h * 64:(h + 1) * 64]
                        mm = pe.matmul(o, MASKED[:, k * NH + h, 2, :], v, start=True, stop=k == 0)
                        if k:
                            mm = pe.matmul(o, AR[r, c, k, 0, :], STATE[r, c, :], start=False, stop=True)
                    mm.then_inc(chunk_x, 1)
                    out_product(2 * k, 1, 0)
                    pe.wait_ge(chunk_x_out, k + 1)
                    for h in range(NH):
                        mm = pe.matmul(PS[:, 1, h * 64:(h + 1) * 64], TT[:, k * NH + h, :], XU[:, 0, h * 64:(h + 1) * 64],
                                       start=True, stop=True)
                    mm.then_inc(chunk_u, 1)
                    out_product(2 * k, 1, 1)
                    pe.wait_ge(chunk_u_out, k + 1)
                    for h in range(NH):
                        c, r = h // 2, slice(64 * (h % 2), 64 * (h % 2) + 64)
                        o = PS[:, 2 + 3 * (h % 2), c * 64:(c + 1) * 64]
                        pe.matmul(o, MASKED[:, k * NH + h, 1, :], XU[:, 1, h * 64:(h + 1) * 64], start=True, stop=False)
                        mm = pe.matmul(o, MASKED[:, k * NH + h, 3, :], VTOK[:, k, h * 64:(h + 1) * 64], start=False, stop=k == 0)
                        if k:
                            mm = pe.matmul(o, AR[r, c, k, 1, :], STATE[r, c, :], start=False, stop=True)
                    mm.then_inc(chunk_o, 1)
                    if k == 0:
                        for h in range(NH):
                            r = slice(64 * (h % 2), 64 * (h % 2) + 64)
                            o, hc = PS[r, 3, (h // 2) * 64:(h // 2 + 1) * 64], slice(h * 64, (h + 1) * 64)
                            pe.matmul(o, BTOK[:, hc], XU[:, 1, hc], start=True, stop=False)
                            mm = pe.matmul(o, KTOK[:, hc], VTOK[:, 0, hc], start=False, stop=True)
                        mm.then_inc(state_done, 1)
                    for f in range(2):
                        out_product(2 * k + 1, 1, f)

            def turn_qk():
                pe.wait_ge(gg_out, 2)
                for t in range(NT):
                    pe.wait_ge(rot_ready, t + 1)
                    for b in range(4):
                        mm = pe.transpose(PS[:, 6 + t, b * P:(b + 1) * P],
                                          ROT[:, t, 2 * b:2 * b + 2, :, :], ident)
                    mm.then_inc(rot_done, 1)

            def scores(b, bank):
                for i in range(2):
                    r = slice(64 * i, 64 * i + 64)
                    pe.matmul(PS[:, bank + i, 0:256], QKT[r, 2 + b, 0:P], QKT[r, b, :], start=True, stop=True)
                    pe.matmul(PS[:, bank + i, 256:384], QKT[r, 2 + b, P:S], QKT[r, b, P:S], start=True, stop=True).then_inc(score_done, 1)

            def retention_outputs():
                pe.wait_ge(score_out, RH)
                pe.wait_ge(proj_out, 11)
                for t in range(NT):
                    for h in range(RH):
                        o = PS[:, 6 + t, h * 64:(h + 1) * 64]
                        v = [ZRET[:, j, 512 + h * 64:512 + (h + 1) * 64] for j in range(NT)]
                        if t == 0:
                            mm = pe.matmul(o, SCR[:, h, 0:P], v[0], start=True, stop=True)
                        else:
                            pe.matmul(o, SCR[:, h, P:256], v[0], start=True, stop=False)
                            mm = pe.matmul(o, SCR[:, h, 256:384], v[1], start=False, stop=True)
                    mm.then_inc(ret_o, 1)

            def level(n, bank):
                if n:
                    pe.wait_ge(gx_ready, n)
                for t in range(NT if n < 8 else 1):
                    for h in range(GH):
                        r, b = slice(64 * (h % 2), 64 * (h % 2) + 64), h // 2
                        if n == 0:
                            lhs, rhs = GQK[r, 2 + b, t * P:(t + 1) * P], GQK[r, b, t * P:(t + 1) * P]
                        elif n < 8:
                            lhs = rhs = GX[r, n % 2, b, t * P:(t + 1) * P]
                        else:
                            lhs, rhs = GX[r, n % 2, b, 0:P], GX[r, n % 2, b, P:S]
                        o = PS[:, bank + h % 2, (2 * t + b) * P:(2 * t + b + 1) * P]
                        mm = pe.matmul(o, lhs, rhs, start=True, stop=True)
                mm.then_inc(gs_done, 1)

            def gla_outputs():
                pe.wait_ge(proj_out, N_IN)
                for t in range(NT):
                    for h in range(GH):
                        o = PS[:, t, h * GDV:(h + 1) * GDV]
                        v = [ZGLA[:, j, h * GDV:(h + 1) * GDV] for j in range(NT)]
                        if t == 0:
                            mm = pe.matmul(o, GACC[:, 0, h, :], v[0], start=True, stop=True)
                        else:
                            pe.matmul(o, GACC[:, 2, h, :], v[0], start=True, stop=False)
                            mm = pe.matmul(o, GACC[:, 1, h, :], v[1], start=False, stop=True)
                    mm.then_inc(gla_o, 1)

            def turn_out(first, last):
                for t in range(NT):
                    for i, c in enumerate(OUT_CHUNKS[first:last]):
                        mm = pe.transpose(PS[:, 2 * t + i // 4, (i % 4) * P:(i % 4 + 1) * P], HN[:, t, c * P:(c + 1) * P], ident)
                    mm.then_inc(ot_done, 1)

            def out_product(i, t, f):
                n = N_IN + i // 2
                pe.wait_ge(ring_landed[n % 2], 16 * (n // 2))
                w = RING[:, n % 2, :].rearrange("p (c n) -> p c n", c=2)
                return pe.matmul(PS[:, 4 + 2 * t + f, :], OT[:, i, t * P:(t + 1) * P], w[:, i % 2, f * 512:(f + 1) * 512],
                                 start=i == 0, stop=i == DC - 1, skip_group_check=True)

            def out_group_used(g):
                pe.wait_ge(res_done, g + 1)
                pe.sem_inc(ring_free, 1)

            def project_out():
                pe.wait_ge(chunk_o_out, 2)
                for i in range(N_EARLY):
                    for t in range(NT if i >= 4 else 1):
                        for f in range(2):
                            mm = out_product(i, t, f)
                    if i in (1, 3):
                        mm.then_inc(res_done, 1)
                        out_group_used(i // 2)
                pe.wait_ge(rwkv_ready, 1)
                turn_out(N_EARLY, DC)
                pe.wait_ge(ot_out, 4)
                for i in range(N_EARLY, DC):
                    for t in range(NT):
                        for f in range(2):
                            mm = out_product(i, t, f)
                        if i == DC - 1:
                            mm.then_inc(res_done, 1)
                    if i == 5:
                        mm.then_inc(res_done, 1)
                        out_group_used(2)
                pe.wait_ge(res_done, 5)
                pe.sem_inc(ring_free, 1)

            def queries():
                kn = N_IN + N_OUT
                for g in range(PH):
                    n = kn + 1 + g
                    if g == 0:
                        pe.wait_ge(ht_ready, 8)
                        pe.wait_ge(res_out, 4)
                    if g >= 4:
                        pe.wait_ge(q_out, g - 3)
                    if g in Q_SPLIT:
                        if g == Q_SPLIT[0]:
                            pe.wait_ge(split_ready, 4)
                        split_products(SPLIT.index(n), g % 4)
                        continue
                    pe.wait_ge(ring_landed[n % 2], 16 * (n // 2))
                    w = RING[:, n % 2, :].rearrange("p (b c n) -> p b c n", b=2, c=DC)
                    for b in range(2):
                        for c in range(DC):
                            mm = pe.matmul(PS[:, g % 4, b * 256:(b + 1) * 256], w[:, b, c, :], HT[:, c, :],
                                           start=c == 0, stop=c == DC - 1)
                    mm.then_inc(q_done, 1)
                    pe.wait_ge(q_done, 1)
                    pe.sem_inc(ring_free, 1)
                for t in range(NT):
                    for m in range(4):
                        if t:
                            pe.wait_ge(sc_out, m + 1)
                        pe.wait_ge(q_out, 2 * m + 2 if t == 0 else PH)
                        for i in range(4):
                            b = 4 * m + i
                            mm = pe.matmul(PS[:, 4 + m, i * P:(i + 1) * P], QT[:, b, t * P:(t + 1) * P], KEYS[:, b, :],
                                           start=True, stop=True)
                        mm.then_inc(sc_done, 1)

            def turn_sel():
                pe.wait_ge(sel_ready, 1)
                for i, src in enumerate((I1F, I2F, GATE)):
                    for t in range(NT):
                        mm = pe.transpose(PS[:, i, t * P:(t + 1) * P], src[:, t * PH:(t + 1) * PH, :], ident)
                    mm.then_inc(sel_done, 1)

            def u_half(m, j, first, pool):
                e, f = m // 2, m % 2
                if pool:
                    pe.wait_ge(u_lo_pool, 8 * j + m + 1)
                else:
                    pe.wait_ge(u_lo, 8 * (j - POOL_BODIES) + m + 1)
                if f == 0:
                    if first and e < 2:
                        if e == 0:
                            pe.wait_ge(sc_out, 8)
                    else:
                        pe.wait_ge(u_act, 4 * j + e - 1)
                w_hi = EH[:, m % 4, :].rearrange("p (c n) -> p c n", c=4)
                w_lo = EL[:, m % 4, :].rearrange("p (c n) -> p c n", c=4)
                o = PS[:, 4 + e % 2, 0:S]
                for c in range(4):
                    d = 4 * f + c
                    pe.matmul(o, w_hi[:, c, :], HTH[:, d, :], start=d == 0, stop=False)
                    pe.matmul(o, w_hi[:, c, :], HTL[:, d, :], start=False, stop=False)
                    mm = pe.matmul(o, w_lo[:, c, :], HTH[:, d, :], start=False, stop=d == DC - 1)
                mm.then_inc(u_done, 1)

            def quad(i, q, first):
                pe.wait_ge(hot_gate, q + 1)
                pe.wait_ge(hot_pool, q + 1)
                if not first:
                    pe.wait_ge(quad_out, q - 2)
                for t in range(4):
                    mm = pe.matmul(PS[:, i, t * P:(t + 1) * P], HOT[i][:, 4 + t, :], HOT[i][:, t, :], start=True, stop=True)
                mm.then_inc(quad_done, 1)

            def v_half(m, j, first):
                e, f = m // 2, m % 2
                pe.wait_ge(v_lo, 8 * j + m + 1)
                pe.wait_ge(a_lo, 4 * j + e + 1)
                for t in range(NT):
                    o = PS[:, 2 * t + f, :]
                    a_hi_t, a_lo_t = AH[:, e % 2, t * P:(t + 1) * P], AL[:, e % 2, t * P:(t + 1) * P]
                    start = first and e == 0
                    pe.matmul(o, a_hi_t, EH[:, m % 4, :], start=start, stop=False, skip_group_check=True)
                    pe.matmul(o, a_hi_t, EL[:, m % 4, :], start=False, stop=False, skip_group_check=True)
                    mm = pe.matmul(o, a_lo_t, EH[:, m % 4, :], start=False, stop=True, skip_group_check=True)
                mm.then_inc(v_done, 1)

            with pe.Fori(0, L) as l:
                turn_h(HN, 0)
                pe.wait_ge(first_landed, 48 * l + 48)
                for g in range(7):
                    group(g)
                gk_up()
                group(7)
                lora()
                group(8)
                kk_norm()
                group(9)
                gate_and_bonus()
                group(10)
                v_tok()
                group(11, 0)
                pe.wait_ge(vtok_out, 2)
                level(0, 4)
                turn_qk()
                group(11, 1)
                pe.wait_ge(gs_out, 1)
                level(1, 4)
                pe.wait_ge(rot_out, 2)
                scores(0, 6)
                group(12, 0)
                pe.wait_ge(gs_out, 2)
                level(2, 4)
                pe.wait_ge(score_out, 2)
                level(3, 6)
                group(12, 1)
                pe.wait_ge(gs_out, 3)
                scores(1, 4)
                pe.wait_ge(gs_out, 4)
                level(4, 6)
                group(13, 0)
                pe.wait_ge(score_out, 4)
                level(5, 4)
                pe.wait_ge(gs_out, 5)
                retention_outputs()
                group(13, 1)
                pe.wait_ge(gs_out, 6)
                level(6, 4)
                group(14, 0)
                pe.wait_ge(ret_o_out, 1)
                level(7, 6)
                group(14, 1)
                pe.wait_ge(gs_out, 7)
                level(8, 4)
                units()
                invert()
                chunks()
                project_out()
                turn_h(HNF, 1)
                queries()
                for m in range(8):
                    u_half(m, 0, True, True)
                pe.sem_inc(passed, 1)
                with pe.Fori(1, POOL_BODIES) as j:
                    for m in range(8):
                        u_half(m, j, False, True)
                with pe.Fori(POOL_BODIES, SEL_BODY) as j:
                    for m in range(8):
                        u_half(m, j, False, False)
                turn_sel()
                with pe.Fori(SEL_BODY, N_BODY) as j:
                    for m in range(8):
                        u_half(m, j, False, False)
                pe.wait_ge(sel_out, 3)
                for i in range(3):
                    quad(i, i, True)
                with pe.Fori(1, 21) as q:
                    for i in range(3):
                        quad(i, 3 * q + i, False)
                quad(0, 63, False)
                for m in range(8):
                    v_half(m, 0, True)
                with pe.Fori(1, 32) as j:
                    for m in range(8):
                        v_half(m, j, False)
                pe.wait_ge(v_done, 256)
                pe.sem_inc(arrived, 1)
                pe.wait_ge(go, l + 1)

        @block.scalar
        def _(act):
            steps = [0]

            def link(ins):
                steps[0] += 1
                ins.then_inc(act_step, 1)
                act.wait_ge(act_step, steps[0])

            def sumsq_tile(k, dst, t):
                act.activation(dst[:, t, :], X[:, t, :], ACT.Square, accum_out=STAT[:, 4 * k + t:4 * k + t + 1]).then_inc(sumsq_ready, 1)

            def root(k):
                act.wait_ge(rms_ready, k + 1)
                act.activation(STAT[:, 4 * k + 2:4 * k + 4], STAT[:, 4 * k:4 * k + 2], ACT.Sqrt).then_inc(rstd_ready, 1)

            def evac_h(col, k):
                for c in range(DC):
                    if c % 4 == 0:
                        act.wait_ge(h_turned, 4 * k + c // 4 + 1)
                    ins = act.activation(HT[:, c, 0:P], PS[:, c // 4, (c % 4) * P:(c % 4 + 1) * P], ACT.Identity, scale=COLS[:, col + c:col + c + 1])
                    if c % 4 == 3:
                        ins.then_inc(ht_ready, 1)

            def w_split(i):
                n = SPLIT[i]
                if n == 1:
                    act.wait_ge(first_landed, 48 * l + 48)
                else:
                    act.wait_ge(ring_landed[n % 2], 16 * (n // 2))
                for m in range(4):
                    if i:
                        act.wait_ge(w_done, 4 * i - 3 + m)
                    act.copy(EH[:, m, :], RING[:, n % 2, m * 512:(m + 1) * 512]).then_inc(w_hi, 1)

            def w_split_in(g):
                w_split(SPLIT.index(g))

            def evac_group(g):
                act.wait_ge(*in_group_done(g))
                ps = PS[:, g % 4, :].rearrange("p (b n) -> p b n", b=2)
                if g < 6:
                    if g == 0:
                        act.wait_ge(zeros_ready, 1)
                    if g >= 2:
                        act.wait_ge(mixed, g - 1)
                    ins = act.copy(RAW[:, g % 2, :, 1:257], ps)
                elif g == 6:
                    ins = act.mul(GQK[:, 0:2, :], ps, float(GDK) ** -0.5)
                elif g == 7:
                    ins = act.copy(GQK[:, 2:4, :], ps)
                elif g < 12:
                    ins = act.copy(ZRET[:, :, (g - 8) * 256:(g - 7) * 256], ps)
                else:
                    ins = act.copy(ZGLA[:, :, (g - 12) * 256:(g - 11) * 256], ps)
                ins.then_inc(proj_out, 1)

            def keys_out():
                n = N_IN + N_OUT
                act.wait_ge(ring_landed[n % 2], 16 * (n // 2))
                link(act.copy(KEYS, RING[:, n % 2, :].rearrange("p (b n) -> p b n", b=16)))
                act.sem_inc(keys_copied, 1)

            def u_split(m, j, first):
                if m % 4 == 0:
                    act.wait_ge(uring[m // 4], 16 * (j + 1))
                if first and m < 4:
                    act.wait_ge(w_done, 4 * len(SPLIT) - 3 + m)
                else:
                    act.wait_ge(u_done, 8 * j + m - 3)
                act.copy(EH[:, m % 4, :], RING[:, m // 4, (m % 4) * 512:(m % 4 + 1) * 512]).then_inc(u_hi, 1)

            def u_gelu(e, j):
                act.wait_ge(u_done, 8 * j + 2 * e + 2)
                act.activation(ACTS[:, 4 * j + e, :], PS[:, 4 + e % 2, 0:S], ACT.Gelu).then_inc(u_act, 1)

            def u_body(j, first):
                for m in range(8):
                    if not first or m >= 4:
                        u_split(m, j, first)
                    if m == 1 and not first:
                        u_gelu(-1, j)
                    if m >= 3 and m % 2:
                        u_gelu(m // 2 - 1, j)

            def gate_rows(i, q, first):
                own = range(N_EQ[i] - 4, 3)
                if not first:
                    act.wait_ge(quad_done, q - 2)
                for t in own:
                    ins = act.activation(HOT[i][:, 4 + t, :], iota, ACT.Abs, bias=NEGI1[:, bass.ds(4 * q + t, 1)])
                ins.then_inc(hot_dist, 1)
                act.wait_ge(hot_eq, q + 1)
                for t in range(own[0]):
                    act.activation(HOT[i][:, 4 + t, :], HOT[i][:, 4 + t, :], ACT.Identity, scale=GATET[:, bass.ds(4 * q + t, 1)])
                act.wait_ge(hot_dist, q + 1)
                for t in own:
                    ins = act.activation(HOT[i][:, 4 + t, :], HOT[i][:, 4 + t, :], ACT.Relu, bias=GATET[:, bass.ds(4 * q + t, 1)],
                                         scale=NEGATE[:, bass.ds(4 * q + t, 1)])
                ins.then_inc(hot_gate, 1)

            def v_split(m, j, first):
                if m % 4 == 0:
                    act.wait_ge(vring[m // 4], 16 * (j + 1))
                if first and m < 4:
                    if m == 0:
                        act.wait_ge(u_done, 256)
                else:
                    act.wait_ge(v_done, 8 * j + m - 3)
                act.copy(EH[:, m % 4, :], RING[:, m // 4, (m % 4) * 512:(m % 4 + 1) * 512]).then_inc(v_hi, 1)

            def a_split(e, j, first):
                if first and e < 2:
                    if e == 0:
                        act.wait_ge(quad_out, 64)
                else:
                    act.wait_ge(v_done, 8 * j + 2 * e - 2)
                act.copy(AH[:, e % 2, :], ACTS[:, 4 * j + e, :]).then_inc(a_hi, 1)

            for t in range(NT):
                act.wait_ge(x_landed[t], 16)
                sumsq_tile(0, HN, t)
            root(0)
            with act.Fori(0, L) as l:
                steps[0] = 0
                act.wait_ge(first_landed, 48 * l + 48)
                evac_h(C_MIX, 0)
                w_split(0)
                act.wait_ge(ht_ready, 4)
                act.copy(HTH[:, :, :], HT[:, :, :]).then_inc(split_ready, 1)
                for g in range(7):
                    evac_group(g)
                    if g < 6:
                        w_split_in(g + 2)
                act.wait_ge(mixed, 6)
                act.activation(FM[0:64, 0, :], FM[0:64, 0, :], ACT.Tanh).then_inc(tanh_ready, 1)
                act.activation(FM[:, 1, :], FM[:, 1, :], ACT.Sigmoid).then_inc(sig_ready, 1)
                act.wait_ge(gk_out, 1)
                link(act.activation(GE[:, 0, :, :], GB[:, :, :], ACT.Abs))
                link(act.activation(GE[:, 0, :, :], GE[:, 0, :, :], ACT.Exp, scale=-1.0))
                act.activation(GE[:, 0, :, :], GE[:, 0, :, :], ACT.Ln, bias=1.0).then_inc(gln_ready, 1)
                w_split_in(8)
                evac_group(7)
                for c in range(CT):
                    act.wait_ge(lora_done, CT)
                    o = slice(c % 2 * 256, c % 2 * 256 + 256)
                    act.activation(SIGA[:, c, 0, :], PS[:, 4 + c // 2, o], ACT.Sigmoid, bias=COLS[:, C_WB + c:C_WB + c + 1]).then_inc(sig_ready, 1)
                    act.activation(SIGA[:, c, 1, :], PS[:, 6 + c // 2, o], ACT.Sigmoid, bias=COLS[:, C_AB + c:C_AB + c + 1]).then_inc(sig_ready, 1)
                w_split_in(9)
                evac_group(8)
                act.wait_ge(kkmax_ready, 1)
                act.activation(KKN[:, :, :], KKN[:, :, :], ACT.Sqrt).then_inc(kksqrt_ready, 1)
                act.wait_ge(cum_ready, 1)
                for c in range(CT):
                    for k in range(NT):
                        n = 16 + 2 * (c * NT + k)
                        act.activation(E1[:, c, k, :], CUM[:, c, k, :], ACT.Exp, bias=STAT[:, n:n + 1])
                        act.activation(E2[:, c, k * P:(k + 1) * P], CUM[:, c, k, 1:129], ACT.Exp, scale=-1.0, bias=STAT[:, n + 1:n + 2])
                act.activation(STAT[:, 28:31], CUM[:, :, 1, 64], ACT.Exp).then_inc(exp_ready, 1)
                w_split_in(10)
                evac_group(9)
                for i in range(NT):
                    act.wait_ge(gg_done, i + 1)
                    act.copy(GG[:, i, :], PS[:, 6 + i, 0:390]).then_inc(gg_out, 1)
                w_split_in(11)
                evac_group(10)
                act.wait_ge(ab_ready, 1)
                for i in range(NT):
                    act.wait_ge(vtok_done, i + 1)
                    act.copy(VTOK[:, i, :], PS[:, 4 + i, 0:384]).then_inc(vtok_out, 1)
                def level_exp(n):
                    act.wait_ge(gd_ready, n)
                    act.activation(GE[:, n % 2, :, :], GE[:, n % 2, :, :], ACT.Exp).then_inc(ge_ready, 1)

                level_exp(1)
                for t in range(NT):
                    act.wait_ge(rot_done, t + 1)
                    act.copy(QKT[:, :, t * P:(t + 1) * P], PS[:, 6 + t, :].rearrange("p (b n) -> p b n", b=4)).then_inc(rot_out, 1)
                level_exp(2)
                w_split_in(12)
                level_exp(3)
                evac_group(11)
                for n in range(4, 8):
                    level_exp(n)
                w_split_in(13)
                evac_group(12)
                level_exp(8)
                act.wait_ge(ret_o, 2)
                act.copy(HN[:, :, 0:256], PS[:, 6:8, 0:256]).then_inc(ret_o_out, 1)
                w_split_in(14)
                evac_group(13)
                evac_group(14)
                for t in range(NT):
                    act.wait_ge(gla_o, t + 1)
                    act.copy(HN[:, t, 640:1024], PS[:, t, 0:384]).then_inc(gla_o_out, 1)
                for i in range(2):
                    act.wait_ge(bk_done, i + 1)
                    act.copy((BTOK, KTOK)[i], PS[:, 4 + i, 0:384]).then_inc(bk_out, 1)
                act.wait_ge(ret_o_out, 1)
                act.wait_ge(gla_o_out, 2)
                for t in range(NT):
                    for h in range(RH):
                        act.activation(RSQ[:, t, h * 64:(h + 1) * 64], HN[:, t, h * 64:(h + 1) * 64], ACT.Square, accum_out=STAT[:, 64 + 4 * t + h:65 + 4 * t + h])
                    for h in range(GH):
                        o = 640 + h * GDV
                        ins = act.activation(GSQ[:, t, o - 640:o - 640 + GDV], HN[:, t, o:o + GDV], ACT.Square, accum_out=STAT[:, 72 + 4 * t + h:73 + 4 * t + h])
                ins.then_inc(sq_ready, 1)
                act.wait_ge(proj_out, N_IN)
                act.activation(ZRET[:, :, 768:1024], ZRET[:, :, 768:1024], ACT.Silu).then_inc(silu_ready, 1)
                act.activation(ZGLA[:, :, 384:768], ZGLA[:, :, 384:768], ACT.Silu).then_inc(silu_ready, 1)
                act.wait_ge(hvar_ready, 1)
                act.activation(STAT[:, 80:96], STAT[:, 64:80], ACT.Sqrt).then_inc(hsd_ready, 1)
                for t in range(NT):
                    act.wait_ge(ot_done, t + 1)
                    act.copy(OT[:, 0:4, t * P:(t + 1) * P], PS[:, 2 * t, :].rearrange("p (c n) -> p c n", c=4))
                    act.copy(OT[:, 4, t * P:(t + 1) * P], PS[:, 2 * t + 1, 0:P]).then_inc(ot_out, 1)
                act.wait_ge(var_ready, 1)
                act.activation(STAT[:, 44:56], STAT[:, 32:44], ACT.Sqrt).then_inc(sd_ready, 1)
                for t in range(NT):
                    act.wait_ge(ot_done, NT + t + 1)
                    act.copy(OT[:, N_EARLY:DC, t * P:(t + 1) * P], PS[:, 2 * t, 0:384].rearrange("p (c n) -> p c n", c=3)).then_inc(ot_out, 1)
                for t in range(NT):
                    act.wait_ge(res_out, 2 * t + 2)
                    sumsq_tile(1, HNF, t)
                root(1)
                keys_out()
                evac_h(C_FFN, 1)
                act.wait_ge(ht_ready, 8)
                act.copy(HTH[:, :, :], HT[:, :, :]).then_inc(split_ready, 1)
                w_split(len(IN_SPLIT))
                for g in range(PH):
                    act.wait_ge(*q_group_done(g))
                    act.copy(QT[:, 2 * g:2 * g + 2, :], PS[:, g % 4, :].rearrange("p (b n) -> p b n", b=2)).then_inc(q_out, 1)
                    if g + 2 < PH:
                        w_split(len(IN_SPLIT) + g + 1)
                for t in range(NT):
                    if t == NT - 1:
                        for m in range(4):
                            u_split(m, 0, True)
                    for m in range(4):
                        act.wait_ge(sc_done, 4 * t + m + 1)
                        act.copy(SC[:, 16 * t + 4 * m:16 * t + 4 * m + 4, :], PS[:, 4 + m, :].rearrange("p (b n) -> p b n", b=4)).then_inc(sc_out, 1)
                u_body(0, True)
                act.sem_inc(passed, 1)
                with act.Fori(1, EXP_BODY) as j:
                    u_body(j, False)
                act.wait_ge(gdiff_ready, 1)
                act.activation(GATE[:, :, :], GATE[:, :, :], ACT.Exp).then_inc(gexp_ready, 1)
                u_body(EXP_BODY, False)
                with act.Fori(EXP_BODY + 1, SEL_BODY) as j:
                    u_body(j, False)
                pair = IDXQ[:, :, :].rearrange("p q (m t) -> p m q t", m=2)
                for i in range(3):
                    act.wait_ge(sel_done, i + 1)
                    src = PS[:, i, 0:S]
                    if i == 0:
                        act.mul(NEGI1[:, :], src, -1.0)
                    if i == 2:
                        act.mul(NEGATE[:, :], src, -1.0)
                    if i < 2:
                        act.copy(pair[:, 1 - i], src.rearrange("p (q t) -> p q t", t=4)).then_inc(sel_out, 1)
                    else:
                        act.copy(GATET[:, :], src).then_inc(sel_out, 1)
                with act.Fori(SEL_BODY, N_BODY) as j:
                    u_body(j, False)
                for i in range(3):
                    gate_rows(i, i, True)
                u_gelu(-1, N_BODY)
                with act.Fori(1, 21) as q:
                    for i in range(3):
                        gate_rows(i, 3 * q + i, False)
                gate_rows(0, 63, False)
                for m in range(4):
                    v_split(m, 0, True)
                for e in range(2):
                    a_split(e, 0, True)
                for m in range(4, 8):
                    if m % 2 == 0:
                        a_split(m // 2, 0, True)
                    v_split(m, 0, True)
                with act.Fori(1, 32) as j:
                    for m in range(8):
                        if m % 2 == 0:
                            a_split(m // 2, j, False)
                        v_split(m, j, False)
                act.wait_ge(v_hi, 256)
                for t in range(NT):
                    act.wait_ge(peer_out, 3 + t)
                    if t == NT - 1:
                        act.sem_inc(arrived, 1)
                    sumsq_tile(0, HN, t)
                root(0)
                act.wait_ge(go, l + 1)

        @block.vector
        def _(dve):
            dve.wait_ge(const_landed, 16)
            for t in range(NT):
                dve.wait_ge(x_landed[t], 16)
            steps = [0]

            def link(ins):
                steps[0] += 1
                ins.then_inc(dve_step, 1)
                dve.wait_ge(dve_step, steps[0])

            def norm_rows(k, dst):
                dve.wait_ge(sumsq_ready, NT * (k + 1))
                a = 4 * k
                dve.tensor_scalar(STAT[:, a:a + 2], STAT[:, a:a + 2], 1.0 / D, NORM_EPS, ALU.mult, ALU.add).then_inc(rms_ready, 1)
                dve.wait_ge(rstd_ready, k + 1)
                dve.reciprocal(STAT[:, a:a + 2], STAT[:, a + 2:a + 4]).then_inc(rstd_turned, 1)
                dve.wait_ge(rstd_turned, k + 1)
                for t in range(NT):
                    dve.tensor_scalar(dst[:, t, :], X[:, t, :], STAT[:, a + t:a + t + 1], None, ALU.mult).then_inc(h_ready, 1)

            def evac_h(col, k):
                for c in range(DC):
                    if c % 4 == 0:
                        dve.wait_ge(h_turned, 4 * k + 3 + c // 4)
                    ins = dve.tensor_scalar(HT[:, c, P:S], PS[:, 2 + c // 4, (c % 4) * P:(c % 4 + 1) * P], COLS[:, col + c:col + c + 1], None, ALU.mult)
                    if c % 4 == 3:
                        ins.then_inc(ht_ready, 1)

            def h_lows(n):
                dve.wait_ge(split_ready, n)
                dve.tensor_tensor(HTL[:, :, :], HT[:, :, :], HTH[:, :, :].bitcast(F32), ALU.subtract).then_inc(split_ready, 1)

            def w_lows(i):
                for m in range(4):
                    dve.wait_ge(w_hi, 4 * i + m + 1)
                    dve.tensor_tensor(EL[:, m, :], RING[:, SPLIT[i] % 2, m * 512:(m + 1) * 512], EH[:, m, :].bitcast(F32), ALU.subtract).then_inc(w_lo, 1)

            def mix(g):
                dve.wait_ge(proj_out, g + 1)
                r = RAW[:, g % 2, :, :]
                link(dve.tensor_tensor(TMP[:, 0:2, :], r[:, :, 0:256], r[:, :, 1:257], ALU.subtract))
                for b in range(2):
                    n = 2 * g + b
                    if n < 11:
                        ins = dve.scalar_tensor_tensor(FM[:, n, :], TMP[:, b, :], COLS[:, C_MU + n:C_MU + n + 1], r[:, b, 1:257], ALU.mult, ALU.add)
                    else:
                        ins = dve.tensor_copy(FM[:, n, :], r[:, b, 1:257])
                    link(ins)
                dve.sem_inc(mixed, 1)

            def col(n, c):
                return COLS[:, n + c:n + c + 1]

            def rwkv_prep():
                dve.wait_ge(params_landed, 48)
                K, R = FM[:, 2:5, :], FM[:, 5:8, :]
                for c in range(CT):
                    ins = dve.tensor_scalar(BT[:, c, :], K[:, c, :], col(C_KK, c), None, ALU.mult)
                link(ins)
                dve.tensor_tensor(TMP[:, :, :], BT[:, :, :], BT[:, :, :], ALU.mult).then_inc(kksq_ready, 1)
                gla_gates()
                dve.wait_ge(sig_ready, 7)
                link(dve.tensor_scalar(E2[:, :, :], SIGA[:, :, 0, :], LOG_DECAY_SCALE, None, ALU.mult))
                dve.memset(CUM[:, :, :, 0:1], 0.0)
                for c in range(CT):
                    for k in range(NT):
                        ins = dve.tensor_tensor_scan(CUM[:, c, k, 1:129], XC[:, X_ONES:X_ONES + 1].broadcast_to([P, P]), E2[:, c, k * P:(k + 1) * P], 0.0, ALU.mult, ALU.add)
                link(ins)
                for c in range(CT):
                    for k in range(NT):
                        n = 16 + 2 * (c * NT + k)
                        dve.tensor_scalar(STAT[:, n:n + 1], CUM[:, c, k, 64:65], -1.0, None, ALU.mult)
                        ins = dve.tensor_copy(STAT[:, n + 1:n + 2], CUM[:, c, k, 64:65])
                link(ins)
                dve.sem_inc(cum_ready, 1)
                for c in range(CT):
                    ins = dve.tensor_scalar(KT[:, c, :], SIGA[:, c, 1, :], 1.0, col(C_KA, c), ALU.subtract, ALU.mult)
                link(ins)
                link(dve.scalar_tensor_tensor(KT[:, :, :], KT[:, :, :], 1.0, K, ALU.add, ALU.mult))
                dve.wait_ge(kknorm_done, 1)
                dve.tensor_scalar(KKN[:, 0:2, :], PS[:, 7, :].rearrange("p (c n) -> p c n", c=2), 1e-24, None, ALU.max)
                link(dve.tensor_scalar(KKN[:, 2, :], PS[:, 4, 0:256], 1e-24, None, ALU.max))
                dve.sem_inc(kkmax_ready, 1)
                for c in range(CT):
                    ins = dve.scalar_tensor_tensor(TMP[:, c, :], R[:, c, :], col(C_RK, c), KT[:, c, :], ALU.mult, ALU.mult)
                link(ins)
                dve.sem_inc(rk_ready, 1)
                dve.wait_ge(kksqrt_ready, 1)
                link(dve.reciprocal(KKN[:, :, :], KKN[:, :, :]))
                link(dve.tensor_tensor(KKN[:, :, :], KKN[:, :, :], BT[:, :, :], ALU.mult))
                dve.wait_ge(exp_ready, 1)
                for c in range(CT):
                    for k in range(NT):
                        s = slice(k * P, (k + 1) * P)
                        dve.scalar_tensor_tensor(AR[:, c, k, 0, :], KKN[:, c, s], -1.0, E1[:, c, k, 0:128], ALU.mult, ALU.mult)
                        dve.tensor_tensor(AR[:, c, k, 1, :], R[:, c, s], E1[:, c, k, 1:129], ALU.mult)
                link(dve.tensor_tensor(BT[:, :, :], KKN[:, :, :], SIGA[:, :, 1, :], ALU.mult))
                dve.tensor_tensor(BT[:, :, :], BT[:, :, :], E2[:, :, :], ALU.mult)
                link(dve.tensor_tensor(KT[:, :, :], KT[:, :, :], E2[:, :, :], ALU.mult))
                link(dve.tensor_tensor(STAT[:, 28:31], STAT[:, 28:31], E1[:, :, 0, 128], ALU.mult))
                dve.sem_inc(ab_ready, 1)

            def gla_gates():
                dve.wait_ge(gk_done, 1)
                for b in range(2):
                    ins = dve.tensor_scalar(GB[:, b, :], PS[:, 5, b * 256:(b + 1) * 256], col(C_GB, b), None, ALU.add)
                link(ins)
                dve.sem_inc(gk_out, 1)
                dve.wait_ge(gln_ready, 1)
                link(dve.scalar_tensor_tensor(GX[:, 0, :, :], GB[:, :, :], 0.0, GE[:, 0, :, :], ALU.min, ALU.subtract))
                link(dve.tensor_scalar(GX[:, 0, :, :], GX[:, 0, :, :], 1.0 / 16.0, None, ALU.mult))
                for b in range(2):
                    ins = dve.tensor_tensor_scan(GB[:, b, :], XC[:, X_ONES:X_ONES + 1].broadcast_to([P, S]), GX[:, 0, b, :], 0.0, ALU.mult, ALU.add)
                ins.then_inc(gcum_ready, 1)

            def rwkv_units():
                mask2 = XC[:, X_MASK2:X_MASK2 + 256].unsqueeze(1).broadcast_to([P, 2, 256])
                up1 = XC[:, X_UP:X_UP + P].unsqueeze(1).broadcast_to([P, NH, P])
                id6 = ident.unsqueeze(1).broadcast_to([P, NH, P])
                halves = [slice(k * NH, (k + 1) * NH) for k in range(NT)]

                def start_tt(k):
                    dve.wait_ge(unit_out, (k + 1) * NH)
                    link(dve.tensor_tensor(TT[:, halves[k], :], MASKED[:, halves[k], 0, :], up1, ALU.mult))
                    dve.tensor_tensor(TT[:, halves[k], :], TT[:, halves[k], :], id6, ALU.add).then_inc(tt_ready, 1)

                for u in range(12):
                    dve.wait_ge(unit_done, u + 1)
                    dve.tensor_tensor(MASKED[:, u, :, :].rearrange("p (a b) n -> p a (b n)", a=2), PS[:, 4 + u % 4, :].rearrange("p (a n) -> p a n", a=2), mask2,
                                      ALU.mult).then_inc(unit_out, 1)
                    if u == 8:
                        start_tt(0)
                low1 = XC[:, X_LOW:X_LOW + P].unsqueeze(1).broadcast_to([P, 4, P])
                ti_pairs = TI.rearrange("p (e r) n -> p r e n", r=2)
                for m in range(4):
                    n, e0, r = (4, 0, m) if m < 2 else (2, 4, m - 2)
                    dve.wait_ge(mrow_done, m + 1)
                    dve.tensor_tensor(ti_pairs[:, r, e0:e0 + n, :], PS[:, 2 * r + e0 // 4, 0:n * P].rearrange("p (u n) -> p u n", u=n), low1[:, 0:n, :],
                                      ALU.mult).then_inc(mrow_out, 1)
                dve.wait_ge(mrow_out, 4)
                for k in range(NT):
                    dve.tensor_tensor(TI[:, halves[k], :], TI[:, halves[k], :], id6, ALU.add).then_inc(ti_ready, 1)
                start_tt(1)
                for n, b in enumerate(LEVELS[1:]):
                    if n == 1:
                        dve.wait_ge(sq_ready, 1)
                        dve.tensor_scalar(STAT[:, 64:72], STAT[:, 64:72], 1.0 / RDK, HEAD_EPS, ALU.mult, ALU.add)
                        dve.tensor_scalar(STAT[:, 72:80], STAT[:, 72:80], 1.0 / GDV, HEAD_EPS, ALU.mult, ALU.add).then_inc(hvar_ready, 1)
                    if n == 2:
                        dve.wait_ge(hsd_ready, 1)
                        dve.reciprocal(STAT[:, 80:96], STAT[:, 80:96]).then_inc(hrstd_ready, 1)
                    low = XC[:, X_LOW + P * (n + 1):X_LOW + P * (n + 2)]
                    for k in range(NT):
                        dve.wait_ge(y_done, 2 * n + k + 1)
                        u0 = k * NH
                        dve.tensor_tensor(Y[:, u0:u0 + NH, :], PS[:, 2 * k:2 * k + 2, :].rearrange("p a n -> p (a n)")[:, 0:768].rearrange("p (u n) -> p u n", u=NH),
                                          low.unsqueeze(1).broadcast_to([P, NH, P]), ALU.mult).then_inc(y_out, 1)
                    for k in range(NT):
                        dve.wait_ge(z_done, 2 * n + k + 1)
                        u0 = k * NH
                        for i, dst in enumerate((TI, TT)):
                            z = PS[:, 4 + 2 * k + i, 0:384]
                            if b < 64:
                                half = dst[:, u0:u0 + NH, :].rearrange("p u (q a b) -> p (u q) a b", a=2, b=b)[:, :, i, :]
                                zz = z.rearrange("p (m b) -> p m b", b=b)
                            else:
                                half = dst[:, u0:u0 + NH, 64 * i:64 * i + 64]
                                zz = z.rearrange("p (m b) -> p m b", b=64)
                            ins = dve.tensor_tensor(half, half, zz, ALU.add)
                        ins.then_inc(z_out, 1)

            def rwkv_chunks():
                for k in range(NT):
                    dve.wait_ge(chunk_x, k + 1)
                    for r in range(2):
                        ins = dve.tensor_copy(XU[:, 0, :].rearrange("p (c r n) -> p r c n", c=CT, r=2)[:, r], PS[:, 4 * r, 0:192].rearrange("p (c n) -> p c n", c=CT))
                    ins.then_inc(chunk_x_out, 1)
                    dve.wait_ge(chunk_u, k + 1)
                    dve.tensor_copy(XU[:, 1, :], PS[:, 1, 0:384]).then_inc(chunk_u_out, 1)
                    if k == 0:
                        dve.wait_ge(state_done, 1)
                        dve.tensor_tensor(STATE[:, :, :], PS[:, 3, 0:192].rearrange("p (c n) -> p c n", c=CT),
                                          STAT[:, 28:31].unsqueeze(2).broadcast_to([P, CT, 64]), ALU.mult).then_inc(state_out, 1)
                    dve.wait_ge(chunk_o, k + 1)
                    for r in range(2):
                        ins = dve.tensor_copy(HN[:, k, 256:640].rearrange("p (c r n) -> p r c n", c=CT, r=2)[:, r], PS[:, 2 + 3 * r, 0:192].rearrange("p (c n) -> p c n", c=CT))
                    ins.then_inc(chunk_o_out, 1)

            def rwkv_out():
                dve.wait_ge(chunk_o_out, 2)
                O = HN[:, :, 256:640]
                for t in range(NT):
                    ins = dve.tensor_reduce(STAT[:, 32 + 6 * t:38 + 6 * t], O[:, t, :].rearrange("p (h n) -> p h n", h=NH), AX.X, ALU.add)
                link(ins)
                link(dve.tensor_scalar(STAT[:, 32:44], STAT[:, 32:44], 1.0 / 64, None, ALU.mult))
                for t in range(NT):
                    o = O[:, t, :].rearrange("p (h n) -> p h n", h=NH)
                    ins = dve.tensor_tensor(o, o, STAT[:, 32 + 6 * t:38 + 6 * t].unsqueeze(2).broadcast_to([P, NH, 64]), ALU.subtract)
                link(ins)
                link(dve.tensor_tensor(XB[:, :, :], O, O, ALU.mult))
                link(dve.tensor_reduce(STAT[:, 32:44], XB[:, :, :].rearrange("p t (h n) -> p (t h) n", h=NH), AX.X, ALU.add))
                link(dve.tensor_scalar(STAT[:, 32:44], STAT[:, 32:44], 1.0 / 64, GN_EPS, ALU.mult, ALU.add))
                dve.sem_inc(var_ready, 1)
                dve.wait_ge(sd_ready, 1)
                link(dve.reciprocal(STAT[:, 44:56], STAT[:, 44:56]))
                for t in range(NT):
                    o = O[:, t, :].rearrange("p (h n) -> p h n", h=NH)
                    ins = dve.tensor_tensor(o, o, STAT[:, 44 + 6 * t:50 + 6 * t].unsqueeze(2).broadcast_to([P, NH, 64]), ALU.mult)
                link(ins)
                dve.wait_ge(rwkv_affine, 1)
                link(dve.tensor_tensor(O, O, GG[:, :, 0:384], ALU.mult))
                link(dve.tensor_tensor(O, O, GBIAS, ALU.add))

            def rotate():
                dve.wait_ge(proj_out, 10)
                for t in range(NT):
                    z = ZRET[:, t, 0:512].rearrange("p (g h c) -> p g h c", g=8, h=2)
                    rope = XC[:, X_ROPE + 64 * t:X_ROPE + 64 * (t + 1)].rearrange("p (a c) -> p a c", a=2)
                    cos, sin = (rope[:, a, :].unsqueeze(1).broadcast_to([P, 8, 32]) for a in range(2))
                    tmp = RTMP[:, t, :].rearrange("p (g c) -> p g c", g=8)
                    dve.tensor_tensor(ROT[:, t, :, 0, :], z[:, :, 0, :], cos, ALU.mult)
                    link(dve.tensor_tensor(tmp, z[:, :, 1, :], sin, ALU.mult))
                    link(dve.tensor_tensor(ROT[:, t, :, 0, :], ROT[:, t, :, 0, :], tmp, ALU.subtract))
                    dve.tensor_tensor(ROT[:, t, :, 1, :], z[:, :, 0, :], sin, ALU.mult)
                    link(dve.tensor_tensor(tmp, z[:, :, 1, :], cos, ALU.mult))
                    link(dve.tensor_tensor(ROT[:, t, :, 1, :], ROT[:, t, :, 1, :], tmp, ALU.add))
                    dve.sem_inc(rot_ready, 1)

            def decayed(b, bank):
                for i in range(2):
                    h = 2 * b + i
                    dm = XC[:, X_DM + 256 * h:X_DM + 256 * (h + 1)]
                    dve.wait_ge(score_done, h + 1)
                    dve.tensor_tensor(SCR[:, h, 0:256], PS[:, bank + i, 0:256], dm, ALU.mult)
                    dve.tensor_tensor(SCR[:, h, 256:384], PS[:, bank + i, 256:384], dm[:, 0:P], ALU.mult).then_inc(score_out, 1)

            gacc = GACC.rearrange("p t (c r) n -> p t r c n", r=2)
            masks = [ident] + [XC[:, X_UP + P * n:X_UP + P * (n + 1)] for n in range(7)]

            def level(n, bank):
                dve.wait_ge(gs_done, n + 1)
                if 1 <= n < 8:
                    dve.wait_ge(gs_out, n)
                for r in range(2):
                    if n < 8:
                        mask = masks[n].bitcast(U32).unsqueeze(1).unsqueeze(1).broadcast_to([P, NT, 2, P])
                        ins = dve.copy_predicated(gacc[:, 0:2, r], mask, PS[:, bank + r, :].rearrange("p (t c n) -> p t c n", t=NT, c=2))
                    else:
                        ins = dve.tensor_copy(gacc[:, 2, r], PS[:, bank + r, 0:256].rearrange("p (c n) -> p c n", c=2))
                ins.then_inc(gs_out, 1)

            def topk():
                for t in range(NT):
                    dve.wait_ge(sc_out, 4 * t + 4)
                    us = range(16 * t, 16 * t + 16)
                    for u in us:
                        ins = dve.max(VAL[:, u, 0:8], SC[:, u, :])
                    link(ins)
                    for u in us:
                        dve.max_index(IDX[:, u, 0:8].bitcast(U32), VAL[:, u, 0:8], SC[:, u, :])
                        ins = dve.match_replace(SC2[:, u % 16, :], VAL[:, u, 0:8], SC[:, u, :], NEG)
                    link(ins)
                    for u in us:
                        ins = dve.max(VAL[:, u, 8:16], SC2[:, u % 16, :])
                    link(ins)
                    for u in us:
                        ins = dve.max_index(IDX[:, u, 8:16].bitcast(U32), VAL[:, u, 8:16], SC2[:, u % 16, :])
                    link(ins)
                link(dve.tensor_copy(IDXF[:, :, :], IDX[:, :, :].bitcast(U32)))
                v = VAL[:, :, :].rearrange("p (u h) n -> p u h n", h=2)
                x = IDXF[:, :, :].rearrange("p (u h) n -> p u h n", h=2)
                o = 0
                for i in range(8):
                    n = CAND_ROWS[i]
                    dve.tensor_tensor(CAND[:, :, o:o + n], v[:, :, 0, i:i + 1].broadcast_to([P, 16, n]), v[:, :, 1, 0:n], ALU.add)
                    dve.scalar_tensor_tensor(CIDX[:, :, o:o + n], x[:, :, 0, i:i + 1].broadcast_to([P, 16, n]), float(NKEYS), x[:, :, 1, 0:n], ALU.mult, ALU.add)
                    o += n
                dve.tensor_tensor(CAND[:, :, o:o + 8], v[:, :, 0, 8:16], v[:, :, 1, 0:1].broadcast_to([P, 16, 8]), ALU.add)
                link(dve.scalar_tensor_tensor(CIDX[:, :, o:o + 8], x[:, :, 0, 8:16], float(NKEYS), x[:, :, 1, 0:1].broadcast_to([P, 16, 8]), ALU.mult, ALU.add))
                for u in range(16):
                    ins = dve.max(TOPV[:, u, 0:8], CAND[:, u, :])
                link(ins)
                for u in range(16):
                    dve.max_index(POS[:, u, 0:8].bitcast(U32), TOPV[:, u, 0:8], CAND[:, u, :])
                    ins = dve.match_replace(CAND2[:, u, :], TOPV[:, u, 0:8], CAND[:, u, :], NEG)
                link(ins)
                for u in range(16):
                    ins = dve.max(TOPV[:, u, 8:16], CAND2[:, u, :])
                link(ins)
                for u in range(16):
                    ins = dve.max_index(POS[:, u, 8:16].bitcast(U32), TOPV[:, u, 8:16], CAND2[:, u, :])
                link(ins)
                link(dve.tensor_tensor(GATE[:, :, :], TOPV[:, :, :], TOPV[:, :, 0:1].broadcast_to([P, 16, 16]), ALU.subtract))
                dve.sem_inc(gdiff_ready, 1)
                link(dve.tensor_copy(POSF[:, :, :], POS[:, :, :].bitcast(U32)))
                cpos = iota[:, 0:NC].unsqueeze(1).broadcast_to([P, 16, NC])
                for u in range(16):
                    e = EQ[:, u % 2, :, :]
                    link(dve.tensor_tensor(e, POSF[:, u, :].unsqueeze(2).broadcast_to([P, 16, NC]), cpos, ALU.is_equal))
                    link(dve.tensor_tensor(e, e, CIDX[:, u, :].unsqueeze(1).broadcast_to([P, 16, NC]), ALU.mult))
                    ins = dve.tensor_reduce(EIDX[:, u, :], e, AX.X, ALU.add)
                link(ins)
                link(dve.tensor_copy(POS[:, :, :].bitcast(I32), EIDX[:, :, :]))
                dve.tensor_scalar(I1F[:, :, :].bitcast(I32), POS[:, :, :].bitcast(I32), 7, None, ALU.logical_shift_right)
                link(dve.tensor_scalar(I2F[:, :, :].bitcast(I32), POS[:, :, :].bitcast(I32), NKEYS - 1, None, ALU.bitwise_and))
                dve.tensor_copy(I1F[:, :, :], I1F[:, :, :].bitcast(I32))
                dve.tensor_copy(I2F[:, :, :], I2F[:, :, :].bitcast(I32))

            def gates():
                dve.wait_ge(gexp_ready, 1)
                link(dve.tensor_reduce(STAT[:, 16:32], GATE[:, :, :], AX.X, ALU.add))
                link(dve.reciprocal(STAT[:, 32:48], STAT[:, 16:32]))
                link(dve.tensor_tensor(GATE[:, :, :], GATE[:, :, :], STAT[:, 32:48].unsqueeze(2).broadcast_to([P, 16, 16]), ALU.mult))
                dve.sem_inc(sel_ready, 1)

            def u_lows(m, j):
                dve.wait_ge(u_hi, 8 * j + m + 1)
                dve.tensor_tensor(EL[:, m % 4, :], RING[:, m // 4, (m % 4) * 512:(m % 4 + 1) * 512], EH[:, m % 4, :].bitcast(F32), ALU.subtract).then_inc(u_lo, 1)

            def v_lows(m, j):
                dve.wait_ge(v_hi, 8 * j + m + 1)
                dve.tensor_tensor(EL[:, m % 4, :], RING[:, m // 4, (m % 4) * 512:(m % 4 + 1) * 512], EH[:, m % 4, :].bitcast(F32), ALU.subtract).then_inc(v_lo, 1)

            def a_lows(e, j):
                dve.wait_ge(a_hi, 4 * j + e + 1)
                dve.tensor_tensor(AL[:, e % 2, :], ACTS[:, 4 * j + e, :], AH[:, e % 2, :].bitcast(F32), ALU.subtract).then_inc(a_lo, 1)

            def hots(i, q, first):
                n = N_EQ[i]
                if not first:
                    dve.wait_ge(quad_done, q - 2)
                dve.tensor_tensor(HOT[i][:, 0:n, :], iota.unsqueeze(1).broadcast_to([P, n, P]),
                                  IDXQ[:, bass.ds(q, 1), 0:n].rearrange("p a m -> p (a m)").unsqueeze(2).broadcast_to([P, n, P]), ALU.is_equal).then_inc(hot_eq, 1)

            def gated(i, q):
                dve.wait_ge(quad_done, q + 1)
                a = ACTS[:, :, bass.ds(4 * q, 4)]
                dve.tensor_tensor(a, a, PS[:, i, :].rearrange("p (t e) -> p e t", t=4), ALU.mult).then_inc(quad_out, 1)

            norm_rows(0, HN)
            with dve.Fori(0, L) as l:
                steps[0] = 0
                dve.wait_ge(first_landed, 48 * l + 48)
                evac_h(C_MIX, 0)
                h_lows(1)
                for g in range(6):
                    mix(g)
                rwkv_prep()
                w_lows(SPLIT.index(11))
                rotate()
                dve.wait_ge(gacc_zero, 1)
                level(0, 4)
                w_lows(SPLIT.index(12))
                level(1, 4)
                decayed(0, 6)
                level(2, 4)
                level(3, 6)
                w_lows(SPLIT.index(13))
                decayed(1, 4)
                level(4, 6)
                level(5, 4)
                w_lows(SPLIT.index(14))
                level(6, 4)
                level(7, 6)
                level(8, 4)
                rwkv_units()
                rwkv_chunks()
                rwkv_out()
                dve.sem_inc(rwkv_ready, 1)
                for t in range(NT):
                    dve.wait_ge(res_done, N_OUT + t)
                    for f in range(2):
                        xs = X[:, t, f * 512:(f + 1) * 512]
                        dve.tensor_tensor(xs, xs, PS[:, 4 + 2 * t + f, :], ALU.add).then_inc(res_out, 1)
                dve.wait_ge(res_out, 4)
                norm_rows(1, HNF)
                evac_h(C_FFN, 1)
                h_lows(3)
                for i in range(len(IN_SPLIT), len(SPLIT)):
                    w_lows(i)
                topk()
                dve.sem_inc(passed, 1)
                with dve.Fori(POOL_BODIES, GATE_BODY) as j:
                    for m in range(8):
                        u_lows(m, j)
                gates()
                with dve.Fori(GATE_BODY, N_BODY) as j:
                    for m in range(8):
                        u_lows(m, j)
                dve.wait_ge(sel_out, 3)
                for i in range(3):
                    hots(i, i, True)
                dve.wait_ge(u_act, 128)
                gated(0, 0)
                with dve.Fori(1, 21) as q:
                    for i in range(3):
                        hots(i, 3 * q + i, False)
                        gated((i + 1) % 3, 3 * q + i - 2)
                hots(0, 63, False)
                for q in range(61, 63):
                    gated(q % 3, q)
                for m in range(2):
                    v_lows(m, 0)
                gated(0, 63)
                a_lows(0, 0)
                for m in range(2, 8):
                    if m % 2 == 0:
                        a_lows(m // 2, 0)
                    v_lows(m, 0)
                with dve.Fori(1, 32) as j:
                    for m in range(8):
                        if m % 2 == 0:
                            a_lows(m // 2, j)
                        v_lows(m, j)
                for f in range(2):
                    dve.wait_ge(v_done, 255 + f)
                    for t in range(NT):
                        xs = X[:, t, f * 512:(f + 1) * 512]
                        dve.tensor_tensor(xs, xs, PS[:, 2 * t + f, :], ALU.add).then_inc(peer_out, 1)
                dve.wait_ge(peer_out, 4)
                dve.sem_inc(arrived, 1)
                norm_rows(0, HN)
                dve.wait_ge(go, l + 1)
            dve.wait_ge(final_row, 16)
            for t in range(NT):
                dve.scalar_tensor_tensor(YOUT[:, t, :], X[:, t, :], STAT[:, t:t + 1], FROW, ALU.mult, ALU.mult).then_inc(y_ready, 1)

        @block.gpsimd
        def _(pool):
            pool.wait_ge(const_landed, 16)

            def u_lows(m, j):
                pool.wait_ge(u_hi, 8 * j + m + 1)
                pool.tensor_tensor(EL[:, m % 4, :], RING[:, m // 4, (m % 4) * 512:(m % 4 + 1) * 512], EH[:, m % 4, :].bitcast(F32), ALU.subtract).then_inc(u_lo_pool, 1)

            steps = [0]

            def link(ins):
                steps[0] += 1
                ins.then_inc(pool_step, 1)
                pool.wait_ge(pool_step, steps[0])

            def blocks(v, n):
                return v.rearrange("p b (q a n) -> p (b q) a n", a=2, n=2 ** (n - 1))

            def level_gates(n):
                b = 2 ** (n - 1)
                B, E = blocks(GB[:, :, :], n), blocks(GE[:, n % 2, :, :], n)
                ref = B[:, :, 0, b - 1:b].broadcast_to([P, S // b, b])
                pool.tensor_tensor(E[:, :, 0, :], ref, B[:, :, 0, :], ALU.subtract)
                pool.tensor_tensor(E[:, :, 1, :], B[:, :, 1, :], ref, ALU.subtract).then_inc(gd_ready, 1)

            def level_operand(n):
                E, XX, Q, K = (blocks(v, n) for v in (GE[:, n % 2, :, :], GX[:, n % 2, :, :], GQK[:, 0:2, :], GQK[:, 2:4, :]))
                if n >= 2:
                    pool.wait_ge(gs_done, n - 1)
                pool.wait_ge(ge_ready, n)
                pool.tensor_tensor(XX[:, :, 0, :], K[:, :, 0, :], E[:, :, 0, :], ALU.mult)
                link(pool.tensor_tensor(XX[:, :, 1, :], Q[:, :, 1, :], E[:, :, 1, :], ALU.mult))
                pool.sem_inc(gx_ready, 1)

            def finish_heads(dst, heads, w, at, gate):
                for t in range(NT):
                    d = dst[:, t, :].rearrange("p (h n) -> p h n", h=heads)
                    link(pool.tensor_tensor(d, d, STAT[:, at + heads * t:at + heads * (t + 1)].unsqueeze(2).broadcast_to([P, heads, w]), ALU.mult))
                link(pool.tensor_tensor(dst, dst, gate, ALU.mult))

            def last_row(i, q, first):
                if not first:
                    pool.wait_ge(quad_done, q - 2)
                pool.tensor_copy(PQ[:, i, 0:1], IDXQ[:, bass.ds(q, 1), 7])
                pool.tensor_copy(PQ[:, i, 1:2], GATET[:, bass.ds(4 * q + 3, 1)]).then_inc(pool_copied, 1)
                pool.wait_ge(pool_copied, q + 1)
                pool.sem_inc(pool_seen, 1)
                pool.tensor_scalar(HOT[i][:, 7, :], iota, PQ[:, i, 0:1], PQ[:, i, 1:2], ALU.is_equal, ALU.mult).then_inc(hot_pool, 1)

            with pool.Fori(0, L) as l:
                pool.memset(RAW[:, :, :, 0:1], 0.0).then_inc(zeros_ready, 1)
                steps[0] = 0
                for i in range(POOL_SPLIT):
                    for m in range(4):
                        pool.wait_ge(w_hi, 4 * i + m + 1)
                        pool.tensor_tensor(EL[:, m, :], RING[:, SPLIT[i] % 2, m * 512:(m + 1) * 512], EH[:, m, :].bitcast(F32), ALU.subtract).then_inc(w_lo_pool, 1)
                pool.wait_ge(gcum_ready, 1)
                pool.wait_ge(proj_out, 8)
                level_gates(1)
                pool.wait_ge(ab_ready, 1)
                pool.memset(GACC[:, 0:2, :, :], 0.0).then_inc(gacc_zero, 1)
                for n in range(1, 9):
                    if n < 8:
                        level_gates(n + 1)
                    level_operand(n)
                pool.wait_ge(hrstd_ready, 1)
                pool.wait_ge(silu_ready, 2)
                finish_heads(HN[:, :, 0:256], RH, RDK, 80, ZRET[:, :, 768:1024])
                pool.sem_inc(mix_ready, 1)
                finish_heads(HN[:, :, 640:1024], GH, GDV, 88, ZGLA[:, :, 384:768])
                for t in range(NT):
                    link(pool.tensor_tensor(HN[:, t, 640:1024], HN[:, t, 640:1024], ROWS[:, 768:1152], ALU.mult))
                pool.sem_inc(mix_ready, 1)
                for t in range(NT):
                    link(pool.tensor_tensor(GBIAS[:, t, :].rearrange("p (h n) -> p h n", h=NH), VTOK[:, t, :].rearrange("p (h n) -> p h n", h=NH),
                                            GG[:, t, 384:390].unsqueeze(2).broadcast_to([P, NH, 64]), ALU.mult))
                for t in range(NT):
                    link(pool.tensor_tensor(GBIAS[:, t, :], GBIAS[:, t, :], ROWS[:, 384:768], ALU.add))
                for t in range(NT):
                    link(pool.tensor_tensor(GBIAS[:, t, :], GBIAS[:, t, :], GG[:, t, 0:384], ALU.mult))
                for t in range(NT):
                    link(pool.tensor_tensor(GG[:, t, 0:384], GG[:, t, 0:384], ROWS[:, 0:384], ALU.mult))
                pool.sem_inc(rwkv_affine, 1)
                for m in range(8):
                    u_lows(m, 0)
                pool.sem_inc(passed, 1)
                with pool.Fori(1, POOL_BODIES) as j:
                    for m in range(8):
                        u_lows(m, j)
                pool.wait_ge(sel_out, 3)
                for i in range(3):
                    last_row(i, i, True)
                with pool.Fori(1, 21) as q:
                    for i in range(3):
                        last_row(i, 3 * q + i, False)
                last_row(0, 63, False)
                pool.sem_inc(arrived, 1)
                pool.wait_ge(go, l + 1)


def constants():
    const = np.zeros((P, N_CONST), np.float32)
    const[:, K_ID:K_ID + P] = np.eye(P)
    const[:, K_IOTA:K_IOTA + P] = np.arange(P)
    x = np.zeros((P, N_XCONST), np.float32)
    i = np.arange(P)
    x[:, X_MASK2:X_MASK2 + P] = i[:, None] < i[None, :]
    x[:, X_MASK2 + P:X_MASK2 + 256] = i[:, None] <= i[None, :]
    for n, b in enumerate(LEVELS):
        low = (i[:, None] // (2 * b) == i[None, :] // (2 * b)) & ((i[:, None] // b) % 2 == 1) & ((i[None, :] // b) % 2 == 0)
        x[:, X_LOW + P * n:X_LOW + P * (n + 1)] = low
        x[:, X_UP + P * n:X_UP + P * (n + 1)] = low.T
    x[:, X_ONES:X_ONES + 2] = 1
    x[:, X_BLK:X_BLK + P] = i[:, None] // 64 == i[None, :] // 64
    x[:, X_HEAD:X_HEAD + 2] = i[:, None] // 64 == np.arange(2)[None, :]
    lg = np.log1p(-np.exp(np.linspace(np.log(1 / 32), np.log(1 / 512), RH)))
    for h in range(RH):
        diff = (i[None, :] - i[:, None]).astype(np.float64)
        x[:, X_DM + 256 * h:X_DM + 256 * h + P] = np.where(diff >= 0, np.exp(lg[h] * np.maximum(diff, 0)), 0) * RDK ** -0.5
        x[:, X_DM + 256 * h + P:X_DM + 256 * (h + 1)] = np.exp(lg[h] * (diff + P)) * RDK ** -0.5
    inv = (10000.0 ** (-np.arange(32, dtype=np.float32) / 32)).astype(np.float32)
    ang = np.arange(S, dtype=np.float32)[:, None] * inv[None, :]
    for t in range(NT):
        a = ang[t * P:(t + 1) * P]
        x[:, X_ROPE + 64 * t:X_ROPE + 64 * t + 32] = np.cos(a)
        x[:, X_ROPE + 64 * t + 32:X_ROPE + 64 * (t + 1)] = np.sin(a)
    return const, x


def lay_out(a):
    f = np.float32

    def chunked(w):
        g = w.shape[2] // GC
        return np.ascontiguousarray(w.reshape(L, DC, P, g, GC).transpose(0, 3, 2, 1, 4)).reshape(L, g, P, DC * GC)

    def by_channels(w):
        return np.ascontiguousarray(w.reshape(L, -1, P, DC, 2, P).transpose(0, 1, 2, 4, 3, 5)).reshape(L, -1, P, DC * GC)

    def head_pad(w):
        w = w.reshape(*w.shape[:-1], GH, GDK)
        return np.concatenate([w, np.zeros((*w.shape[:-1], 64 - GDK), f)], -1).reshape(*w.shape[:-2], GH * 64)

    w = a["w_in"]
    r0 = 1024
    g0 = r0 + 1408
    rwkv = w[:, :, r0:g0]
    rw = [rwkv[:, :, 1152:1280], rwkv[:, :, 1280:1408], rwkv[:, :, 384:768], rwkv[:, :, 0:384], rwkv[:, :, 768:1152]]
    gkd = w[:, :, g0 + 768:g0 + 784]
    w_in = chunked(np.concatenate([*rw, gkd, np.zeros((L, D, 112), f), head_pad(w[:, :, g0:g0 + 192]), head_pad(w[:, :, g0 + 192:g0 + 384]),
                                   w[:, :, 0:1024], w[:, :, g0 + 384:g0 + 768], w[:, :, g0 + 784:g0 + 1168]], -1))
    w_out = a["w_out"].reshape(L, DC, P, D)[:, OUT_CHUNKS].reshape(L, N_OUT, 2, P, D)
    w_out = np.ascontiguousarray(w_out.transpose(0, 1, 3, 2, 4)).reshape(L, N_OUT, P, 2 * D)
    w_in[:, :N_CH] = by_channels(w_in[:, :N_CH])
    mu = a["rwkv_mu"]
    mu = np.concatenate([mu[:, 1152:1280], mu[:, 1280:1408], mu[:, 384:768], mu[:, 0:384], mu[:, 768:1152]], -1)

    def column(v):
        return v.reshape(L, -1, P).transpose(0, 2, 1)

    cols = np.concatenate([column(v) for v in (a["norm_mix"], a["norm_ffn"], mu, a["rwkv_w_bias"], a["rwkv_a_bias"], a["rwkv_k_k"],
                                               a["rwkv_k_a"], a["rwkv_r_k"].reshape(L, -1), head_pad(a["gla_gk_bias"]))], -1)
    small = np.zeros((L, P, N_SMALL), f)
    small[:, 0:64, W_WA:W_WA + 384] = a["rwkv_w_up"]
    small[:, 64:128, W_WA:W_WA + 384] = a["rwkv_a_up"]
    small[:, :, W_G:W_G + 384] = a["rwkv_g_up"]
    small[:, 0:16, W_GK:W_GK + 256] = head_pad(a["gla_gk_up"])
    rows = np.concatenate([a["rwkv_ln_w"], a["rwkv_ln_b"], a["gla_norm_w"]], -1)
    keys = np.ascontiguousarray(a["peer_sub_keys"].reshape(L, 16, P, P).transpose(0, 3, 1, 2)).reshape(L, P, 2048)
    u_t = a["peer_u"].reshape(L, P, 64, 2, DC, P).transpose(0, 2, 5, 3, 4, 1)
    v_t = a["peer_v"].reshape(L, P, 64, 2, D).transpose(0, 2, 1, 3, 4)
    const, xconst = constants()
    return {"x_in": a["x"], "w_in": w_in, "w_out": w_out, "cols": cols, "small": small, "rows": rows, "norm_final": a["norm_final"],
            "w_q": by_channels(chunked(a["peer_w_q"])), "keys": keys, "u_t": u_t.reshape(L, 64, P, 2048), "v_t": v_t.reshape(L, 64, P, 2048),
            "const": const, "xconst": xconst}


def kernel(**inputs):
    import concourse.bacc as _bacc
    from concourse.bass_utils import run_bass_kernel_spmd as _run

    arrays = {k: np.ascontiguousarray(v) for k, v in lay_out({k: np.asarray(v) for k, v in inputs.items()}).items()}
    nc = _bacc.Bacc("TRN2", target_bir_lowering=False, num_devices=1)
    args = {k: nc.dram_tensor(k, v.shape, F32, kind="ExternalInput").ap() for k, v in arrays.items()}
    out = nc.dram_tensor("y_out", (1, S, D), F32, kind="ExternalOutput").ap()
    trunk(nc, *args.values(), out)
    r = _run(nc, [arrays], core_ids=[0])
    return r.results[0]["y_out"]
```
